# Optimizing a Trainium2 kernel written in Bass

```python
import math
import jax, jax.numpy as jnp
from jax import lax
import numpy as np

D_MODEL = 1024
BATCH = 1
SEQ = 256
DEPTH = 2
DEC_BATCH = 8
DEC_SEQ = 4
PAST_LEN = 1024
PAGE_SIZE = 128

HEAD_DIM = 64
N_HEADS_A = D_MODEL // (2 * HEAD_DIM)
N_HEADS_B = D_MODEL // (2 * HEAD_DIM)
W_A = N_HEADS_A * HEAD_DIM
W_B = N_HEADS_B * HEAD_DIM
MIX_WIDTH = W_A + W_B
SPLITS = (W_A, 2 * W_A, 3 * W_A, 3 * W_A + W_B, 3 * W_A + 2 * W_B)
DILATED_BRANCHES = ((128, 1), (512, 4), (2048, 16))
MAX_WINDOW = 2048
Q_BLOCK = 128
D_FF = 2816
N_EXPERTS = 8
TOP_K = 2
D_FF_EXPERT = 3584
N_DENSE = (DEPTH + 1) // 2
N_MOE = DEPTH // 2
DEEPNORM_ALPHA = (2 * DEPTH) ** 0.25
DEEPNORM_BETA = (8 * DEPTH) ** -0.25
SB_BIAS_INIT = -7.0
LN_EPS = 1e-5
RMS_EPS = 1e-6

kernel_name = 'hybrid_dilated_stickbreaking_decode_step'

def layer_norm(x, g, b):
    xf = x.astype(jnp.float32)
    mu = jnp.mean(xf, axis=-1, keepdims=True)
    var = jnp.mean(jnp.square(xf - mu), axis=-1, keepdims=True)
    y = (xf - mu) * lax.rsqrt(var + LN_EPS) * g.astype(jnp.float32) + b.astype(jnp.float32)
    return y.astype(x.dtype)

def rms_norm(x, g):
    xf = x.astype(jnp.float32)
    y = xf * lax.rsqrt(jnp.mean(jnp.square(xf), axis=-1, keepdims=True) + RMS_EPS) * g.astype(jnp.float32)
    return y.astype(x.dtype)

def alibi_slopes(n):
    return jnp.exp2(-8.0 * jnp.arange(1, n + 1, dtype=jnp.float32) / n)

def project(x, w_in):
    B, T = x.shape[:2]
    h = jnp.einsum('btd,de->bte', x, w_in)
    qa, ka, va, qb, kb, vb = jnp.split(h, SPLITS, axis=-1)
    ha = lambda t: t.reshape(B, T, N_HEADS_A, HEAD_DIM)
    hb = lambda t: t.reshape(B, T, N_HEADS_B, HEAD_DIM)
    return ha(qa), ha(ka), ha(va), hb(qb), hb(kb), hb(vb)

def dilated_mixture(q, k_ext, v_ext, qidx, slopes):
    scale = HEAD_DIM ** -0.5
    lses, outs = [], []
    for window, dil in DILATED_BRANCHES:
        n_keys = window // dil + 1
        dist = jnp.arange(n_keys, dtype=jnp.int32) * dil
        idx = qidx[:, None] - dist[None, :]
        valid = idx >= 0
        idx = jnp.maximum(idx, 0)
        kg = k_ext[:, idx]
        vg = v_ext[:, idx]
        s = jnp.einsum('bqhd,bqjhd->bhqj', q, kg).astype(jnp.float32) * scale
        s = s - slopes[:, None, None] * dist.astype(jnp.float32)
        s = jnp.where(valid[None, None], s, -jnp.inf)
        lse = jax.nn.logsumexp(s, axis=-1)
        p = jnp.exp(s - lse[..., None]).astype(v_ext.dtype)
        outs.append(jnp.einsum('bhqj,bqjhd->bqhd', p, vg))
        lses.append(lse)
    wts = jax.nn.softmax(jnp.stack(lses, 0), axis=0)
    wts = jnp.transpose(wts, (0, 1, 3, 2))[..., None].astype(q.dtype)
    return jnp.sum(wts * jnp.stack(outs, 0), axis=0)

def dilated_prompt(q, k, v, slopes):
    B, S = q.shape[:2]
    nb = S // Q_BLOCK
    qb = q.reshape(B, nb, Q_BLOCK, N_HEADS_A, HEAD_DIM).transpose(1, 0, 2, 3, 4)
    starts = jnp.arange(nb, dtype=jnp.int32) * Q_BLOCK
    o = lax.map(lambda a: dilated_mixture(a[0], k, v, a[1] + jnp.arange(Q_BLOCK, dtype=jnp.int32), slopes),
                (qb, starts))
    return o.transpose(1, 0, 2, 3, 4).reshape(B, S, N_HEADS_A, HEAD_DIM)

def stick_breaking(q, k, v, qpos, sb_bias):
    scale = HEAD_DIM ** -0.5
    z = jnp.einsum('bqhd,bkhd->bhqk', q, k).astype(jnp.float32) * scale
    z = z + sb_bias.astype(jnp.float32)[None, :, None, None]
    kpos = jnp.arange(k.shape[1], dtype=jnp.int32)
    valid = kpos[None, :] < qpos[:, None]
    log_beta = jax.nn.log_sigmoid(z)
    log_keep = jnp.where(valid, jax.nn.log_sigmoid(-z), 0.0)
    later = lax.cumsum(log_keep, axis=3, reverse=True) - log_keep
    a = jnp.where(valid, jnp.exp(log_beta + later), 0.0).astype(v.dtype)
    return jnp.einsum('bhqk,bkhd->bqhd', a, v)

def stick_breaking_prompt(q, k, v, sb_bias):
    B, S = q.shape[:2]
    nb = S // Q_BLOCK
    qb = q.reshape(B, nb, Q_BLOCK, N_HEADS_B, HEAD_DIM).transpose(1, 0, 2, 3, 4)
    starts = jnp.arange(nb, dtype=jnp.int32) * Q_BLOCK
    o = lax.map(lambda a: stick_breaking(a[0], k, v, a[1] + jnp.arange(Q_BLOCK, dtype=jnp.int32), sb_bias),
                (qb, starts))
    return o.transpose(1, 0, 2, 3, 4).reshape(B, S, N_HEADS_B, HEAD_DIM)

def merge_groups(o_a, o_b, g_a, g_b, w_o):
    B, T = o_a.shape[:2]
    oa = rms_norm(o_a.reshape(B, T, W_A), g_a)
    ob = rms_norm(o_b.reshape(B, T, W_B), g_b)
    return jnp.einsum('bte,ed->btd', jnp.concatenate([oa, ob], axis=-1), w_o)

def swiglu(x, wg, wu, wd):
    h = jax.nn.silu(jnp.einsum('btd,df->btf', x, wg)) * jnp.einsum('btd,df->btf', x, wu)
    return jnp.einsum('btf,fd->btd', h, wd)

def moe_swiglu(x, w_router, we_gate, we_up, we_down):
    logits = jnp.einsum('btd,de->bte', x, w_router).astype(jnp.float32)
    top_val, top_idx = lax.top_k(logits, TOP_K)
    top_w = jax.nn.softmax(top_val, axis=-1)
    gates = jnp.sum(top_w[..., None] * jax.nn.one_hot(top_idx, N_EXPERTS, dtype=jnp.float32), axis=-2)
    gates = gates.astype(x.dtype)
    out = jnp.zeros_like(x)
    for e in range(N_EXPERTS):
        out = out + gates[..., e:e + 1] * swiglu(x, we_gate[e], we_up[e], we_down[e])
    return out

def setup_inputs(seed: int = 0) -> dict:
    key = jax.random.key(seed)
    ks = jax.random.split(key, 24)
    f32 = jnp.float32
    n_pages = PAST_LEN // PAGE_SIZE
    n_used = DEC_BATCH * n_pages
    n_pool = n_used + n_used // 4
    win_buf = min(MAX_WINDOW, PAST_LEN)
    nrm = lambda k, shape: jax.random.normal(k, shape, f32)
    col_scale = jnp.concatenate([jnp.ones((2 * W_A,), f32), jnp.full((W_A,), DEEPNORM_BETA, f32),
                                 jnp.ones((2 * W_B,), f32), jnp.full((W_B,), DEEPNORM_BETA, f32)])
    page_table = jax.random.permutation(ks[0], n_pool)[:n_used].reshape(DEC_BATCH, n_pages).astype(jnp.int32)
    return {
        'x_prompt': nrm(ks[1], (BATCH, SEQ, D_MODEL)),
        'x_sample': nrm(ks[2], (DEC_BATCH, DEC_SEQ, D_MODEL)),
        'cache_sb_k': nrm(ks[3], (DEPTH, n_pool, PAGE_SIZE, N_HEADS_B, HEAD_DIM)),
        'cache_sb_v': nrm(ks[4], (DEPTH, n_pool, PAGE_SIZE, N_HEADS_B, HEAD_DIM)),
        'cache_swa_k': nrm(ks[5], (DEPTH, DEC_BATCH, win_buf, N_HEADS_A, HEAD_DIM)),
        'cache_swa_v': nrm(ks[6], (DEPTH, DEC_BATCH, win_buf, N_HEADS_A, HEAD_DIM)),
        'page_table': page_table,
        'w_in': nrm(ks[7], (DEPTH, D_MODEL, 3 * W_A + 3 * W_B)) * (D_MODEL ** -0.5) * col_scale,
        'sb_bias': SB_BIAS_INIT + 0.1 * nrm(ks[22], (DEPTH, N_HEADS_B)),
        'g_mix_a': 1.0 + 0.02 * nrm(ks[8], (DEPTH, W_A)),
        'g_mix_b': 1.0 + 0.02 * nrm(ks[9], (DEPTH, W_B)),
        'w_o': nrm(ks[10], (DEPTH, MIX_WIDTH, D_MODEL)) * (MIX_WIDTH ** -0.5) * DEEPNORM_BETA,
        'ln_mix_g': 1.0 + 0.02 * nrm(ks[11], (DEPTH, D_MODEL)),
        'ln_mix_b': 0.02 * nrm(ks[12], (DEPTH, D_MODEL)),
        'ln_ffn_g': 1.0 + 0.02 * nrm(ks[13], (DEPTH, D_MODEL)),
        'ln_ffn_b': 0.02 * nrm(ks[14], (DEPTH, D_MODEL)),
        'w_gate': nrm(ks[15], (N_DENSE, D_MODEL, D_FF)) * (D_MODEL ** -0.5),
        'w_up': nrm(ks[16], (N_DENSE, D_MODEL, D_FF)) * (D_MODEL ** -0.5),
        'w_down': nrm(ks[17], (N_DENSE, D_FF, D_MODEL)) * (D_FF ** -0.5) * DEEPNORM_BETA,
        'w_router': nrm(ks[18], (N_MOE, D_MODEL, N_EXPERTS)) * (D_MODEL ** -0.5),
        'we_gate': nrm(ks[19], (N_MOE, N_EXPERTS, D_MODEL, D_FF_EXPERT)) * (D_MODEL ** -0.5),
        'we_up': nrm(ks[20], (N_MOE, N_EXPERTS, D_MODEL, D_FF_EXPERT)) * (D_MODEL ** -0.5),
        'we_down': nrm(ks[21], (N_MOE, N_EXPERTS, D_FF_EXPERT, D_MODEL)) * (D_FF_EXPERT ** -0.5) * DEEPNORM_BETA,
    }

def reference(x_prompt, x_sample, cache_sb_k, cache_sb_v, cache_swa_k, cache_swa_v, page_table,
              w_in, sb_bias, g_mix_a, g_mix_b, w_o, ln_mix_g, ln_mix_b, ln_ffn_g, ln_ffn_b,
              w_gate, w_up, w_down, w_router, we_gate, we_up, we_down):
    slopes = alibi_slopes(N_HEADS_A)
    win_buf = min(MAX_WINDOW, PAST_LEN)
    win_prompt = min(MAX_WINDOW, SEQ)
    q_rows_sample = win_buf + jnp.arange(DEC_SEQ, dtype=jnp.int32)
    q_pos_sample = PAST_LEN + jnp.arange(DEC_SEQ, dtype=jnp.int32)
    xp, xs = x_prompt, x_sample
    sbk_p, sbv_p, sbk_s, sbv_s = [], [], [], []
    swk_p, swv_p, swk_s, swv_s = [], [], [], []
    for layer in range(DEPTH):
        qa, ka, va, qb, kb, vb = project(xp, w_in[layer])
        oa = dilated_prompt(qa, ka, va, slopes)
        ob = stick_breaking_prompt(qb, kb, vb, sb_bias[layer])
        mix_p = merge_groups(oa, ob, g_mix_a[layer], g_mix_b[layer], w_o[layer])
        sbk_p.append(kb)
        sbv_p.append(vb)
        swk_p.append(ka[:, SEQ - win_prompt:])
        swv_p.append(va[:, SEQ - win_prompt:])
        qa_s, ka_s, va_s, qb_s, kb_s, vb_s = project(xs, w_in[layer])
        k_ext = jnp.concatenate([cache_swa_k[layer], ka_s], axis=1)
        v_ext = jnp.concatenate([cache_swa_v[layer], va_s], axis=1)
        oa_s = dilated_mixture(qa_s, k_ext, v_ext, q_rows_sample, slopes)
        past_k = cache_sb_k[layer][page_table].reshape(DEC_BATCH, PAST_LEN, N_HEADS_B, HEAD_DIM)
        past_v = cache_sb_v[layer][page_table].reshape(DEC_BATCH, PAST_LEN, N_HEADS_B, HEAD_DIM)
        k_all = jnp.concatenate([past_k, kb_s], axis=1)
        v_all = jnp.concatenate([past_v, vb_s], axis=1)
        ob_s = stick_breaking(qb_s, k_all, v_all, q_pos_sample, sb_bias[layer])
        mix_s = merge_groups(oa_s, ob_s, g_mix_a[layer], g_mix_b[layer], w_o[layer])
        sbk_s.append(kb_s)
        sbv_s.append(vb_s)
        swk_s.append(k_ext[:, DEC_SEQ:])
        swv_s.append(v_ext[:, DEC_SEQ:])
        xp = layer_norm(DEEPNORM_ALPHA * xp + mix_p, ln_mix_g[layer], ln_mix_b[layer])
        xs = layer_norm(DEEPNORM_ALPHA * xs + mix_s, ln_mix_g[layer], ln_mix_b[layer])
        i = layer // 2
        if layer % 2 == 0:
            fp = swiglu(xp, w_gate[i], w_up[i], w_down[i])
            fs = swiglu(xs, w_gate[i], w_up[i], w_down[i])
        else:
            fp = moe_swiglu(xp, w_router[i], we_gate[i], we_up[i], we_down[i])
            fs = moe_swiglu(xs, w_router[i], we_gate[i], we_up[i], we_down[i])
        xp = layer_norm(DEEPNORM_ALPHA * xp + fp, ln_ffn_g[layer], ln_ffn_b[layer])
        xs = layer_norm(DEEPNORM_ALPHA * xs + fs, ln_ffn_g[layer], ln_ffn_b[layer])
    return (xp, xs,
            jnp.stack(sbk_p), jnp.stack(sbv_p), jnp.stack(sbk_s), jnp.stack(sbv_s),
            jnp.stack(swk_p), jnp.stack(swv_p), jnp.stack(swk_s), jnp.stack(swv_s))


_drawn_inputs = setup_inputs


def setup_inputs(seed=0):
    import zlib

    import numpy as np

    out = dict(_drawn_inputs(seed))
    spreads = {}
    factors = {'g_mix_a': 5.433, 'g_mix_b': 5.004}
    for name, (base, spread) in spreads.items():
        noise = np.random.default_rng([zlib.crc32(name.encode()), seed]).standard_normal(out[name].shape)
        drawn = base * np.exp(spread * noise) if base else spread * noise
        out[name] = __import__('jax').numpy.asarray(drawn.astype(out[name].dtype))
    for name, factor in factors.items():
        out[name] = (out[name] * factor).astype(out[name].dtype)
    return out
```

```python
from contextlib import ExitStack

import numpy as np

import concourse.bass as bass
from concourse import mybir

F32 = mybir.dt.float32
I32 = mybir.dt.int32
ALU = mybir.AluOpType
ACT = mybir.ActivationFunctionType
AX = mybir.AxisListType.X

P = 128
D = 1024
KD = D // P
SEQ, NS, DEC = 256, 8, 4
LAYERS = 2
HEADS, HD = 8, 64
HP = HEADS // 2
WID = HEADS * HD
PAST, PAGE = 1024, 128
PAGES = PAST // PAGE
SAMPLE = NS * DEC
ROWS = (P, P, SAMPLE)
T = len(ROWS)
TOK = SEQ + SAMPLE
FF, FFE, EXPERTS = 2816, 3584, 8
CH = 512
FPC = CH // P
SLOT = KD * CH
NSLOT = 7
TOP_K = 2
ITEM = 128
PASSES = -(-TOK // ITEM)
ITEMS = TOP_K * TOK // ITEM + EXPERTS
SPARSE = 512
SWA_TILES = 5
SWA_KEYS = SWA_TILES * P
SCALE = HD ** -0.5
ALPHA = (2 * LAYERS) ** 0.25
LN_EPS, RMS_EPS = 1e-5, 1e-6
BIG = 1e34
NEG = -1e30
BRANCHES = ((128, 1), (512, 4), (2048, 16))


def position_tables():
    def ln_count(dist):
        n = sum((dist % d == 0) & (dist <= w) for w, d in BRANCHES)
        return np.where((dist >= 0) & (n > 0), np.log(np.maximum(n, 1)), NEG)

    q, k = np.arange(P)[:, None], np.arange(P)[None, :]
    dist = np.concatenate([q - k, q - k + P, q - k], 1)
    slopes = 2.0 ** (-8.0 * np.arange(1, HEADS + 1) / HEADS)
    col = np.arange(SWA_KEYS)
    dense = SPARSE + (SWA_TILES - 1) * (col % P) + col // P
    s = col - (PAST - SPARSE)
    row = np.where(s < 0, dense, 16 * (s % 32) + s // 32)
    far = PAST + np.arange(DEC)[:, None] - row[None, :]
    past = -slopes[:, None, None] * far[None] + ln_count(far)[None]
    i, seq, owner, j = (a.reshape(s) for a, s in ((np.arange(DEC), (DEC, 1, 1, 1)), (np.arange(NS), (1, NS, 1, 1)),
                                                 (np.arange(NS), (1, 1, NS, 1)), (np.arange(DEC), (1, 1, 1, DEC))))
    own = np.where(seq == owner, ln_count(i - j), NEG)
    new_a = -slopes[:, None, None, None, None] * (i - j)[None] + own[None]
    new_b = np.broadcast_to(np.where((seq == owner) & (j < i), 0.0, NEG), new_a.shape)
    tok = np.arange(P)[:, None, None] + P * np.arange(T)[None, :, None]
    one = np.ones((1, 1, EXPERTS))
    tabs = {
        "distance": dist, "ln_branches": ln_count(dist), "strict_mask": np.where(dist > 0, 0.0, NEG),
        "past_bias": past.reshape(HEADS * DEC, SWA_KEYS),
        "new_bias_a": new_a.reshape(HEADS * DEC, NS * SAMPLE), "new_bias_b": new_b.reshape(HEADS * DEC, NS * SAMPLE),
        "identity": np.eye(P), "earlier": np.triu(np.ones((P, P)), 1), "ones": np.ones((P, P)),
        "slot_number": np.broadcast_to(1.0 + np.arange(ITEM), (P, ITEM)),
        "descending": np.broadcast_to(np.arange(EXPERTS, 0, -1), (P, T, EXPERTS)),
        "is_token": (tok < TOK) * one,
        "item_number": np.broadcast_to(np.arange(ITEMS + 1)[None, :, None], (P, ITEMS + 1, EXPERTS)),
        "expert_number": np.broadcast_to(np.arange(EXPERTS)[None, None, :], (P, ITEMS + 1, EXPERTS)),
    }
    return {n: np.ascontiguousarray(a, np.float32) for n, a in tabs.items()}


class Steps:

    def __init__(self, eng, sem):
        self.eng, self.sem, self.n, self.base = eng, sem, 0, None

    def value(self):
        return self.n if self.base is None else self.base + self.n

    def go(self, ins):
        self.n += 1
        ins.then_inc(self.sem, 1)

    def did(self, ins):
        self.go(ins)
        self.eng.wait_ge(self.sem, self.value())


PROJ_SLOTS = ((3, 4, 5, 6, 0, 1), (6, 3, 4, 5, 2, 0))
WO_SLOTS = ((2, 0), (1, 2))
CYCLE = ((1, 3, 4, 5, 6, 2, 0), (0, 3, 4, 5, 6, 1, 2))
DENSE_CHUNKS = [(c, min(FPC, FF // P - FPC * c)) for c in range(-(-FF // CH))]
DENSE_F = FF // P
MOE_CHUNKS = FFE // CH
MOE_F = FFE // P
UNITS_Q, UNITS_KV = FPC, T
PROJ_UNITS = 2 * UNITS_Q + 4 * UNITS_KV
DEC_UNITS = 16
ITEM_LOADS = 3 * MOE_CHUNKS


def hybrid_decode_step(nc, ins, outs):
    y_p, y_s, sbk_p, sbv_p, sbk_s, sbv_s, swk_p, swv_p, swk_s, swv_s = outs
    ctx = ExitStack()
    with ctx:
        def sb(name, shape, dt=F32):
            return ctx.enter_context(nc.sbuf_tensor(name, shape, dt))

        def sem(name):
            return ctx.enter_context(nc.semaphore(name))

        ring = sb("ring", [P, NSLOT * SLOT])
        xT = sb("xT", [P, KD * TOK])
        x_tok = sb("x_tok", [P, T, D])
        kv_or_h = sb("kv_or_h", [P, DENSE_F * TOK])
        q_or_o = sb("q_or_o", [P, KD * TOK])
        k_or_ln = sb("k_or_ln", [P, KD * TOK])
        o_or_acc = sb("o_or_acc", [P, T, D])
        prompt_tab = sb("prompt_tab", [P, 3, 3 * P])
        past_bias = sb("past_bias", [SAMPLE, SWA_KEYS])
        new_bias = sb("new_bias", [SAMPLE, 2, NS * SAMPLE])
        ident = sb("ident", [P, P])
        probT = sb("probT", [P, 2, 3 * P])
        decT = sb("decT", [P, 2, (PAGES + 1) * SAMPLE])
        qblk = sb("qblk", [P, 2, HP * SAMPLE])
        oS = sb("oS", [P, KD, SAMPLE])
        g_mix = sb("g_mix", [P, LAYERS, KD])
        sb_bias = sb("sb_bias", [P, LAYERS, HEADS])
        sb_bias_rows = sb("sb_bias_rows", [SAMPLE, LAYERS])
        stat = sb("stat", [P, 2, 8])
        norm = sb("norm", [P, T, 24])
        dstat = sb("dstat", [SAMPLE, 4])
        pages = sb("pages", [1, NS * PAGES], I32)
        plan = sb("plan", [1, ITEMS + 2], I32)
        psum = ctx.enter_context(nc.psum_tensor("psum", [P, 8 * CH], F32))

        def bank(b, n=1):
            return psum[:, b * CH:(b + n) * CH]

        xTv = xT[:, :].rearrange("p (k t) -> p k t", k=KD)
        kv = kv_or_h[:, 0:T * 4 * WID].rearrange("p (t g f) -> p t g f", t=T, g=4)
        hT = kv_or_h[:, :].rearrange("p (f t) -> p f t", f=DENSE_F)
        hE = kv_or_h[:, 0:MOE_F * ITEM].rearrange("p (f t) -> p f t", f=MOE_F)
        qT = q_or_o[:, :].rearrange("p (k t) -> p k t", k=KD)
        kT = k_or_ln[:, :].rearrange("p (k t) -> p k t", k=KD)
        ln_gb = k_or_ln[:, 0:2 * D].rearrange("p (a d) -> p a d", a=2)
        probs = xT[:, 0:1056]
        keeps = xT[:, 1056:2113]
        kv0 = 3 * SLOT
        k_sb = ring[:, kv0:kv0 + PAGES * WID].rearrange("p (j f) -> p j f", f=WID)
        v_sb = ring[:, kv0 + 4096:kv0 + 8192].rearrange("p (j f) -> p j f", f=WID)
        k_swa = ring[:, kv0 + 8192:kv0 + 10752].rearrange("p (j f) -> p j f", f=WID)
        v_swa = ring[:, kv0 + 10752:kv0 + 13312].rearrange("p (j f) -> p j f", f=WID)
        kstage = ring[:, kv0 + 13312:kv0 + 15360].rearrange("p (j f) -> p j f", f=WID)
        swa_s = ring[0:SAMPLE, kv0 + 15360:kv0 + 15360 + SWA_KEYS + SAMPLE]
        silu_r = [q_or_o[:, a * CH:(a + 1) * CH] for a in (0, 2)]
        silu_t = [q_or_o[:, a * CH:(a + 1) * CH] for a in (1, 3)]
        beside_h = kv_or_h[:, MOE_F * ITEM:]
        pick = beside_h[:, 0:T * ITEM].rearrange("p (t s) -> p t s", t=T)
        pickT = beside_h[:, T * ITEM:T * ITEM + TOK]
        xg = xT[:, 0:KD * ITEM].rearrange("p (k s) -> p k s", k=KD)
        y_item = xT[:, KD * ITEM:KD * ITEM + D]
        ptab = prompt_tab[:, :, :].rearrange("p a b -> p (a b)")
        earlier, ones, slot_number = ptab[:, 0:P], ptab[:, P:2 * P], ptab[:, 2 * P:3 * P]
        w_router = ptab[:, 3 * P:3 * P + KD * EXPERTS].rearrange("p (k e) -> p k e", k=KD)
        NI = ITEMS + 1

        def rows_of(where, at, n, m):
            return where[:, at:at + n * m].rearrange("p (t e) -> p t e", t=n)
        descending, is_token = rows_of(ptab, 448, T, 8), rows_of(ptab, 472, T, 8)
        item_number, expert_number = rows_of(ptab, 496, NI, 8), rows_of(ptab, 600, NI, 8)
        rank_of, gate_of = rows_of(ptab, 704, T, NI), rows_of(ptab, 744, T, NI)
        chosen, gates, ranks = (rows_of(ptab, 784 + 24 * a, T, 8) for a in range(3))
        vals = rows_of(ptab, 856, T, 8)
        logit, tie, hot1, hot2 = (rows_of(q_or_o, 24 * a, T, 8) for a in range(4))
        of_item, first_rank, wide = (rows_of(q_or_o, 104 + 104 * a, NI, 8) for a in range(3))
        per_expert = rows_of(q_or_o, 420, 4, 8)
        plan_f = q_or_o[:, 460:460 + NI + 1]
        mean_sq_out = xT[:, 0:WID]

        w_loaded = [sem(f"w_loaded{s}") for s in range(NSLOT)]
        tables_in, ident_in, x_in, router_in = sem("tables_in"), sem("ident_in"), sem("x_in"), sem("router_in")
        ln_in = sem("ln_in")
        tp_full, tp_free = sem("transposes_done"), sem("transposes_copied")
        proj_done, proj_free = sem("projections_done"), sem("projections_copied")
        scored, masked, expd, prob_ready = sem("scored"), sem("masked"), sem("exponentials"), sem("probs_ready")
        pv_done, o_copied = sem("pv_done"), sem("o_copied")
        ksb_in, vsb_in, kswa_in, vswa_in = sem("ksb_in"), sem("vsb_in"), sem("kswa_in"), sem("vswa_in")
        qblk_ready = sem("qblk_ready")
        d_full, d_free = sem("dec_transposes_done"), sem("dec_transposes_copied")
        d_scored, d_new, d_newm = sem("dec_scored"), sem("dec_new_scored"), sem("dec_new_masked")
        d_exp, d_prob, d_biased, d_swaexp = sem("dec_sb_exp"), sem("dec_probs"), sem("dec_swa_biased"), sem("dec_swa_exp")
        d_o, d_ocopied = sem("dec_o_done"), sem("dec_o_copied")
        sq_done, rms_root, rms_scaled = sem("squares_summed"), sem("rms_root"), sem("rms_scaled")
        wo_done, wo_added = sem("wo_done"), sem("wo_added")
        var_ready, ln_root, ln_done = sem("var_ready"), sem("ln_root"), sem("ln_done")
        gu_done, gu_exp, gu_free = sem("gate_up_done"), sem("gate_exp"), sem("gate_up_used")
        down_done, ffn_added = sem("down_done"), sem("ffn_added")
        stored_kv, stored_win, stored_y, shifted = sem("stored_kv"), sem("stored_window"), sem("stored_y"), sem("shifted")
        kT_read = sem("kT_read")
        logits_done, logits_copied, chosen_ready = sem("logits_done"), sem("logits_copied"), sem("chosen_ready")
        gate_exp2, ranks_done, plan_ready, acc_zero = sem("gate_exp2"), sem("ranks_done"), sem("plan_ready"), sem("acc_zero")
        pick_ready, gathered, gather_copied = sem("pick_ready"), sem("gathered"), sem("gather_copied")
        pick_turned, pickT_copied = sem("pick_turned"), sem("pickT_copied")
        e_gu, e_exp, e_h, e_down = sem("expert_gate_up"), sem("expert_exp"), sem("expert_h"), sem("expert_down")
        y_copied, combined, added = sem("y_copied"), sem("combined"), sem("combined_added")
        act_step, dve_step, dve_tail = sem("act_step"), sem("dve_step"), sem("dve_tail")

        DENSE_GU = 2 * DENSE_F
        tp_at = {}
        u = 0
        for L in range(LAYERS):
            for name, n in ((("x", 6),) if L == 0 else ()) + (("k", 6), ("prompt", 2 * HEADS), ("sample", 2),
                                                              ("merge", 6), ("mix", 6)) + ((("ffn", 6),) if L == 0 else ()):
                tp_at[L, name] = u
                u += n
        loads = [0] * NSLOT

        def slot_view(s, k=KD):
            return ring[:, s * SLOT:(s + 1) * SLOT].rearrange("p (k f) -> p k f", k=k)

        stream = []
        used = [None] * NSLOT

        def chunk(key, slot, src, shape_k, freed):
            loads[slot] += 1
            stream.append((key, slot, src, shape_k, used[slot], loads[slot]))
            used[slot] = freed

        for L in range(LAYERS):
            w_in = ins["w_in"][L].rearrange("(k p) f -> p k f", p=P)
            at = 0
            for c in range(6):
                at += UNITS_Q if c % 3 == 0 else UNITS_KV
                chunk((L, "proj", c), PROJ_SLOTS[L][c], w_in[:, :, c * CH:(c + 1) * CH], KD, (proj_done, PROJ_UNITS * L + at))
            w_o = ins["w_o"][L].rearrange("(k p) f -> p k f", p=P)
            for c in range(2):
                chunk((L, "wo", c), WO_SLOTS[L][c], w_o[:, :, c * CH:(c + 1) * CH], KD, (wo_done, 6 * L + 3 * (c + 1)))
            if L == 0:
                n = 0
                wg, wu = (ins[w][0].rearrange("(k p) f -> p k f", p=P) for w in ("w_gate", "w_up"))
                for c, m in DENSE_CHUNKS:
                    for b, w in enumerate((wg, wu)):
                        chunk((L, "gu"[b], c), CYCLE[L][n % NSLOT], w[:, :, c * CH:c * CH + m * P], KD,
                              (gu_done, 2 * (FPC * c + m) - 1 + b))
                        n += 1
                wd = ins["w_down"][0].rearrange("(f p) d -> p f d", p=P)
                for c, m in DENSE_CHUNKS:
                    chunk((L, "d", c), CYCLE[L][n % NSLOT], wd[:, FPC * c:FPC * c + m, :], FPC, (down_done, c + 1))
                    n += 1
        loaded_at = {key: (slot, 16 * n) for key, slot, _, _, _, n in stream}
        moe_base, moe_used = list(loads), list(used)
        we = [ins[w].rearrange("o e (k p) f -> (o e) p k f", p=P) for w in ("we_gate", "we_up")]
        wed = ins["we_down"].rearrange("o e (f p) d -> (o e) p f d", p=P)
        item_loads = [("gu"[n % 2], n // 2) if n < 2 * MOE_CHUNKS else ("d", n - 2 * MOE_CHUNKS) for n in range(ITEM_LOADS)]

        def item_slot(n):
            return CYCLE[1][n % NSLOT]

        def item_loaded(eng, n, i):
            s = item_slot(n)
            eng.wait_ge(w_loaded[s], 16 * 3 * i + 16 * (moe_base[s] + n // NSLOT + 1))

        def arrived(eng, key):
            s, v = loaded_at[key]
            eng.wait_ge(w_loaded[s], v)
            return slot_view(s, FPC if key[1] == "d" else KD)

        def out_rows(L, pair):
            return pair

        block = ctx.enter_context(nc.Block())

        @block.sync
        def _(sp):
            def tab(dst, name):
                sp.dma_start(dst, ins[name]).then_inc(tables_in, 16)

            for t in range(2):
                sp.dma_start(x_tok[:, t, :], ins["x_prompt"][0, t * P:(t + 1) * P, :]).then_inc(x_in, 16)
            sp.dma_start(x_tok[0:SAMPLE, 2, :], ins["x_sample"].rearrange("b t d -> (b t) d")).then_inc(x_in, 16)
            sp.dma_start(ident[:, :], ins["identity"]).then_inc(ident_in, 16)

            def load(n):
                key, slot, src, k, freed, _ = stream[n]
                if freed:
                    sp.wait_ge(*freed)
                w = src.shape[-1] if k == KD else None
                dst = slot_view(slot, k)
                dst = dst[:, :, 0:w] if k == KD else dst[:, 0:src.shape[1], :]
                sp.dma_start(dst, src).then_inc(w_loaded[slot], 16)

            names = {key: n for n, (key, *_) in enumerate(stream)}
            for n in range(6):
                load(n)
            for a, name in enumerate(("distance", "ln_branches", "strict_mask")):
                tab(prompt_tab[:, a, :], name)
            tab(past_bias[:, :], "past_bias")
            tab(new_bias[:, 0, :], "new_bias_a")
            tab(new_bias[:, 1, :], "new_bias_b")
            tab(g_mix[:, :, :], "g_mix_cols")
            tab(sb_bias[:, :, :], "sb_bias_all")
            tab(sb_bias_rows[:, :], "sb_bias_rows")
            sp.dma_start(pages[:, :], ins["page_table"].rearrange("(o a) b -> o (a b)", o=1)).then_inc(tables_in, 16)

            for L in range(LAYERS):
                if L == 1:
                    for c in range(6):
                        load(names[L, "proj", c])
                for c in range(2):
                    load(names[L, "wo", c])
                if L == 0:
                    load(names[L, "g", 0])
                caches = {n: ins[n][L].rearrange("b n h d -> b n (h d)")
                          for n in ("cache_sb_k", "cache_sb_v", "cache_swa_k", "cache_swa_v")}

                def load_pages(dst, name, loaded, i, free=None):
                    entries = [pages[0:1, j:j + 1] if free is None else pages[0:1, bass.ds(PAGES * i + j, 1)]
                               for j in range(PAGES)]
                    numbers = [sp.value_load(n, min_val=0, max_val=ins[name].shape[1] - 1) for n in entries]
                    if free is not None:
                        sp.wait_ge(*free)
                    for j, page in enumerate(numbers):
                        sp.dma_start(dst[:, j, :], caches[name][bass.ds(page, 1), :, :].rearrange("o p f -> (o p) f"))\
                          .then_inc(loaded, 16)

                def load_window(dst, name, loaded, i):
                    c = caches[name]
                    seq = c[bass.ds(i, 1)]
                    near = seq[:, SPARSE:PAST, :].rearrange("o (p c) f -> (o p) c f", c=SWA_TILES - 1)
                    sp.dma_start(dst[:, 0:SWA_TILES - 1, :], near).then_inc(loaded, 16)
                    far = seq[:, 0:SPARSE, :].rearrange("o (a b) f -> (o a) b f", b=16)
                    for b in range(DEC):
                        sp.dma_start(dst[32 * b:32 * b + 32, SWA_TILES - 1, :], far[:, b, :]).then_inc(loaded, 16)

                sp.wait_ge(tables_in, 16 * 10)
                sp.wait_ge(proj_done, PROJ_UNITS * (L + 1))
                load_pages(k_sb, "cache_sb_k", ksb_in, 0)
                load_window(k_swa, "cache_swa_k", kswa_in, 0)
                load_pages(v_sb, "cache_sb_v", vsb_in, 0)
                load_window(v_swa, "cache_swa_v", vswa_in, 0)
                units, outs_ = DEC_UNITS * NS * L, 2 * NS * L
                with sp.Fori(1, NS) as i:
                    load_pages(k_sb, "cache_sb_k", ksb_in, i, (d_full, DEC_UNITS * i + (units - DEC_UNITS + PAGES)))
                    sp.wait_ge(d_full, DEC_UNITS * i + (units - DEC_UNITS + PAGES + SWA_TILES))
                    load_window(k_swa, "cache_swa_k", kswa_in, i)
                    load_pages(v_sb, "cache_sb_v", vsb_in, i, (d_o, 2 * i + (outs_ - 1)))
                    sp.wait_ge(d_o, 2 * i + outs_)
                    load_window(v_swa, "cache_swa_v", vswa_in, i)
                sp.wait_ge(d_o, 2 * NS * (L + 1))
                sp.wait_ge(tp_full, tp_at[L, "sample"])
                for a, name in enumerate(("ln_mix_g", "ln_mix_b")):
                    sp.dma_start(ln_gb[:, a, :], ins[name][L].partition_broadcast(P)).then_inc(ln_in, 16)
                if L == 0:
                    first = names[L, "g", 0] + 1
                    for n in range(first, names[L, "d", 0]):
                        load(n)
                    sp.wait_ge(ln_done, 2 * T * L + T)
                    for a, name in enumerate(("ln_ffn_g", "ln_ffn_b")):
                        sp.dma_start(ln_gb[:, a, :], ins[name][L].partition_broadcast(P)).then_inc(ln_in, 16)
                    for n in range(names[L, "d", 0], names[L, "d", 0] + len(DENSE_CHUNKS)):
                        load(n)

            def item_load(n, e, i):
                what, c = item_loads[n]
                s = item_slot(n)
                if n < NSLOT:
                    if i is None:
                        sp.wait_ge(*moe_used[s])
                    else:
                        sp.wait_ge(e_down, MOE_CHUNKS * i + (n + 1 - MOE_CHUNKS))
                elif n - NSLOT < 2 * MOE_CHUNKS:
                    v = n - NSLOT + 1
                    sp.wait_ge(e_gu, v if i is None else 2 * MOE_CHUNKS * i + v)
                if what == "d":
                    src, dst = wed[bass.ds(e, 1), :, FPC * c:FPC * (c + 1), :], slot_view(s, FPC)
                else:
                    src, dst = we["gu".index(what)][bass.ds(e, 1), :, :, c * CH:(c + 1) * CH], slot_view(s)
                sp.dma_start(dst, src.rearrange("o p k f -> (o p) k f")).then_inc(w_loaded[s], 16)

            sp.wait_ge(masked, 2 * HEADS * LAYERS)
            for dst, name in ((earlier, "earlier"), (ones, "ones"), (slot_number, "slot_number"),
                              (descending, "descending"), (is_token, "is_token"),
                              (item_number, "item_number"), (expert_number, "expert_number")):
                sp.dma_start(dst, ins[name]).then_inc(router_in, 16)
            sp.dma_start(w_router, ins["w_router"][0].rearrange("(k p) e -> p k e", p=P)).then_inc(router_in, 16)
            def item_expert(i):
                return sp.value_load(plan[0:1, bass.ds(i + 1, 1)], min_val=0, max_val=EXPERTS - 1)

            sp.wait_ge(plan_ready, 1)
            count = sp.value_load(plan[0:1, 0:1], min_val=0, max_val=ITEMS)
            first_expert = sp.value_load(plan[0:1, 1:2], min_val=0, max_val=EXPERTS - 1)
            for n in range(ITEM_LOADS):
                item_load(n, first_expert, None)
                if n == NSLOT - 1:
                    sp.wait_ge(ln_done, 2 * T + T)
                    for a, name in enumerate(("ln_ffn_g", "ln_ffn_b")):
                        sp.dma_start(ln_gb[:, a, :], ins[name][1].partition_broadcast(P)).then_inc(ln_in, 16)
            with sp.Fori(1, ITEMS) as i:
                with sp.If(i < count):
                    e = item_expert(i)
                    for n in range(ITEM_LOADS):
                        item_load(n, e, i)
            for t, dst in enumerate((y_p[0, 0:P, :], y_p[0, P:SEQ, :], y_s.rearrange("b t d -> (b t) d"))):
                sp.wait_ge(ln_done, 2 * T * LAYERS - T + t + 1)
                sp.dma_start(dst, x_tok[0:ROWS[t], t, :]).then_inc(stored_y, 16)
            sp.wait_ge(stored_y, 16 * T)

        @block.gpsimd
        def _(pool):
            def shift(L, half):
                for src, dst in ((ins["cache_swa_k"], swk_s), (ins["cache_swa_v"], swv_s)):
                    s = src[L].rearrange("b n h d -> b (n h d)")
                    d = dst[L].rearrange("b n h d -> b (n h d)")
                    for b in range(4 * half, 4 * half + 4):
                        n = (PAST - DEC) * WID
                        pool.dma_start(d[b, 0:n].rearrange("(a c) -> a c", a=240),
                                       s[b, DEC * WID:PAST * WID].rearrange("(a c) -> a c", a=240)).then_inc(shifted, 16)

            for L in range(LAYERS):
                pool.wait_ge(proj_free, PROJ_UNITS * (L + 1))
                for g, (prompt, sample) in enumerate(((swk_p, None), (swv_p, None), (sbk_p, sbk_s), (sbv_p, sbv_s))):
                    for t in range(2):
                        pool.dma_start(prompt[L, 0, t * P:(t + 1) * P].rearrange("t h d -> t (h d)"), kv[:, t, g, :])\
                            .then_inc(stored_kv, 16)
                    if sample is not None:
                        pool.dma_start(sample[L].rearrange("b t h d -> (b t) (h d)"), kv[0:SAMPLE, 2, g, :])\
                            .then_inc(stored_kv, 16)
                for g, dst in enumerate((swk_s, swv_s)):
                    for b in range(NS):
                        pool.dma_start(dst[L, b, PAST - DEC:PAST].rearrange("t h d -> t (h d)"),
                                       kv[DEC * b:DEC * b + DEC, 2, g, :]).then_inc(stored_win, 16)
                if L == 0:
                    pool.wait_ge(wo_done, 1)
                    for M in range(LAYERS):
                        for half in range(2):
                            pool.wait_ge(gu_done, 8 * (2 * M + half) + 1)
                            shift(M, half)
            pool.wait_ge(stored_kv, 16 * LAYERS * 10)
            pool.wait_ge(stored_win, 16 * LAYERS * 2 * NS)
            pool.wait_ge(shifted, 16 * LAYERS * 2 * NS)

        @block.tensor
        def _(pe):
            def transpose_unit(u, parts, dst):
                if u >= 2:
                    pe.wait_ge(tp_free, u - 1)
                for o, src in zip(dst(bank(u % 2)), parts):
                    last = pe.transpose(o, src, ident[0:src.shape[0], 0:src.shape[0]])
                last.then_inc(tp_full, 1)

            def token_to_feature(u, src):
                for t, ready in enumerate(src):
                    ready(t)
                    r = ROWS[t]
                    for g in range(2):
                        transpose_unit(u + 2 * t + g, [src_tok[0:r, t, (4 * g + j) * P:(4 * g + j + 1) * P] for j in range(4)],
                                       lambda b: [b[:, j * r:(j + 1) * r] for j in range(4)])

            pe.wait_ge(ident_in, 16)
            pe.wait_ge(x_in, 48)
            src_tok = x_tok
            token_to_feature(0, [lambda t: None] * T)
            for L in range(LAYERS):
                pe.wait_ge(tp_free, tp_at[L, "k"])
                unit = PROJ_UNITS * L
                for c in range(6):
                    w = arrived(pe, (L, "proj", c))
                    for n in range(UNITS_Q if c % 3 == 0 else UNITS_KV):
                        if L == 1 and unit - PROJ_UNITS * L < 6:
                            pe.wait_ge(ffn_added, 6)
                        if unit >= 6:
                            pe.wait_ge(proj_free, unit - 5)
                        b = bank(2 + unit % 6)
                        for k in range(KD):
                            if c % 3 == 0:
                                last = pe.matmul(b[:, 0:TOK], w[:, k, n * P:(n + 1) * P], xTv[:, k, :],
                                                 start=k == 0, stop=k == KD - 1)
                            else:
                                last = pe.matmul(b[0:ROWS[n], :], xTv[:, k, n * P:n * P + ROWS[n]], w[:, k, :],
                                                 start=k == 0, stop=k == KD - 1)
                        last.then_inc(proj_done, 1)
                        unit += 1
                pe.wait_ge(proj_free, PROJ_UNITS * (L + 1))
                for m in range(2):
                    for t in range(T):
                        r = ROWS[t]
                        transpose_unit(tp_at[L, "k"] + T * m + t, [kv[0:r, t, 2 * m, j * P:(j + 1) * P] for j in range(4)],
                                       lambda b: [b[:, j * r:(j + 1) * r] for j in range(4)])
                pe.wait_ge(tp_free, tp_at[L, "prompt"])
                n0 = 2 * HEADS * L

                def score(n):
                    m, h = divmod(n - n0, HEADS)
                    rows = slice(HD * (h % 2), HD * (h % 2) + HD)
                    k = HP * m + h // 2
                    if n >= 2:
                        pe.wait_ge(masked, n - 1)
                    b = bank(2 + n % 2)
                    pe.matmul(b[:, 0:P], qT[rows, k, 0:P], kT[rows, k, 0:P], start=True, stop=True)
                    pe.matmul(b[:, P:3 * P], qT[rows, k, P:SEQ], kT[rows, k, 0:SEQ], start=True, stop=True)\
                        .then_inc(scored, 1)

                score(n0)
                for n in range(n0, n0 + 2 * HEADS):
                    m, h = divmod(n - n0, HEADS)
                    if n + 1 < n0 + 2 * HEADS:
                        score(n + 1)
                    pe.wait_ge(prob_ready, n + 1)
                    u = tp_at[L, "prompt"] + n - n0
                    e = probs[:, 384 * (n % 2):384 * (n % 2) + 384]
                    transpose_unit(u, [e[:, j * P:(j + 1) * P] for j in range(3)],
                                   lambda b: [b[:, j * P:(j + 1) * P] for j in range(3)])
                    pe.wait_ge(tp_free, u + 1)
                    if n >= 2:
                        pe.wait_ge(o_copied, n - 1)
                    b = bank(4 + n % 2)
                    v = [kv[:, t, 2 * m + 1, h * HD:(h + 1) * HD] for t in range(2)]
                    pT = probT[:, n % 2, :]
                    pe.matmul(b[:, 0:HD], pT[:, 0:P], v[0], start=True, stop=True)
                    pe.matmul(b[:, HD:2 * HD], pT[:, P:2 * P], v[0], start=True, stop=False)
                    pe.matmul(b[:, HD:2 * HD], pT[:, 2 * P:3 * P], v[1], start=False, stop=True).then_inc(pv_done, 1)
                pe.wait_ge(masked, n0 + 2 * HEADS)
                pe.wait_ge(o_copied, n0 + 2 * HEADS)

                B = NS * L
                with pe.Fori(0, NS) as i:
                    def transpose_keys(j):
                        src = k_sb[:, j, :] if j < PAGES else k_swa[:, j - PAGES, :]
                        return [src[:, a * P:(a + 1) * P] for a in range(HP)]

                    def key_unit(j):
                        if j == PAGES:
                            pe.wait_ge(kswa_in, 16 * 5 * i + 16 * 5 * (B + 1))
                        for_bank = bank(j % 2)
                        for a, src in enumerate(transpose_keys(j)):
                            last = pe.transpose(for_bank[:, a * P:(a + 1) * P], src, ident[:, :])
                        last.then_inc(d_full, 1)

                    def wait_bank(j):
                        if j >= 2:
                            pe.wait_ge(d_free, DEC_UNITS * i + (DEC_UNITS * B + j - 1))

                    def block_scores(j):
                        pe.wait_ge(d_free, DEC_UNITS * i + (DEC_UNITS * B + j + 1))
                        m = 1 if j < PAGES else 0
                        at = 2 * CH + j * P if j < PAGES else 4 * CH + (j - PAGES) * P
                        for a in range(HP):
                            last = pe.matmul(psum[0:SAMPLE, at:at + P], qblk[:, m, a * SAMPLE:(a + 1) * SAMPLE],
                                             kstage[:, j % 4, a * P:(a + 1) * P], start=a == 0, stop=a == HP - 1)
                        last.then_inc(d_scored, 1)

                    def new_scores(m, at, done):
                        for a in range(HP):
                            last = pe.matmul(psum[0:SAMPLE, at:at + SAMPLE], qblk[:, m, a * SAMPLE:(a + 1) * SAMPLE],
                                             kT[:, HP * m + a, SEQ:TOK], start=a == 0, stop=a == HP - 1)
                        last.then_inc(done, 1)

                    pe.wait_ge(qblk_ready, i + (B + 1))
                    new_scores(1, 7 * CH, d_new)
                    pe.wait_ge(ksb_in, 16 * PAGES * i + 16 * PAGES * (B + 1))
                    for j in range(PAGES + SWA_TILES):
                        wait_bank(j)
                        key_unit(j)
                        if j:
                            block_scores(j - 1)
                    block_scores(PAGES + SWA_TILES - 1)
                    new_scores(0, 5 * CH + P, d_new)

                    def values(m, count, v, vnew):
                        at = (7 if m else 6) * CH
                        pT = decT[:, m, :].rearrange("p (j q) -> p j q", q=SAMPLE)
                        for a in range(HP):
                            o = psum[:, at + a * SAMPLE:at + (a + 1) * SAMPLE]
                            for j in range(count):
                                pe.matmul(o, v[:, j, a * P:(a + 1) * P], pT[:, j, :], start=j == 0, stop=False)
                            last = pe.matmul(o, vnew[:, a * P:(a + 1) * P], pT[0:SAMPLE, PAGES, :], start=False, stop=True)
                        last.then_inc(d_o, 1)

                    def turn(dst, src):
                        return pe.matmul(dst, src, ident[0:SAMPLE, 0:SAMPLE], start=True, stop=True)

                    pe.wait_ge(d_prob, 2 * i + (2 * B + 1))
                    wait_bank(13)
                    for j in range(PAGES - 1):
                        last = turn(bank(1)[:, j * SAMPLE:(j + 1) * SAMPLE], probs[0:SAMPLE, j * P:(j + 1) * P])
                    last.then_inc(d_full, 1)
                    wait_bank(14)
                    turn(bank(0)[:, 0:SAMPLE], probs[0:SAMPLE, PAST - P:PAST])
                    turn(bank(0)[0:SAMPLE, SAMPLE:2 * SAMPLE], probs[0:SAMPLE, PAST:PAST + SAMPLE]).then_inc(d_full, 1)
                    pe.wait_ge(vsb_in, 16 * PAGES * i + 16 * PAGES * (B + 1))
                    pe.wait_ge(d_free, DEC_UNITS * i + (DEC_UNITS * B + 15))
                    values(1, PAGES, v_sb, kv[0:SAMPLE, 2, 3, :])
                    pe.wait_ge(d_prob, 2 * i + (2 * B + 2))
                    for j in range(SWA_TILES):
                        turn(bank(1)[:, j * SAMPLE:(j + 1) * SAMPLE], swa_s[:, j * P:(j + 1) * P])
                    turn(bank(1)[0:SAMPLE, SWA_TILES * SAMPLE:(SWA_TILES + 1) * SAMPLE],
                         swa_s[:, SWA_KEYS:SWA_KEYS + SAMPLE]).then_inc(d_full, 1)
                    pe.wait_ge(vswa_in, 16 * 5 * i + 16 * 5 * (B + 1))
                    pe.wait_ge(d_free, DEC_UNITS * i + (DEC_UNITS * B + 16))
                    values(0, SWA_TILES, v_swa, kv[0:SAMPLE, 2, 1, :])
                    pe.wait_ge(d_ocopied, 2 * i + (2 * B + 2))

                for g in range(2):
                    transpose_unit(tp_at[L, "sample"] + g, [oS[:, 4 * g + j, :] for j in range(4)],
                                   lambda b: [b[0:SAMPLE, j * P:(j + 1) * P] for j in range(4)])
                src_tok = o_or_acc
                token_to_feature(tp_at[L, "merge"], [lambda t: pe.wait_ge(rms_scaled, T * L + t + 1)] * T)
                pe.wait_ge(tp_free, tp_at[L, "mix"])
                for c in range(2):
                    w = arrived(pe, (L, "wo", c))
                    for t in range(T):
                        b = bank(2 + T * c + t)
                        for k in range(KD):
                            last = pe.matmul(b[0:ROWS[t], :], qT[:, k, t * P:t * P + ROWS[t]], w[:, k, :],
                                             start=k == 0, stop=k == KD - 1)
                        last.then_inc(wo_done, 1)
                src_tok = x_tok
                token_to_feature(tp_at[L, "mix"], [lambda t: pe.wait_ge(ln_done, 2 * T * L + t + 1)] * T)
                pe.wait_ge(tp_free, tp_at[L, "mix"] + 6)
                pe.wait_ge(wo_added, 6 * (L + 1))
                if L == 0:
                    for c, m in DENSE_CHUNKS:
                        wg, wu = arrived(pe, (L, "g", c)), arrived(pe, (L, "u", c))
                        for j in range(m):
                            f = FPC * c + j
                            if f >= 2:
                                pe.wait_ge(gu_free, f - 1)
                            for a, w in enumerate((wg, wu)):
                                for k in range(KD):
                                    last = pe.matmul(bank(2 + 2 * (f % 2) + a)[:, 0:TOK], w[:, k, j * P:(j + 1) * P],
                                                     xTv[:, k, :], start=k == 0, stop=k == KD - 1)
                                last.then_inc(gu_done, 1)
                    pe.wait_ge(gu_free, DENSE_F)
                    for c, m in DENSE_CHUNKS:
                        w = arrived(pe, (L, "d", c))
                        for j in range(m):
                            f = FPC * c + j
                            for t in range(T):
                                for h in range(2):
                                    last = pe.matmul(bank(2 + 2 * t + h)[0:ROWS[t], :], hT[:, f, t * P:t * P + ROWS[t]],
                                                     w[:, j, h * CH:(h + 1) * CH], start=f == 0, stop=f == DENSE_F - 1)
                        last.then_inc(down_done, 1)
                    token_to_feature(tp_at[L, "ffn"], [lambda t: pe.wait_ge(ln_done, T + t + 1)] * T)

            pe.wait_ge(router_in, 16 * 8)
            for t in range(T):
                for k in range(KD):
                    last = pe.matmul(bank(2)[0:ROWS[t], t * EXPERTS:(t + 1) * EXPERTS], xTv[:, k, t * P:t * P + ROWS[t]],
                                     w_router[:, k, :], start=k == 0, stop=k == KD - 1)
            last.then_inc(logits_done, 1)
            pe.wait_ge(chosen_ready, 1)
            for t in range(T):
                for s in range(t + 1):
                    pe.matmul(bank(3)[:, t * EXPERTS:(t + 1) * EXPERTS], earlier if s == t else ones, chosen[:, s, :],
                              start=s == 0, stop=s == t)
            for s in range(T):
                last = pe.matmul(bank(3)[:, T * EXPERTS:(T + 1) * EXPERTS], ones, chosen[:, s, :],
                                 start=s == 0, stop=s == T - 1)
            last.then_inc(ranks_done, 1)
            pe.wait_ge(plan_ready, 1)

            def gather(value):
                pe.wait_ge(pick_ready, value)
                for g in range(2):
                    for j in range(4):
                        k = 4 * g + j
                        for t in range(T):
                            last = pe.matmul(bank(g)[:, j * ITEM:(j + 1) * ITEM],
                                             x_tok[0:ROWS[t], t, k * P:(k + 1) * P], pick[0:ROWS[t], t, :],
                                             start=t == 0, stop=t == T - 1)
                    last.then_inc(gathered, 1)

            def item(i):
                pe.wait_ge(gather_copied, 2 * i + 2)
                for c in range(MOE_CHUNKS):
                    b = 2 + 2 * (c % 2)
                    if c >= 2:
                        pe.wait_ge(e_h, MOE_CHUNKS * i + (c - 1))
                    for a in range(2):
                        item_loaded(pe, 2 * c + a, i)
                        w = slot_view(item_slot(2 * c + a))
                        for j in range(FPC):
                            for k in range(KD):
                                last = pe.matmul(bank(b + a)[:, j * ITEM:(j + 1) * ITEM],
                                                 w[:, k, j * P:(j + 1) * P], xg[:, k, :], start=k == 0, stop=k == KD - 1)
                        last.then_inc(e_gu, 1)
                pe.wait_ge(added, 6 * i + 6)
                for t in range(T):
                    last = pe.transpose(bank(0)[:, t * P:t * P + ROWS[t]], pick[0:ROWS[t], t, :],
                                        ident[0:ROWS[t], 0:ROWS[t]])
                last.then_inc(pick_turned, 1)
                pe.wait_ge(e_h, MOE_CHUNKS * i + (MOE_CHUNKS - 1))
                for c in range(MOE_CHUNKS):
                    if c == MOE_CHUNKS - 1:
                        pe.wait_ge(e_h, MOE_CHUNKS * i + MOE_CHUNKS)
                    item_loaded(pe, 2 * MOE_CHUNKS + c, i)
                    w = slot_view(item_slot(2 * MOE_CHUNKS + c), FPC)
                    for j in range(FPC):
                        f = FPC * c + j
                        for h in range(2):
                            last = pe.matmul(bank(6 + h), hE[:, f, :], w[:, j, h * CH:(h + 1) * CH],
                                             start=f == 0, stop=f == MOE_F - 1)
                    last.then_inc(e_down, 1)
                pe.wait_ge(pickT_copied, i + 1)
                gather(i + 2)
                for n in range(2 * T):
                    t, h = divmod(n, 2)
                    if n == 0:
                        pe.wait_ge(y_copied, i + 1)
                    elif n == 2:
                        pe.wait_ge(gather_copied, 2 * i + 4)
                    elif n >= 4:
                        pe.wait_ge(added, 6 * i + (n + 3))
                    pe.matmul(bank((6, 7, 0, 1)[n % 4])[0:ROWS[t], :], pickT[:, t * P:t * P + ROWS[t]],
                              y_item[:, h * CH:(h + 1) * CH], start=True, stop=True).then_inc(combined, 1)

            gather(1)
            count = pe.value_load(plan[0:1, 0:1], min_val=0, max_val=ITEMS)
            with pe.Fori(0, ITEMS) as i:
                with pe.If(i < count):
                    item(i)

        @block.scalar
        def _(act):
            st = Steps(act, act_step)

            def copy_unit(u, dst, src, scale=None):
                act.wait_ge(tp_full, u + 1)
                act.copy(dst, src(bank(u % 2))).then_inc(tp_free, 1)

            def to_feature(u, dst, gains=None):
                for t in range(T):
                    r = ROWS[t]
                    for g in range(2):
                        n = u + 2 * t + g
                        src = bank(n % 2)[:, 0:4 * r].rearrange("p (j r) -> p j r", j=4)
                        out = dst[:, 4 * g:4 * g + 4, t * P:t * P + r]
                        act.wait_ge(tp_full, n + 1)
                        if gains is None:
                            act.copy(out, src).then_inc(tp_free, 1)
                        else:
                            for j in range(4):
                                last = act.activation(out[:, j, :], src[:, j, :], ACT.Copy, scale=gains(4 * g + j))
                            last.then_inc(tp_free, 1)

            to_feature(0, xTv)
            for L in range(LAYERS):
                for m in range(2):
                    for t in range(T):
                        r = ROWS[t]
                        copy_unit(tp_at[L, "k"] + T * m + t, kT[:, HP * m:HP * m + HP, t * P:t * P + r],
                                  lambda b: b[:, 0:4 * r].rearrange("p (j r) -> p j r", j=4))
                n0 = 2 * HEADS * L
                if L == 0:
                    act.wait_ge(tables_in, 16 * 10)

                def exps(n):
                    m, h = divmod(n - n0, HEADS)
                    e = probs[:, 384 * (n % 2):384 * (n % 2) + 384]
                    s = stat[:, n % 2, :]
                    act.wait_ge(masked, n + 1)
                    if m == 0:
                        for q, cols in enumerate((slice(0, P), slice(P, 3 * P))):
                            last = act.activation(e[:, cols], e[:, cols], ACT.Exp, bias=s[:, q:q + 1],
                                                  accum_out=s[:, 2 + q:3 + q])
                    else:
                        last = act.activation(e, e, ACT.Exp, bias=sb_bias[:, L, h:h + 1])
                    last.then_inc(expd, 1)

                exps(n0)
                for n in range(n0, n0 + 2 * HEADS):
                    if n + 1 < n0 + 2 * HEADS:
                        exps(n + 1)
                    if n >= 2:
                        act.wait_ge(pv_done, n - 1)
                    copy_unit(tp_at[L, "prompt"] + n - n0, probT[:, n % 2, :], lambda b: b[:, 0:3 * P])
                B = NS * L
                with act.Fori(0, NS) as i:
                    def full(j):
                        act.wait_ge(d_full, DEC_UNITS * i + (DEC_UNITS * B + j + 1))

                    for j in range(PAGES + SWA_TILES):
                        full(j)
                        if j >= 4:
                            act.wait_ge(d_scored, 13 * i + (13 * B + j - 3))
                        act.copy(kstage[:, j % 4, :], bank(j % 2)).then_inc(d_free, 1)
                        if j == PAGES + 1:
                            act.wait_ge(d_scored, 13 * i + (13 * B + PAGES))
                            act.activation(probs[0:SAMPLE, 0:PAST], psum[0:SAMPLE, 2 * CH:4 * CH], ACT.Exp,
                                           bias=sb_bias_rows[:, L:L + 1], scale=SCALE).then_inc(d_exp, 1)
                            act.wait_ge(d_newm, i + (B + 1))
                            act.activation(probs[0:SAMPLE, PAST:PAST + SAMPLE], probs[0:SAMPLE, PAST:PAST + SAMPLE], ACT.Exp,
                                           bias=sb_bias_rows[:, L:L + 1]).then_inc(d_exp, 1)
                    act.wait_ge(d_biased, i + (B + 1))
                    act.activation(swa_s, swa_s, ACT.Exp, bias=dstat[:, 0:1], accum_out=dstat[:, 1:2]).then_inc(d_swaexp, 1)
                    full(13)
                    last8 = (PAGES - 1) * SAMPLE
                    act.copy(decT[:, 1, 0:last8], bank(1)[:, 0:last8]).then_inc(d_free, 1)
                    full(14)
                    act.copy(decT[:, 1, last8:last8 + SAMPLE], bank(0)[:, 0:SAMPLE])
                    act.copy(decT[0:SAMPLE, 1, last8 + SAMPLE:last8 + 2 * SAMPLE], bank(0)[0:SAMPLE, SAMPLE:2 * SAMPLE])\
                        .then_inc(d_free, 1)
                    full(15)
                    act.copy(decT[:, 0, 0:SWA_TILES * SAMPLE], bank(1)[:, 0:SWA_TILES * SAMPLE])
                    act.copy(decT[0:SAMPLE, 0, PAGES * SAMPLE:(PAGES + 1) * SAMPLE],
                             bank(1)[0:SAMPLE, SWA_TILES * SAMPLE:(SWA_TILES + 1) * SAMPLE]).then_inc(d_free, 1)
                for g in range(2):
                    copy_unit(tp_at[L, "sample"] + g, o_or_acc[0:SAMPLE, 2, 4 * g * P:4 * (g + 1) * P], lambda b: b[0:SAMPLE, :])
                for t in range(T):
                    r = ROWS[t]
                    if t == 0:
                        act.wait_ge(o_copied, n0 + 2 * HEADS)
                    if t == 2:
                        act.wait_ge(tp_free, tp_at[L, "merge"])
                    for m in range(2):
                        st.did(act.activation(mean_sq_out[0:r, :], o_or_acc[0:r, t, m * WID:(m + 1) * WID], ACT.Square,
                                              accum_out=norm[0:r, t, m:m + 1]))
                    act.wait_ge(sq_done, T * L + t + 1)
                    act.activation(norm[0:r, t, 4:6], norm[0:r, t, 2:4], ACT.Sqrt).then_inc(rms_root, 1)
                to_feature(tp_at[L, "merge"], qT, lambda k: g_mix[:, L, k:k + 1])

                def ln_roots(base):
                    for t in range(T):
                        act.wait_ge(var_ready, base + t + 1)
                        act.activation(norm[0:ROWS[t], t, 23:24], norm[0:ROWS[t], t, 22:23], ACT.Sqrt).then_inc(ln_root, 1)

                ln_roots(2 * T * L)
                to_feature(tp_at[L, "mix"], xTv)
                if L == 0:
                    for f in range(DENSE_F):
                        act.wait_ge(gu_done, 2 * f + 1)
                        if f >= 2:
                            act.wait_ge(gu_free, f - 1)
                        act.activation(silu_r[f % 2][:, 0:TOK], bank(2 + 2 * (f % 2))[:, 0:TOK], ACT.Exp, scale=-1.0)\
                            .then_inc(gu_exp, 1)
                    ln_roots(T)
                    to_feature(tp_at[L, "ffn"], xTv)
            act.wait_ge(logits_copied, 1)
            act.activation(vals[:, :, 3:4], vals[:, :, 2:3], ACT.Exp).then_inc(gate_exp2, 1)
            act.wait_ge(plan_ready, 1)

            def copy_gathered(i):
                for g in range(2):
                    act.wait_ge(gathered, 2 * i + (g + 1))
                    act.copy(xg[:, 4 * g:4 * g + 4, :], bank(g).rearrange("p (k s) -> p k s", k=4)).then_inc(gather_copied, 1)

            copy_gathered(0)
            count = act.value_load(plan[0:1, 0:1], min_val=0, max_val=ITEMS)
            with act.Fori(0, ITEMS) as i:
                with act.If(i < count):
                    for c in range(MOE_CHUNKS):
                        act.wait_ge(e_gu, 2 * MOE_CHUNKS * i + (2 * c + 1))
                        if c >= 2:
                            act.wait_ge(e_h, MOE_CHUNKS * i + (c - 1))
                        act.activation(silu_r[c % 2], bank(2 + 2 * (c % 2)), ACT.Exp, scale=-1.0).then_inc(e_exp, 1)
                    act.wait_ge(pick_turned, i + 1)
                    act.copy(pickT, bank(0)[:, 0:TOK]).then_inc(pickT_copied, 1)
                    act.wait_ge(e_down, MOE_CHUNKS * i + MOE_CHUNKS)
                    act.copy(y_item, psum[:, 6 * CH:8 * CH]).then_inc(y_copied, 1)
                    copy_gathered(i + 1)
            for t in range(T):
                act.wait_ge(var_ready, 3 * T + t + 1)
                act.activation(norm[0:ROWS[t], t, 23:24], norm[0:ROWS[t], t, 22:23], ACT.Sqrt).then_inc(ln_root, 1)

        @block.vector
        def _(v):
            st = Steps(v, dve_step)

            def layer_norm(t, base, gb_in, st):
                r = ROWS[t]
                x = x_tok[0:r, t, :]
                n = norm[0:r, t, :]
                for h in range(2):
                    st.did(v.bn_stats(n[:, 6 + 6 * h:12 + 6 * h], x[:, h * CH:(h + 1) * CH]))
                st.did(v.bn_aggr(n[:, 20:22], n[:, 6:18]))
                v.tensor_scalar(n[:, 22:23], n[:, 21:22], LN_EPS, None, ALU.add).then_inc(var_ready, 1)
                v.wait_ge(ln_root, base + t + 1)
                st.did(v.reciprocal(n[:, 19:20], n[:, 23:24]))
                st.did(v.tensor_scalar(x, x, n[:, 20:21], n[:, 19:20], ALU.subtract, ALU.mult))
                v.wait_ge(ln_in, gb_in)
                st.did(v.tensor_tensor(x, x, ln_gb[0:r, 0, :], ALU.mult))
                v.tensor_tensor(x, x, ln_gb[0:r, 1, :], ALU.add).then_inc(ln_done, 1)

            st.did(v.memset(qblk[:, :, :], 0.0))
            for L in range(LAYERS):
                unit = PROJ_UNITS * L
                for c in range(6):
                    for n in range(UNITS_Q if c % 3 == 0 else UNITS_KV):
                        b = bank(2 + unit % 6)
                        if c % 3 == 0:
                            v.wait_ge(proj_done, unit + 1)
                            v.tensor_copy(qT[:, HP * (c // 3) + n, :], b[:, 0:TOK]).then_inc(proj_free, 1)
                        else:
                            v.wait_ge(proj_done, unit + 1)
                            v.tensor_copy(kv[0:ROWS[n], n, 2 * (c // 3) + c % 3 - 1, :], b[0:ROWS[n], :]).then_inc(proj_free, 1)
                        unit += 1
                n0 = 2 * HEADS * L
                if L == 0:
                    v.wait_ge(tables_in, 16 * 10)
                v.wait_ge(proj_free, PROJ_UNITS * (L + 1))

                def mask(n):
                    m, h = divmod(n - n0, HEADS)
                    e = probs[:, 384 * (n % 2):384 * (n % 2) + 384]
                    s = stat[:, n % 2, :]
                    tmp = keeps[:, 0:384]
                    if m == 0:
                        st.did(v.scalar_tensor_tensor(tmp, prompt_tab[:, 0, :], -(2.0 ** (-8.0 * (h + 1) / HEADS)),
                                                      prompt_tab[:, 1, :], ALU.mult, ALU.add))
                    v.wait_ge(scored, n + 1)
                    score = v.scalar_tensor_tensor(e, bank(2 + n % 2)[:, 0:384], SCALE,
                                                   tmp if m == 0 else prompt_tab[:, 2, :], ALU.mult, ALU.add)
                    if m == 0:
                        st.did(score)
                        st.go(v.reduce_max(s[:, 0:1], e[:, 0:P], AX, negate=True))
                        v.reduce_max(s[:, 1:2], e[:, P:3 * P], AX, negate=True).then_inc(masked, 1)
                    else:
                        score.then_inc(masked, 1)

                def weigh(n):
                    m, h = divmod(n - n0, HEADS)
                    e = probs[:, 384 * (n % 2):384 * (n % 2) + 384]
                    s = stat[:, n % 2, :]
                    v.wait_ge(expd, n + 1)
                    if m == 0:
                        v.reciprocal(s[:, 4:6], s[:, 2:4]).then_inc(prob_ready, 1)
                        return
                    keep = keeps[:, 0:3 * P + 2]
                    halves = ((slice(0, P), slice(0, P), slice(1, P + 1)),
                              (slice(P, 3 * P), slice(P + 1, 3 * P + 1), slice(P + 2, 3 * P + 2)))
                    st.go(v.memset(keep[:, P:P + 1], 1.0))
                    st.go(v.memset(keep[:, 3 * P + 1:3 * P + 2], 1.0))
                    for cols, at, _ in halves:
                        st.did(v.tensor_scalar(keep[:, at], e[:, cols], BIG, 1.0, ALU.min, ALU.add))
                    for cols, at, _ in halves:
                        st.did(v.reciprocal(keep[:, at], keep[:, at]))
                    for cols, at, _ in halves:
                        st.did(v.scalar_tensor_tensor(e[:, cols], e[:, cols], BIG, keep[:, at], ALU.min, ALU.mult))
                    for cols, at, _ in halves:
                        k = keep[:, at]
                        st.did(v.tensor_tensor_scan(k[:, ::-1], k[:, ::-1], k[:, ::-1], 1.0, ALU.mult, ALU.min))
                    cols, _, later = halves[0]
                    st.go(v.tensor_tensor(e[:, cols], e[:, cols], keep[:, later], ALU.mult))
                    cols, _, later = halves[1]
                    v.tensor_tensor(e[:, cols], e[:, cols], keep[:, later], ALU.mult).then_inc(prob_ready, 1)

                def take(n):
                    m, h = divmod(n - n0, HEADS)
                    s = stat[:, n % 2, :]
                    v.wait_ge(pv_done, n + 1)
                    b = bank(4 + n % 2)
                    o = o_or_acc[:, 0:2, m * WID + h * HD:m * WID + (h + 1) * HD]
                    if m == 0:
                        st.go(v.tensor_scalar(o[:, 0, :], b[:, 0:HD], s[:, 4:5], None, ALU.mult))
                        v.tensor_scalar(o[:, 1, :], b[:, HD:2 * HD], s[:, 5:6], None, ALU.mult).then_inc(o_copied, 1)
                    else:
                        v.tensor_copy(o, b[:, 0:2 * HD].rearrange("p (t d) -> p t d", t=2)).then_inc(o_copied, 1)

                mask(n0)
                for n in range(n0, n0 + 2 * HEADS):
                    if n > n0:
                        take(n - 1)
                    if n + 1 < n0 + 2 * HEADS:
                        v.wait_ge(prob_ready, n) if n > n0 else None
                        v.wait_ge(o_copied, n) if n > n0 else None
                        mask(n + 1)
                    weigh(n)
                take(n0 + 2 * HEADS - 1)
                B = NS * L
                K = 11
                entry = st.n
                v.wait_ge(tp_free, tp_at[L, "prompt"])
                with v.Fori(0, NS) as i:
                    st.base, st.n = K * i, entry
                    for m in range(2):
                        for u in range(2):
                            rows = slice(HD * u, HD * u + HD)
                            dst = qblk[rows, m, 4 * u:4 * u + 124].rearrange("p (a x) -> p a x", x=4)[:, ::10, :]
                            last = v.tensor_copy(dst, qT[rows, HP * m:HP * m + HP, bass.ds(DEC * i + SEQ, DEC)])
                            if (m, u) == (1, 1):
                                last.then_inc(qblk_ready, 1)
                            else:
                                st.go(last)
                    v.wait_ge(d_new, 2 * i + (2 * B + 1))
                    v.scalar_tensor_tensor(probs[0:SAMPLE, PAST:PAST + SAMPLE], psum[0:SAMPLE, 7 * CH:7 * CH + SAMPLE], SCALE,
                                           new_bias[:, 1, bass.ds(SAMPLE * i, SAMPLE)], ALU.mult, ALU.add).then_inc(d_newm, 1)
                    v.wait_ge(d_exp, 2 * i + (2 * B + 2))
                    e, keep = probs[0:SAMPLE, 0:PAST + SAMPLE], keeps[0:SAMPLE, 0:PAST + SAMPLE]
                    st.go(v.memset(keeps[0:SAMPLE, PAST + SAMPLE:PAST + SAMPLE + 1], 1.0))
                    st.did(v.tensor_scalar(keep, e, BIG, 1.0, ALU.min, ALU.add))
                    st.did(v.reciprocal(keep, keep))
                    st.did(v.scalar_tensor_tensor(e, e, BIG, keep, ALU.min, ALU.mult))
                    st.did(v.tensor_tensor_scan(keep[:, ::-1], keep[:, ::-1], keep[:, ::-1], 1.0, ALU.mult, ALU.min))
                    v.tensor_tensor(e, e, keeps[0:SAMPLE, 1:PAST + SAMPLE + 1], ALU.mult).then_inc(d_prob, 1)
                    v.wait_ge(d_new, 2 * i + (2 * B + 2))
                    st.go(v.scalar_tensor_tensor(swa_s[:, 0:SWA_KEYS], psum[0:SAMPLE, 4 * CH:4 * CH + SWA_KEYS], SCALE,
                                                 past_bias[:, :], ALU.mult, ALU.add))
                    st.did(v.scalar_tensor_tensor(swa_s[:, SWA_KEYS:SWA_KEYS + SAMPLE],
                                                  psum[0:SAMPLE, 5 * CH + P:5 * CH + P + SAMPLE], SCALE,
                                                  new_bias[:, 0, bass.ds(SAMPLE * i, SAMPLE)], ALU.mult, ALU.add))
                    v.reduce_max(dstat[:, 0:1], swa_s, AX, negate=True).then_inc(d_biased, 1)
                    v.wait_ge(d_swaexp, i + (B + 1))
                    st.did(v.reciprocal(dstat[:, 2:3], dstat[:, 1:2]))
                    v.tensor_scalar(swa_s, swa_s, dstat[:, 2:3], None, ALU.mult).then_inc(d_prob, 1)
                    for n, m in enumerate((1, 0)):
                        v.wait_ge(d_o, 2 * i + (2 * B + n + 1))
                        for u in range(2):
                            at = (7 if m else 6) * CH + 4 * u
                            src = psum[HD * u:HD * u + HD, at:at + 124].rearrange("p (a x) -> p a x", x=4)[:, ::10, :]
                            last = v.tensor_copy(oS[HD * u:HD * u + HD, HP * m:HP * m + HP, bass.ds(DEC * i, DEC)], src)
                            if u == 1:
                                last.then_inc(d_ocopied, 1)
                    st_used = st.n - entry
                assert st_used == K, st_used
                st.base, st.n = None, entry + K * NS
                for t in range(T):
                    r = ROWS[t]
                    n = norm[0:r, t, :]
                    v.wait_ge(act_step, 2 * T * L + 2 * (t + 1))
                    v.tensor_scalar(n[:, 2:4], n[:, 0:2], 1.0 / WID, RMS_EPS, ALU.mult, ALU.add).then_inc(sq_done, 1)
                    v.wait_ge(rms_root, T * L + t + 1)
                    st.did(v.reciprocal(n[:, 18:20], n[:, 4:6]))
                    for m in range(2):
                        o = o_or_acc[0:r, t, m * WID:(m + 1) * WID]
                        last = v.tensor_scalar(o, o, n[:, 18 + m:19 + m], None, ALU.mult)
                        if m == 0:
                            st.go(last)
                        else:
                            last.then_inc(rms_scaled, 1)
                for c in range(2):
                    for t in range(T):
                        r = ROWS[t]
                        v.wait_ge(wo_done, 6 * L + T * c + t + 1)
                        x = x_tok[0:r, t, c * CH:(c + 1) * CH]
                        v.scalar_tensor_tensor(x, x, ALPHA, bank(2 + T * c + t)[0:r, :], ALU.mult, ALU.add).then_inc(wo_added, 1)
                v.wait_ge(wo_added, 6 * (L + 1))
                for t in range(T):
                    layer_norm(t, 2 * T * L, 64 * L + 32, st)
                if L == 0:
                    v.wait_ge(stored_kv, 160 * (L + 1))
                    v.wait_ge(stored_win, 16 * 2 * NS * (L + 1))
                    for f in range(DENSE_F):
                        a = 2 + 2 * (f % 2)
                        rr, tt = silu_r[f % 2][:, 0:TOK], silu_t[f % 2][:, 0:TOK]
                        v.wait_ge(gu_exp, f + 1)
                        st.did(v.tensor_scalar(rr, rr, BIG, 1.0, ALU.min, ALU.add))
                        st.did(v.reciprocal(rr, rr))
                        st.did(v.tensor_tensor(tt, rr, bank(a)[:, 0:TOK], ALU.mult))
                        v.wait_ge(gu_done, 2 * f + 2)
                        v.tensor_tensor(hT[:, f, :], tt, bank(a + 1)[:, 0:TOK], ALU.mult).then_inc(gu_free, 1)
                    v.wait_ge(down_done, len(DENSE_CHUNKS))
                    for t in range(T):
                        r = ROWS[t]
                        v.scalar_tensor_tensor(x_tok[0:r, t, :], x_tok[0:r, t, :], ALPHA,
                                               psum[0:r, (2 + 2 * t) * CH:(4 + 2 * t) * CH], ALU.mult, ALU.add)\
                            .then_inc(ffn_added, 2)
                        v.wait_ge(ffn_added, 2 * t + 2)
                        layer_norm(t, T, 64, st)
            v.wait_ge(router_in, 16 * 8)
            st.did(v.memset(logit, 0.0))
            v.wait_ge(logits_done, 1)
            for t in range(T):
                r = ROWS[t]
                st.did(v.tensor_copy(logit[0:r, t, :], bank(2)[0:r, t * EXPERTS:(t + 1) * EXPERTS]))
            for n, hot in enumerate((hot1, hot2)):
                st.did(v.reduce_max(vals[:, :, n:n + 1], logit, AX))
                st.did(v.tensor_tensor(tie, logit, vals[:, :, n:n + 1].to_broadcast([P, T, EXPERTS]), ALU.is_equal))
                st.did(v.tensor_tensor(tie, tie, descending, ALU.mult))
                st.did(v.reduce_max(vals[:, :, 4:5], tie, AX))
                st.did(v.tensor_tensor(hot, descending, vals[:, :, 4:5].to_broadcast([P, T, EXPERTS]), ALU.is_equal))
                if n == 0:
                    st.did(v.scalar_tensor_tensor(logit, hot, NEG, logit, ALU.mult, ALU.add))
            v.tensor_tensor(vals[:, :, 2:3], vals[:, :, 1:2], vals[:, :, 0:1], ALU.subtract).then_inc(logits_copied, 1)
            st.did(v.tensor_tensor(chosen, hot1, hot2, ALU.add))
            v.tensor_tensor(chosen, chosen, is_token, ALU.mult).then_inc(chosen_ready, 1)
            v.wait_ge(gate_exp2, 1)
            st.did(v.tensor_scalar(vals[:, :, 5:6], vals[:, :, 3:4], 1.0, None, ALU.add))
            st.did(v.reciprocal(vals[:, :, 6:7], vals[:, :, 5:6]))
            st.did(v.tensor_tensor(vals[:, :, 7:8], vals[:, :, 3:4], vals[:, :, 6:7], ALU.mult))
            st.did(v.tensor_tensor(hot1, hot1, vals[:, :, 6:7].to_broadcast([P, T, EXPERTS]), ALU.mult))
            st.did(v.tensor_tensor(hot2, hot2, vals[:, :, 7:8].to_broadcast([P, T, EXPERTS]), ALU.mult))
            st.did(v.tensor_tensor(gates, hot1, hot2, ALU.add))
            v.wait_ge(ranks_done, 1)
            v.wait_ge(chosen_ready, 1)
            st.did(v.tensor_scalar(ranks, bank(3)[:, 0:T * EXPERTS].rearrange("p (t e) -> p t e", t=T), 1.0, None, ALU.add))
            st.did(v.tensor_tensor(ranks, ranks, chosen, ALU.mult))
            tokens, items, upto, first = (per_expert[:, a, :] for a in range(4))
            st.did(v.tensor_copy(tokens, bank(3)[:, T * EXPERTS:(T + 1) * EXPERTS]))
            st.did(v.tensor_scalar(items, tokens, 0.0, None, ALU.is_gt))
            for p in range(1, PASSES):
                st.did(v.scalar_tensor_tensor(items, tokens, float(ITEM * p), items, ALU.is_gt, ALU.add))
            st.did(v.tensor_scalar(first, items, 0.0, None, ALU.mult))
            st.did(v.tensor_tensor_scan(upto, items, first, 0.0, ALU.add, ALU.add))
            st.did(v.tensor_tensor(first, upto, items, ALU.subtract))

            def every_item(x):
                return x.unsqueeze(1).to_broadcast([P, NI, EXPERTS])

            st.did(v.tensor_tensor(first_rank, item_number, every_item(first), ALU.subtract))
            st.did(v.tensor_tensor(of_item, first_rank, every_item(items), ALU.is_lt))
            st.did(v.tensor_scalar(wide, first_rank, 0.0, None, ALU.is_ge))
            st.did(v.tensor_tensor(of_item, of_item, wide, ALU.mult))
            st.did(v.tensor_scalar(first_rank, first_rank, float(ITEM), None, ALU.mult))
            for t in range(T):
                st.did(v.tensor_tensor(wide, every_item(ranks[:, t, :]), first_rank, ALU.subtract))
                st.did(v.tensor_tensor(wide, wide, of_item, ALU.mult))
                st.did(v.reduce_sum(rank_of[:, t, :], wide, AX))
                st.did(v.tensor_tensor(wide, every_item(gates[:, t, :]), of_item, ALU.mult))
                st.did(v.reduce_sum(gate_of[:, t, :], wide, AX))
            st.did(v.tensor_tensor(wide, expert_number, of_item, ALU.mult))
            st.did(v.reduce_sum(plan_f[:, 1:NI + 1], wide, AX))
            st.did(v.tensor_copy(plan_f[:, 0:1], upto[:, EXPERTS - 1:EXPERTS]))
            v.memset(o_or_acc[:, :, :], 0.0).then_inc(added, 6)
            v.wait_ge(added, 6)
            v.tensor_copy(plan[0:1, 0:NI + 1], plan_f[0:1, :]).then_inc(plan_ready, 1)
            v.wait_ge(plan_ready, 1)
            v.wait_ge(stored_kv, 160 * LAYERS)
            v.wait_ge(stored_win, 16 * 2 * NS * LAYERS)

            def make_pick(i, steps):
                for t in range(T):
                    r = rank_of[0:ROWS[t], t, :]
                    last = v.tensor_scalar(pick[0:ROWS[t], t, :], slot_number[0:ROWS[t], :], r[:, bass.ds(i, 1)], None, ALU.is_equal)
                    if t < T - 1:
                        steps.go(last)
                last.then_inc(pick_ready, 1)

            make_pick(0, st)
            K = 2 + 3 * MOE_CHUNKS
            entry = st.n
            count = v.value_load(plan[0:1, 0:1], min_val=0, max_val=ITEMS)
            with v.Fori(0, ITEMS) as i:
                with v.If(i < count):
                    st.base, st.n = K * i, entry
                    for c in range(MOE_CHUNKS):
                        b = 2 + 2 * (c % 2)
                        rr, tt = silu_r[c % 2], silu_t[c % 2]
                        v.wait_ge(e_exp, MOE_CHUNKS * i + (c + 1))
                        st.did(v.tensor_scalar(rr, rr, BIG, 1.0, ALU.min, ALU.add))
                        st.did(v.reciprocal(rr, rr))
                        st.did(v.tensor_tensor(tt, rr, bank(b), ALU.mult))
                        v.wait_ge(e_gu, 2 * MOE_CHUNKS * i + (2 * c + 2))
                        v.tensor_tensor(hE[:, FPC * c:FPC * (c + 1), :], tt.rearrange("p (f s) -> p f s", f=FPC),
                                        bank(b + 1).rearrange("p (f s) -> p f s", f=FPC), ALU.mult).then_inc(e_h, 1)
                    v.wait_ge(pick_turned, i + 1)
                    make_pick(i + 1, st)
                    v.wait_ge(added, 6 * i + 6)
                    for n in range(2 * T):
                        t, h = divmod(n, 2)
                        v.wait_ge(combined, 6 * i + (n + 1))
                        acc = o_or_acc[0:ROWS[t], t, h * CH:(h + 1) * CH]
                        v.scalar_tensor_tensor(acc, bank((6, 7, 0, 1)[n % 4])[0:ROWS[t], :],
                                               gate_of[0:ROWS[t], t, bass.ds(i, 1)], acc, ALU.mult, ALU.add).then_inc(added, 1)
                    assert st.n - entry == K, st.n - entry
            tail = Steps(v, dve_tail)
            v.wait_ge(added, count * 6 + 6)
            for t in range(T):
                r = ROWS[t]
                tail.did(v.scalar_tensor_tensor(x_tok[0:r, t, :], x_tok[0:r, t, :], ALPHA, o_or_acc[0:r, t, :], ALU.mult, ALU.add))
                layer_norm(t, 3 * T, 128, tail)


_OUTS = [(1, 256, 1024), (8, 4, 1024),
         (2, 1, 256, 8, 64), (2, 1, 256, 8, 64), (2, 8, 4, 8, 64), (2, 8, 4, 8, 64),
         (2, 1, 256, 8, 64), (2, 1, 256, 8, 64), (2, 8, 1024, 8, 64), (2, 8, 1024, 8, 64)]


def kernel(**inputs):
    import numpy as _np
    import concourse.bacc as _bacc
    from concourse import mybir as _mybir
    from concourse.bass_utils import run_bass_kernel_spmd as _run

    nc = _bacc.Bacc("TRN2", target_bir_lowering=False, num_devices=1)
    arrays, ins = {}, {}
    inputs = {n: _np.asarray(a) for n, a in inputs.items()}
    g = _np.concatenate([inputs["g_mix_a"], inputs["g_mix_b"]], 1).reshape(2, 8, 128)
    inputs["g_mix_cols"] = g.transpose(2, 0, 1)
    inputs["sb_bias_all"] = _np.broadcast_to(inputs["sb_bias"], (128, 2, 8))
    inputs["sb_bias_rows"] = _np.repeat(inputs["sb_bias"], 4, axis=1).T
    for name, a in list(inputs.items()) + list(position_tables().items()):
        a = _np.ascontiguousarray(a)
        arrays[f"in_{name}"] = a
        ins[name] = nc.dram_tensor(f"in_{name}", a.shape, _mybir.dt.from_np(a.dtype), kind="ExternalInput").ap()
    outs = [nc.dram_tensor(f"out_{i}", shape, _mybir.dt.float32, kind="ExternalOutput").ap()
            for i, shape in enumerate(_OUTS)]
    hybrid_decode_step(nc, ins, outs)
    r = _run(nc, [arrays], core_ids=[0])
    return tuple(r.results[0][f"out_{i}"] for i in range(len(_OUTS)))
```

```python
from contextlib import ExitStack

import numpy as np

import concourse.bass as bass
from concourse import mybir

F32 = mybir.dt.float32
I32 = mybir.dt.int32
ALU = mybir.AluOpType
ACT = mybir.ActivationFunctionType
AX = mybir.AxisListType.X

P = 128
D = 1024
KD = D // P
SEQ, NS, DEC = 256, 8, 4
LAYERS = 2
HEADS, HD = 8, 64
HP = HEADS // 2
WID = HEADS * HD
PAST, PAGE = 1024, 128
PAGES = PAST // PAGE
SAMPLE = NS * DEC
ROWS = (P, P, SAMPLE)
T = len(ROWS)
TOK = SEQ + SAMPLE
FF, FFE, EXPERTS = 2816, 3584, 8
CH = 512
FPC = CH // P
SLOT = KD * CH
NSLOT = 7
TOP_K = 2
ITEM = 128
PASSES = -(-TOK // ITEM)
ITEMS = TOP_K * TOK // ITEM + EXPERTS
SPARSE = 512
SWA_TILES = 5
SWA_KEYS = SWA_TILES * P
KTILES = PAGES + SWA_TILES
GSEQ = P // SAMPLE
GROUPS = NS // GSEQ
SCALE = HD ** -0.5
ALPHA = (2 * LAYERS) ** 0.25
LN_EPS, RMS_EPS = 1e-5, 1e-6
BIG = 1e34
NEG = -1e30
BRANCHES = ((128, 1), (512, 4), (2048, 16))


def position_tables():
    def ln_count(dist):
        n = sum((dist % d == 0) & (dist <= w) for w, d in BRANCHES)
        return np.where((dist >= 0) & (n > 0), np.log(np.maximum(n, 1)), NEG)

    q, k = np.arange(P)[:, None], np.arange(P)[None, :]
    dist = np.concatenate([q - k, q - k + P, q - k], 1)
    slopes = 2.0 ** (-8.0 * np.arange(1, HEADS + 1) / HEADS)
    col = np.arange(SWA_KEYS)
    dense = SPARSE + (SWA_TILES - 1) * (col % P) + col // P
    s = col - (PAST - SPARSE)
    row = np.where(s < 0, dense, 16 * (s % 32) + s // 32)
    far = PAST + np.arange(DEC)[:, None] - row[None, :]
    past = -slopes[:, None, None] * far[None] + ln_count(far)[None]
    i, seq, owner, j = (a.reshape(s) for a, s in ((np.arange(DEC), (DEC, 1, 1, 1)), (np.arange(NS), (1, NS, 1, 1)),
                                                 (np.arange(NS), (1, 1, NS, 1)), (np.arange(DEC), (1, 1, 1, DEC))))
    own = np.where(seq == owner, ln_count(i - j), NEG)
    new_a = -slopes[:, None, None, None, None] * (i - j)[None] + own[None]
    new_b = np.broadcast_to(np.where((seq == owner) & (j < i), 0.0, NEG), new_a.shape)

    def by_group(a):
        a = a.transpose(2, 0, 1, 3, 4).reshape(GROUPS, P, SAMPLE)
        return a.transpose(1, 0, 2)

    tok = np.arange(P)[:, None, None] + P * np.arange(T)[None, :, None]
    one = np.ones((1, 1, EXPERTS))
    tabs = {
        "distance": dist, "ln_branches": ln_count(dist), "strict_mask": np.where(dist > 0, 0.0, NEG),
        "past_bias": np.tile(past.reshape(HEADS * DEC, SWA_KEYS), (P // (HEADS * DEC), 1)),
        "new_bias": np.stack([by_group(new_a), by_group(new_b)], 1),
        "identity": np.eye(P), "earlier": np.triu(np.ones((P, P)), 1), "ones": np.ones((P, P)),
        "slot_number": np.broadcast_to(1.0 + np.arange(ITEM), (P, ITEM)),
        "descending": np.broadcast_to(np.arange(EXPERTS, 0, -1), (P, T, EXPERTS)),
        "is_token": (tok < TOK) * one,
        "item_number": np.broadcast_to(np.arange(ITEMS + 1)[None, :, None], (P, ITEMS + 1, EXPERTS)),
        "expert_number": np.broadcast_to(np.arange(EXPERTS)[None, None, :], (P, ITEMS + 1, EXPERTS)),
    }
    return {n: np.ascontiguousarray(a, np.float32) for n, a in tabs.items()}


class Steps:

    def __init__(self, eng, sem):
        self.eng, self.sem, self.n, self.base = eng, sem, 0, None

    def value(self):
        return self.n if self.base is None else self.base + self.n

    def go(self, ins):
        self.n += 1
        ins.then_inc(self.sem, 1)

    def did(self, ins):
        self.go(ins)
        self.eng.wait_ge(self.sem, self.value())


PROJ_SLOTS = ((2, 3, 4, 5, 6, 0), (6, 1, 0, 2, 3, 4))
WO_SLOTS = ((1, 0), (1, 0))
CYCLE = ((2, 3, 4, 5, 6, 1, 0), (2, 3, 4, 5, 6, 1, 0))
DENSE_CHUNKS = [(c, min(FPC, FF // P - FPC * c)) for c in range(-(-FF // CH))]
DENSE_F = FF // P
MOE_CHUNKS = FFE // CH
MOE_F = FFE // P
UNITS_Q, UNITS_KV = FPC, T
PROJ_UNITS = 2 * UNITS_Q + 4 * UNITS_KV


def attention_order():
    heads = {s: [2 * s, 2 * s + 1] for s in range(GSEQ)}
    heads.update({5: [8, 9, 10], 6: [11, 12, 13], 7: [14, 15]})
    steps = []
    for s in range(NS):
        if s == 6:
            steps += [("turn", 0), ("value", 0)]
        if s == 7:
            steps += [("value", 1)]
        mine = heads.get(s, [])
        gap = {2: 6, 3: 4}.get(len(mine))
        for j in range(KTILES):
            if mine and j % gap == 0 and 0 < j // gap <= len(mine):
                steps.append(("probs", mine[j // gap - 1]))
            steps.append(("key", s, j))
            if mine and j % gap == 0 and j // gap < len(mine):
                steps.append(("score", mine[j // gap]))
        if s % GSEQ == GSEQ - 1:
            steps.append(("weigh", s // GSEQ))
    steps += [("value", 2), ("value", 3), ("turn", 1)] + [("value", s) for s in range(4, NS)]
    return steps


ORDER = attention_order()
HEAD_ORDER = [(1, h) for h in range(HEADS)] + [(0, h) for h in range(HEADS)]
UNITS_OF = {"key": 1, "probs": 1, "turn": 4}
UNIT_AT, ATT_UNITS = {}, 0
for _step in ORDER:
    UNIT_AT[_step] = ATT_UNITS
    ATT_UNITS += UNITS_OF.get(_step[0], 0)
ITEM_LOADS = 3 * MOE_CHUNKS


def hybrid_decode_step(nc, ins, outs):
    y_p, y_s, sbk_p, sbv_p, sbk_s, sbv_s, swk_p, swv_p, swk_s, swv_s = outs
    ctx = ExitStack()
    with ctx:
        def sb(name, shape, dt=F32):
            return ctx.enter_context(nc.sbuf_tensor(name, shape, dt))

        def sem(name):
            return ctx.enter_context(nc.semaphore(name))

        ring = sb("ring", [P, NSLOT * SLOT])
        xT = sb("xT", [P, KD * TOK])
        x_tok = sb("x_tok", [P, T, D])
        kv_or_h = sb("kv_or_h", [P, DENSE_F * TOK])
        q_or_o = sb("q_or_o", [P, KD * TOK])
        k_or_ln = sb("k_or_ln", [P, KD * TOK])
        o_or_acc = sb("o_or_acc", [P, T, D])
        prompt_tab = sb("prompt_tab", [P, 3, 3 * P])
        past_bias = sb("past_bias", [P, SWA_KEYS])
        new_bias = sb("new_bias", [P, 2, GROUPS, SAMPLE])
        ident = sb("ident", [P, P])
        sb_probT = sb("sb_probT", [P, PAGES + 1, P])
        swa_probT = sb("swa_probT", [P, SWA_TILES + 1, P])
        oS = sb("oS", [P, KD, SAMPLE])
        g_mix = sb("g_mix", [P, LAYERS, KD])
        sb_bias = sb("sb_bias", [P, LAYERS, HEADS])
        sb_bias_rows = sb("sb_bias_rows", [P, LAYERS])
        stat = sb("stat", [P, 8])
        norm = sb("norm", [P, T, 24])
        dstat = sb("dstat", [P, 4])
        pages = sb("pages", [1, NS * PAGES], I32)
        plan = sb("plan", [1, ITEMS + 2], I32)
        psum = ctx.enter_context(nc.psum_tensor("psum", [P, 8 * CH], F32))

        def bank(b, n=1):
            return psum[:, b * CH:(b + n) * CH]

        xTv = xT[:, :].rearrange("p (k t) -> p k t", k=KD)
        kv = kv_or_h[:, 0:T * 4 * WID].rearrange("p (t g f) -> p t g f", t=T, g=4)
        hT = kv_or_h[:, :].rearrange("p (f t) -> p f t", f=DENSE_F)
        hE = kv_or_h[:, 0:MOE_F * ITEM].rearrange("p (f t) -> p f t", f=MOE_F)
        qT = q_or_o[:, :].rearrange("p (k t) -> p k t", k=KD)
        kT = k_or_ln[:, :].rearrange("p (k t) -> p k t", k=KD)
        ln_gb = k_or_ln[:, 0:2 * D].rearrange("p (a d) -> p a d", a=2)
        probs = xT[:, 0:PAST + SAMPLE]
        keeps = xT[:, PAST + SAMPLE:2 * (PAST + SAMPLE) + 1]
        att, att_at = ring[:, 2 * SLOT:7 * SLOT], [0]

        def take_att(*shape):
            n = int(np.prod(shape))
            v = att[:, att_at[0]:att_at[0] + n]
            att_at[0] += n
            assert att_at[0] <= 5 * SLOT
            return v.rearrange("p (a b) -> p a b", b=shape[-1]) if len(shape) > 1 else v

        k_half = [take_att(PAGES // 2, WID) for _ in range(3)]
        v_sb = take_att(PAGES, WID)
        k_swa, v_swa = take_att(SWA_TILES, WID), take_att(SWA_TILES, WID)
        kstage = take_att(4, WID)
        swa_s = take_att(SWA_KEYS + SAMPLE)
        head_e, head_keep = take_att(3 * P), take_att(3 * P + 2)
        head_pT = take_att(3 * P)
        qblk = [take_att(2, HP * SAMPLE) for _ in range(2)]
        silu_r = [q_or_o[:, a * CH:(a + 1) * CH] for a in (0, 2)]
        silu_t = [q_or_o[:, a * CH:(a + 1) * CH] for a in (1, 3)]
        beside_h = kv_or_h[:, MOE_F * ITEM:]
        pick = beside_h[:, 0:T * ITEM].rearrange("p (t s) -> p t s", t=T)
        pickT = beside_h[:, T * ITEM:T * ITEM + TOK]
        xg = xT[:, 0:KD * ITEM].rearrange("p (k s) -> p k s", k=KD)
        y_item = xT[:, KD * ITEM:KD * ITEM + D]
        ptab = prompt_tab[:, :, :].rearrange("p a b -> p (a b)")
        earlier, ones, slot_number = ptab[:, 0:P], ptab[:, P:2 * P], ptab[:, 2 * P:3 * P]
        w_router = ptab[:, 3 * P:3 * P + KD * EXPERTS].rearrange("p (k e) -> p k e", k=KD)
        NI = ITEMS + 1

        def rows_of(where, at, n, m):
            return where[:, at:at + n * m].rearrange("p (t e) -> p t e", t=n)
        descending, is_token = rows_of(ptab, 448, T, 8), rows_of(ptab, 472, T, 8)
        item_number, expert_number = rows_of(ptab, 496, NI, 8), rows_of(ptab, 600, NI, 8)
        rank_of, gate_of = rows_of(ptab, 704, T, NI), rows_of(ptab, 744, T, NI)
        chosen, gates, ranks = (rows_of(ptab, 784 + 24 * a, T, 8) for a in range(3))
        vals = rows_of(ptab, 856, T, 8)
        logit, tie, hot1, hot2 = (rows_of(q_or_o, 24 * a, T, 8) for a in range(4))
        of_item, first_rank, wide = (rows_of(q_or_o, 104 + 104 * a, NI, 8) for a in range(3))
        per_expert = rows_of(q_or_o, 420, 4, 8)
        plan_f = q_or_o[:, 460:460 + NI + 1]
        mean_sq_out = xT[:, 0:WID]

        w_loaded = [sem(f"w_loaded{s}") for s in range(NSLOT)]
        tables_in, ident_in, x_in, router_in = sem("tables_in"), sem("ident_in"), sem("x_in"), sem("router_in")
        ln_in = sem("ln_in")
        tp_full, tp_free = sem("transposes_done"), sem("transposes_copied")
        proj_done, proj_free = sem("projections_done"), sem("projections_copied")
        scored, masked, expd, prob_ready = sem("scored"), sem("masked"), sem("exponentials"), sem("probs_ready")
        pv_done, o_copied = sem("pv_done"), sem("o_copied")
        khalf_in = [sem(f"khalf_in{a}") for a in range(3)]
        vsb_in, kswa_in, vswa_in = sem("vsb_in"), sem("kswa_in"), sem("vswa_in")
        qblk_ready = sem("qblk_ready")
        d_scored, sb_exped, swa_taken = sem("dec_scored"), sem("sb_exponentials"), sem("swa_scores_taken")
        sb_new_masked, swa_exped = sem("sb_new_masked"), sem("swa_exponentials")
        sb_weights, swa_weights = sem("sb_weights"), sem("swa_weights")
        d_o, d_ocopied = sem("dec_o_done"), sem("dec_o_copied")
        sq_done, rms_root, rms_scaled = sem("squares_summed"), sem("rms_root"), sem("rms_scaled")
        wo_done, wo_added = sem("wo_done"), sem("wo_added")
        var_ready, ln_root, ln_done = sem("var_ready"), sem("ln_root"), sem("ln_done")
        gu_done, gu_exp, gu_free = sem("gate_up_done"), sem("gate_exp"), sem("gate_up_used")
        down_done, ffn_added = sem("down_done"), sem("ffn_added")
        stored_kv, stored_win, stored_y, shifted = sem("stored_kv"), sem("stored_window"), sem("stored_y"), sem("shifted")
        kT_read = sem("kT_read")
        logits_done, logits_copied, chosen_ready = sem("logits_done"), sem("logits_copied"), sem("chosen_ready")
        gate_exp2, ranks_done, plan_ready, acc_zero = sem("gate_exp2"), sem("ranks_done"), sem("plan_ready"), sem("acc_zero")
        pick_ready, gathered, gather_copied = sem("pick_ready"), sem("gathered"), sem("gather_copied")
        pick_turned, pickT_copied = sem("pick_turned"), sem("pickT_copied")
        e_gu, e_exp, e_h, e_down = sem("expert_gate_up"), sem("expert_exp"), sem("expert_h"), sem("expert_down")
        y_copied, combined, added = sem("y_copied"), sem("combined"), sem("combined_added")
        act_step, dve_step, dve_tail = sem("act_step"), sem("dve_step"), sem("dve_tail")

        KHALF_USES = [len(range(a, 2 * NS, 3)) for a in range(3)]
        DENSE_GU = 2 * DENSE_F
        tp_at = {}
        u = 0
        for L in range(LAYERS):
            for name, n in ((("x", 6),) if L == 0 else ()) + (("k", 6), ("att", ATT_UNITS), ("sample", 2),
                                                              ("merge", 6), ("mix", 6)) + ((("ffn", 6),) if L == 0 else ()):
                tp_at[L, name] = u
                u += n
        loads = [0] * NSLOT

        def slot_view(s, k=KD):
            return ring[:, s * SLOT:(s + 1) * SLOT].rearrange("p (k f) -> p k f", k=k)

        stream = []
        used = [None] * NSLOT

        def chunk(key, slot, src, shape_k, freed):
            loads[slot] += 1
            stream.append((key, slot, src, shape_k, used[slot], loads[slot]))
            used[slot] = freed

        for L in range(LAYERS):
            w_in = ins["w_in"][L].rearrange("(k p) f -> p k f", p=P)
            at = 0
            for c in range(6):
                at += UNITS_Q if c % 3 == 0 else UNITS_KV
                chunk((L, "proj", c), PROJ_SLOTS[L][c], w_in[:, :, c * CH:(c + 1) * CH], KD, (proj_done, PROJ_UNITS * L + at))
            w_o = ins["w_o"][L].rearrange("(k p) f -> p k f", p=P)
            for c in range(2):
                chunk((L, "wo", c), WO_SLOTS[L][c], w_o[:, :, c * CH:(c + 1) * CH], KD, (wo_done, 6 * L + 3 * (c + 1)))
            if L == 0:
                n = 0
                wg, wu = (ins[w][0].rearrange("(k p) f -> p k f", p=P) for w in ("w_gate", "w_up"))
                for c, m in DENSE_CHUNKS:
                    for b, w in enumerate((wg, wu)):
                        chunk((L, "gu"[b], c), CYCLE[L][n % NSLOT], w[:, :, c * CH:c * CH + m * P], KD,
                              (gu_done, 2 * (FPC * c + m) - 1 + b))
                        n += 1
                wd = ins["w_down"][0].rearrange("(f p) d -> p f d", p=P)
                for c, m in DENSE_CHUNKS:
                    chunk((L, "d", c), CYCLE[L][n % NSLOT], wd[:, FPC * c:FPC * c + m, :], FPC, (down_done, c + 1))
                    n += 1
        loaded_at = {key: (slot, 16 * n) for key, slot, _, _, _, n in stream}
        moe_base, moe_used = list(loads), list(used)
        we = [ins[w].rearrange("o e (k p) f -> (o e) p k f", p=P) for w in ("we_gate", "we_up")]
        wed = ins["we_down"].rearrange("o e (f p) d -> (o e) p f d", p=P)
        item_loads = [("gu"[n % 2], n // 2) if n < 2 * MOE_CHUNKS else ("d", n - 2 * MOE_CHUNKS) for n in range(ITEM_LOADS)]

        def item_slot(n):
            return CYCLE[1][n % NSLOT]

        def item_loaded(eng, n, i):
            s = item_slot(n)
            eng.wait_ge(w_loaded[s], 16 * 3 * i + 16 * (moe_base[s] + n // NSLOT + 1))

        def arrived(eng, key):
            s, v = loaded_at[key]
            eng.wait_ge(w_loaded[s], v)
            return slot_view(s, FPC if key[1] == "d" else KD)

        def out_rows(L, pair):
            return pair

        block = ctx.enter_context(nc.Block())

        @block.sync
        def _(sp):
            def tab(dst, name):
                sp.dma_start(dst, ins[name]).then_inc(tables_in, 16)

            for t in range(2):
                sp.dma_start(x_tok[:, t, :], ins["x_prompt"][0, t * P:(t + 1) * P, :]).then_inc(x_in, 16)
            sp.dma_start(x_tok[0:SAMPLE, 2, :], ins["x_sample"].rearrange("b t d -> (b t) d")).then_inc(x_in, 16)
            sp.dma_start(ident[:, :], ins["identity"]).then_inc(ident_in, 16)

            def load(n):
                key, slot, src, k, freed, _ = stream[n]
                if freed:
                    sp.wait_ge(*freed)
                w = src.shape[-1] if k == KD else None
                dst = slot_view(slot, k)
                dst = dst[:, :, 0:w] if k == KD else dst[:, 0:src.shape[1], :]
                sp.dma_start(dst, src).then_inc(w_loaded[slot], 16)

            names = {key: n for n, (key, *_) in enumerate(stream)}
            for n in range(6):
                load(n)
            for a, name in enumerate(("distance", "ln_branches", "strict_mask")):
                tab(prompt_tab[:, a, :], name)
            tab(past_bias[:, :], "past_bias")
            tab(new_bias[:, :, :, :], "new_bias")
            tab(g_mix[:, :, :], "g_mix_cols")
            tab(sb_bias[:, :, :], "sb_bias_all")
            tab(sb_bias_rows[:, :], "sb_bias_rows")
            sp.dma_start(pages[:, :], ins["page_table"].rearrange("(o a) b -> o (a b)", o=1)).then_inc(tables_in, 16)

            for L in range(LAYERS):
                if L == 1:
                    for c in range(6):
                        load(names[L, "proj", c])
                for c in range(2):
                    load(names[L, "wo", c])
                caches = {n: ins[n][L].rearrange("b n h d -> b n (h d)")
                          for n in ("cache_sb_k", "cache_sb_v", "cache_swa_k", "cache_swa_v")}

                def load_pages(dst, name, loaded, first_page):
                    n = dst.shape[1]
                    numbers = [sp.value_load(pages[0:1, first_page + j:first_page + j + 1],
                                             min_val=0, max_val=ins[name].shape[1] - 1) for j in range(n)]
                    for j, page in enumerate(numbers):
                        sp.dma_start(dst[:, j, :], caches[name][bass.ds(page, 1), :, :].rearrange("o p f -> (o p) f"))\
                          .then_inc(loaded, 16)

                def load_window(dst, name, loaded, s):
                    seq = caches[name][s]
                    near = seq[SPARSE:PAST, :].rearrange("(p c) f -> p c f", c=SWA_TILES - 1)
                    sp.dma_start(dst[:, 0:SWA_TILES - 1, :], near).then_inc(loaded, 16)
                    far = seq[0:SPARSE, :].rearrange("(a b) f -> a b f", b=16)
                    for b in range(DEC):
                        sp.dma_start(dst[32 * b:32 * b + 32, SWA_TILES - 1, :], far[:, b, :]).then_inc(loaded, 16)

                def unit_done(step):
                    return tp_at[L, "att"] + UNIT_AT[step] + 1

                def load_keys(s):
                    for half in range(2):
                        n = 2 * s + half
                        if n >= 3:
                            sp.wait_ge(tp_full, unit_done(("key", (n - 3) // 2, 4 * ((n - 3) % 2) + 3)))
                        load_pages(k_half[n % 3], "cache_sb_k", khalf_in[n % 3], PAGES * s + 4 * half)
                    if s:
                        sp.wait_ge(tp_full, unit_done(("key", s - 1, KTILES - 1)))
                    load_window(k_swa, "cache_swa_k", kswa_in, s)

                def load_values(s):
                    if s:
                        sp.wait_ge(d_o, 2 * (NS * L + s) - 1)
                    load_pages(v_sb, "cache_sb_v", vsb_in, PAGES * s)
                    if s:
                        sp.wait_ge(d_o, 2 * (NS * L + s))
                    load_window(v_swa, "cache_swa_v", vswa_in, s)

                sp.wait_ge(tables_in, 16 * 9)
                sp.wait_ge(proj_done, PROJ_UNITS * (L + 1))
                for s in (0, 1):
                    load_keys(s)
                load_values(0)
                for s in (2, 3, 4, 5, 6):
                    load_keys(s)
                load_values(1)
                load_keys(7)
                for s in range(2, NS):
                    load_values(s)
                sp.wait_ge(d_o, 2 * NS * (L + 1))
                sp.wait_ge(tp_full, tp_at[L, "sample"])
                for a, name in enumerate(("ln_mix_g", "ln_mix_b")):
                    sp.dma_start(ln_gb[:, a, :], ins[name][L].partition_broadcast(P)).then_inc(ln_in, 16)
                if L == 0:
                    first = names[L, "g", 0]
                    for n in range(first, names[L, "d", 0]):
                        load(n)
                    sp.wait_ge(ln_done, 2 * T * L + T)
                    for a, name in enumerate(("ln_ffn_g", "ln_ffn_b")):
                        sp.dma_start(ln_gb[:, a, :], ins[name][L].partition_broadcast(P)).then_inc(ln_in, 16)
                    for n in range(names[L, "d", 0], names[L, "d", 0] + len(DENSE_CHUNKS)):
                        load(n)

            def item_load(n, e, i):
                what, c = item_loads[n]
                s = item_slot(n)
                if n < NSLOT:
                    if i is None:
                        sp.wait_ge(*moe_used[s])
                    else:
                        sp.wait_ge(e_down, MOE_CHUNKS * i + (n + 1 - MOE_CHUNKS))
                elif n - NSLOT < 2 * MOE_CHUNKS:
                    v = n - NSLOT + 1
                    sp.wait_ge(e_gu, v if i is None else 2 * MOE_CHUNKS * i + v)
                if what == "d":
                    src, dst = wed[bass.ds(e, 1), :, FPC * c:FPC * (c + 1), :], slot_view(s, FPC)
                else:
                    src, dst = we["gu".index(what)][bass.ds(e, 1), :, :, c * CH:(c + 1) * CH], slot_view(s)
                sp.dma_start(dst, src.rearrange("o p k f -> (o p) k f")).then_inc(w_loaded[s], 16)

            sp.wait_ge(masked, 2 * HEADS * LAYERS)
            for dst, name in ((earlier, "earlier"), (ones, "ones"), (slot_number, "slot_number"),
                              (descending, "descending"), (is_token, "is_token"),
                              (item_number, "item_number"), (expert_number, "expert_number")):
                sp.dma_start(dst, ins[name]).then_inc(router_in, 16)
            sp.dma_start(w_router, ins["w_router"][0].rearrange("(k p) e -> p k e", p=P)).then_inc(router_in, 16)
            def item_expert(i):
                return sp.value_load(plan[0:1, bass.ds(i + 1, 1)], min_val=0, max_val=EXPERTS - 1)

            sp.wait_ge(plan_ready, 1)
            count = sp.value_load(plan[0:1, 0:1], min_val=0, max_val=ITEMS)
            first_expert = sp.value_load(plan[0:1, 1:2], min_val=0, max_val=EXPERTS - 1)
            for n in range(ITEM_LOADS):
                item_load(n, first_expert, None)
                if n == NSLOT - 1:
                    sp.wait_ge(ln_done, 2 * T + T)
                    for a, name in enumerate(("ln_ffn_g", "ln_ffn_b")):
                        sp.dma_start(ln_gb[:, a, :], ins[name][1].partition_broadcast(P)).then_inc(ln_in, 16)
            with sp.Fori(1, ITEMS) as i:
                with sp.If(i < count):
                    e = item_expert(i)
                    for n in range(ITEM_LOADS):
                        item_load(n, e, i)
            for t, dst in enumerate((y_p[0, 0:P, :], y_p[0, P:SEQ, :], y_s.rearrange("b t d -> (b t) d"))):
                sp.wait_ge(ln_done, 2 * T * LAYERS - T + t + 1)
                sp.dma_start(dst, x_tok[0:ROWS[t], t, :]).then_inc(stored_y, 16)
            sp.wait_ge(stored_y, 16 * T)

        @block.gpsimd
        def _(pool):
            def shift(L, half):
                for src, dst in ((ins["cache_swa_k"], swk_s), (ins["cache_swa_v"], swv_s)):
                    s = src[L].rearrange("b n h d -> b (n h d)")
                    d = dst[L].rearrange("b n h d -> b (n h d)")
                    for b in range(4 * half, 4 * half + 4):
                        n = (PAST - DEC) * WID
                        pool.dma_start(d[b, 0:n].rearrange("(a c) -> a c", a=240),
                                       s[b, DEC * WID:PAST * WID].rearrange("(a c) -> a c", a=240)).then_inc(shifted, 16)

            for L in range(LAYERS):
                pool.wait_ge(proj_free, PROJ_UNITS * (L + 1))
                for g, (prompt, sample) in enumerate(((swk_p, None), (swv_p, None), (sbk_p, sbk_s), (sbv_p, sbv_s))):
                    for t in range(2):
                        pool.dma_start(prompt[L, 0, t * P:(t + 1) * P].rearrange("t h d -> t (h d)"), kv[:, t, g, :])\
                            .then_inc(stored_kv, 16)
                    if sample is not None:
                        pool.dma_start(sample[L].rearrange("b t h d -> (b t) (h d)"), kv[0:SAMPLE, 2, g, :])\
                            .then_inc(stored_kv, 16)
                for g, dst in enumerate((swk_s, swv_s)):
                    for b in range(NS):
                        pool.dma_start(dst[L, b, PAST - DEC:PAST].rearrange("t h d -> t (h d)"),
                                       kv[DEC * b:DEC * b + DEC, 2, g, :]).then_inc(stored_win, 16)
                if L == 0:
                    pool.wait_ge(wo_done, 1)
                    for M in range(LAYERS):
                        for half in range(2):
                            pool.wait_ge(gu_done, 8 * (2 * M + half) + 1)
                            shift(M, half)
            pool.wait_ge(stored_kv, 16 * LAYERS * 10)
            pool.wait_ge(stored_win, 16 * LAYERS * 2 * NS)
            pool.wait_ge(shifted, 16 * LAYERS * 2 * NS)

        @block.tensor
        def _(pe):
            def transpose_unit(u, parts, dst):
                if u >= 2:
                    pe.wait_ge(tp_free, u - 1)
                for o, src in zip(dst(bank(u % 2)), parts):
                    last = pe.transpose(o, src, ident[0:src.shape[0], 0:src.shape[0]])
                last.then_inc(tp_full, 1)

            def token_to_feature(u, src):
                for t, ready in enumerate(src):
                    ready(t)
                    r = ROWS[t]
                    for g in range(2):
                        transpose_unit(u + 2 * t + g, [src_tok[0:r, t, (4 * g + j) * P:(4 * g + j + 1) * P] for j in range(4)],
                                       lambda b: [b[:, j * r:(j + 1) * r] for j in range(4)])

            pe.wait_ge(ident_in, 16)
            pe.wait_ge(x_in, 48)
            src_tok = x_tok
            token_to_feature(0, [lambda t: None] * T)
            for L in range(LAYERS):
                pe.wait_ge(tp_free, tp_at[L, "k"])
                unit = PROJ_UNITS * L
                for c in range(6):
                    w = arrived(pe, (L, "proj", c))
                    for n in range(UNITS_Q if c % 3 == 0 else UNITS_KV):
                        if L == 1 and unit - PROJ_UNITS * L < 6:
                            pe.wait_ge(ffn_added, 6)
                        if unit >= 6:
                            pe.wait_ge(proj_free, unit - 5)
                        b = bank(2 + unit % 6)
                        for k in range(KD):
                            if c % 3 == 0:
                                last = pe.matmul(b[:, 0:TOK], w[:, k, n * P:(n + 1) * P], xTv[:, k, :],
                                                 start=k == 0, stop=k == KD - 1)
                            else:
                                last = pe.matmul(b[0:ROWS[n], :], xTv[:, k, n * P:n * P + ROWS[n]], w[:, k, :],
                                                 start=k == 0, stop=k == KD - 1)
                        last.then_inc(proj_done, 1)
                        unit += 1
                pe.wait_ge(proj_free, PROJ_UNITS * (L + 1))
                for m in range(2):
                    for t in range(T):
                        r = ROWS[t]
                        transpose_unit(tp_at[L, "k"] + T * m + t, [kv[0:r, t, 2 * m, j * P:(j + 1) * P] for j in range(4)],
                                       lambda b: [b[:, j * r:(j + 1) * r] for j in range(4)])
                pe.wait_ge(tp_free, tp_at[L, "att"])
                n0, B, units = 2 * HEADS * L, NS * L, tp_at[L, "att"]

                seen = {"value": 0}

                def bank6_free(scores, outputs):
                    if n0 + scores:
                        pe.wait_ge(masked, n0 + scores)
                    if n0 + outputs:
                        pe.wait_ge(o_copied, n0 + outputs)
                    if B + seen["value"]:
                        pe.wait_ge(d_ocopied, 2 * (B + seen["value"]))

                def head_scores(n):
                    m, h = HEAD_ORDER[n]
                    rows = slice(HD * (h % 2), HD * (h % 2) + HD)
                    k = HP * m + h // 2
                    bank6_free(n, n)
                    b = bank(6)
                    pe.matmul(b[:, 0:P], qT[rows, k, 0:P], kT[rows, k, 0:P], start=True, stop=True)
                    pe.matmul(b[:, P:3 * P], qT[rows, k, P:SEQ], kT[rows, k, 0:SEQ], start=True, stop=True)\
                        .then_inc(scored, 1)

                def head_values(n):
                    m, h = HEAD_ORDER[n]
                    u = units + UNIT_AT["probs", n]
                    pe.wait_ge(prob_ready, n0 + n + 1)
                    transpose_unit(u, [head_e[:, j * P:(j + 1) * P] for j in range(3)],
                                   lambda b: [b[:, j * P:(j + 1) * P] for j in range(3)])
                    pe.wait_ge(tp_free, u + 1)
                    bank6_free(n + 1, n)
                    o = bank(6)[:, 384:512]
                    v = [kv[:, t, 2 * m + 1, h * HD:(h + 1) * HD] for t in range(2)]
                    pe.matmul(o[:, 0:HD], head_pT[:, 0:P], v[0], start=True, stop=True)
                    pe.matmul(o[:, HD:2 * HD], head_pT[:, P:2 * P], v[0], start=True, stop=False)
                    pe.matmul(o[:, HD:2 * HD], head_pT[:, 2 * P:3 * P], v[1], start=False, stop=True).then_inc(pv_done, 1)

                def keys_scored(s, j):
                    pe.wait_ge(tp_free, units + UNIT_AT["key", s, j] + 1)
                    m = 1 if j < PAGES else 0
                    at = 2 * CH + j * P if j < PAGES else 4 * CH + (j - PAGES) * P
                    rows = slice(SAMPLE * (s % GSEQ), SAMPLE * (s % GSEQ) + SAMPLE)
                    stage = kstage[:, (KTILES * s + j) % 4, :]
                    for a in range(HP):
                        last = pe.matmul(psum[rows, at:at + P], qblk[s % 2][:, m, a * SAMPLE:(a + 1) * SAMPLE],
                                         stage[:, a * P:(a + 1) * P], start=a == 0, stop=a == HP - 1)
                    last.then_inc(d_scored, 1)

                def new_keys_scored(s):
                    rows = slice(SAMPLE * (s % GSEQ), SAMPLE * (s % GSEQ) + SAMPLE)
                    for m in (1, 0):
                        at = 5 * CH + P + SAMPLE * m
                        for a in range(HP):
                            last = pe.matmul(psum[rows, at:at + SAMPLE], qblk[s % 2][:, m, a * SAMPLE:(a + 1) * SAMPLE],
                                             kT[:, HP * m + a, SEQ:TOK], start=a == 0, stop=a == HP - 1)
                    last.then_inc(d_scored, 1)

                def key_tile(s, j):
                    g = s // GSEQ
                    if j == 0:
                        pe.wait_ge(qblk_ready, B + s + 1)
                    if j in (0, PAGES // 2):
                        n = 2 * s + j // 4
                        pe.wait_ge(khalf_in[n % 3], 64 * (KHALF_USES[n % 3] * L + n // 3 + 1))
                    if j == PAGES:
                        pe.wait_ge(kswa_in, 16 * 5 * (B + s + 1))
                    src = k_half[(2 * s + j // 4) % 3][:, j % 4, :] if j < PAGES else k_swa[:, j - PAGES, :]
                    transpose_unit(units + UNIT_AT["key", s, j], [src[:, a * P:(a + 1) * P] for a in range(HP)],
                                   lambda b: [b[:, a * P:(a + 1) * P] for a in range(HP)])
                    if j == 1 and s % GSEQ == 0 and (g or L):
                        pe.wait_ge(sb_exped, 2 * (GROUPS * L + g))
                    if j == PAGES + 1 and s % GSEQ == 0 and (g or L):
                        pe.wait_ge(swa_taken, GROUPS * L + g)
                    if j:
                        keys_scored(s, j - 1)
                    if j == KTILES - 1:
                        keys_scored(s, j)
                        new_keys_scored(s)

                def turn(g):
                    u = units + UNIT_AT["turn", g]
                    pe.wait_ge(sb_weights, GROUPS * L + g + 1)
                    for a in range(2):
                        transpose_unit(u + a, [probs[:, (4 * a + j) * P:(4 * a + j + 1) * P] for j in range(4)],
                                       lambda b: [b[:, j * P:(j + 1) * P] for j in range(4)])
                    pe.wait_ge(swa_weights, GROUPS * L + g + 1)
                    transpose_unit(u + 2, [swa_s[:, j * P:(j + 1) * P] for j in range(4)],
                                   lambda b: [b[:, j * P:(j + 1) * P] for j in range(4)])
                    transpose_unit(u + 3, [swa_s[:, 4 * P:5 * P], swa_s[:, SWA_KEYS:SWA_KEYS + SAMPLE],
                                           probs[:, PAST:PAST + SAMPLE]],
                                   lambda b: [b[:, 0:P], b[0:SAMPLE, P:2 * P], b[0:SAMPLE, 2 * P:3 * P]])

                def value(s):
                    if s % GSEQ == 0:
                        pe.wait_ge(tp_free, units + UNIT_AT["turn", s // GSEQ] + 4)
                    cols = slice(SAMPLE * (s % GSEQ), SAMPLE * (s % GSEQ) + SAMPLE)
                    for m, count, v, pT, vnew, loaded in (
                            (1, PAGES, v_sb, sb_probT, kv[0:SAMPLE, 2, 3, :], (vsb_in, 16 * PAGES * (B + s + 1))),
                            (0, SWA_TILES, v_swa, swa_probT, kv[0:SAMPLE, 2, 1, :], (vswa_in, 16 * 5 * (B + s + 1)))):
                        pe.wait_ge(*loaded)
                        if m == 0:
                            done = sum(x[0] == "probs" for x in ORDER[:ORDER.index(("value", s))])
                            bank6_free(done, done)
                        elif B + s:
                            pe.wait_ge(d_ocopied, 2 * (B + s) - 1)
                        for a in range(HP):
                            o = bank(6 + m)[:, a * SAMPLE:(a + 1) * SAMPLE]
                            for j in range(count):
                                pe.matmul(o, v[:, j, a * P:(a + 1) * P], pT[:, j, cols], start=j == 0, stop=False)
                            last = pe.matmul(o, vnew[:, a * P:(a + 1) * P], pT[0:SAMPLE, count, cols], start=False, stop=True)
                        last.then_inc(d_o, 1)

                for step in ORDER:
                    if step[0] == "score":
                        head_scores(step[1])
                    elif step[0] == "probs":
                        head_values(step[1])
                    elif step[0] == "key":
                        key_tile(step[1], step[2])
                    elif step[0] == "turn":
                        turn(step[1])
                    elif step[0] == "value":
                        value(step[1])
                        seen["value"] += 1
                pe.wait_ge(d_ocopied, 2 * NS * (L + 1))

                for g in range(2):
                    transpose_unit(tp_at[L, "sample"] + g, [oS[:, 4 * g + j, :] for j in range(4)],
                                   lambda b: [b[0:SAMPLE, j * P:(j + 1) * P] for j in range(4)])
                src_tok = o_or_acc
                token_to_feature(tp_at[L, "merge"], [lambda t: pe.wait_ge(rms_scaled, T * L + t + 1)] * T)
                pe.wait_ge(tp_free, tp_at[L, "mix"])
                for c in range(2):
                    w = arrived(pe, (L, "wo", c))
                    for t in range(T):
                        b = bank(2 + T * c + t)
                        for k in range(KD):
                            last = pe.matmul(b[0:ROWS[t], :], qT[:, k, t * P:t * P + ROWS[t]], w[:, k, :],
                                             start=k == 0, stop=k == KD - 1)
                        last.then_inc(wo_done, 1)
                src_tok = x_tok
                token_to_feature(tp_at[L, "mix"], [lambda t: pe.wait_ge(ln_done, 2 * T * L + t + 1)] * T)
                pe.wait_ge(tp_free, tp_at[L, "mix"] + 6)
                pe.wait_ge(wo_added, 6 * (L + 1))
                if L == 0:
                    for c, m in DENSE_CHUNKS:
                        wg, wu = arrived(pe, (L, "g", c)), arrived(pe, (L, "u", c))
                        for j in range(m):
                            f = FPC * c + j
                            if f >= 2:
                                pe.wait_ge(gu_free, f - 1)
                            for a, w in enumerate((wg, wu)):
                                for k in range(KD):
                                    last = pe.matmul(bank(2 + 2 * (f % 2) + a)[:, 0:TOK], w[:, k, j * P:(j + 1) * P],
                                                     xTv[:, k, :], start=k == 0, stop=k == KD - 1)
                                last.then_inc(gu_done, 1)
                    pe.wait_ge(gu_free, DENSE_F)
                    for c, m in DENSE_CHUNKS:
                        w = arrived(pe, (L, "d", c))
                        for j in range(m):
                            f = FPC * c + j
                            for t in range(T):
                                for h in range(2):
                                    last = pe.matmul(bank(2 + 2 * t + h)[0:ROWS[t], :], hT[:, f, t * P:t * P + ROWS[t]],
                                                     w[:, j, h * CH:(h + 1) * CH], start=f == 0, stop=f == DENSE_F - 1)
                        last.then_inc(down_done, 1)
                    token_to_feature(tp_at[L, "ffn"], [lambda t: pe.wait_ge(ln_done, T + t + 1)] * T)

            pe.wait_ge(router_in, 16 * 8)
            for t in range(T):
                for k in range(KD):
                    last = pe.matmul(bank(2)[0:ROWS[t], t * EXPERTS:(t + 1) * EXPERTS], xTv[:, k, t * P:t * P + ROWS[t]],
                                     w_router[:, k, :], start=k == 0, stop=k == KD - 1)
            last.then_inc(logits_done, 1)
            pe.wait_ge(chosen_ready, 1)
            for t in range(T):
                for s in range(t + 1):
                    pe.matmul(bank(3)[:, t * EXPERTS:(t + 1) * EXPERTS], earlier if s == t else ones, chosen[:, s, :],
                              start=s == 0, stop=s == t)
            for s in range(T):
                last = pe.matmul(bank(3)[:, T * EXPERTS:(T + 1) * EXPERTS], ones, chosen[:, s, :],
                                 start=s == 0, stop=s == T - 1)
            last.then_inc(ranks_done, 1)
            pe.wait_ge(plan_ready, 1)

            def gather(value):
                pe.wait_ge(pick_ready, value)
                for g in range(2):
                    for j in range(4):
                        k = 4 * g + j
                        for t in range(T):
                            last = pe.matmul(bank(g)[:, j * ITEM:(j + 1) * ITEM],
                                             x_tok[0:ROWS[t], t, k * P:(k + 1) * P], pick[0:ROWS[t], t, :],
                                             start=t == 0, stop=t == T - 1)
                    last.then_inc(gathered, 1)

            def item(i):
                pe.wait_ge(gather_copied, 2 * i + 2)
                for c in range(MOE_CHUNKS):
                    b = 2 + 2 * (c % 2)
                    if c >= 2:
                        pe.wait_ge(e_h, MOE_CHUNKS * i + (c - 1))
                    for a in range(2):
                        item_loaded(pe, 2 * c + a, i)
                        w = slot_view(item_slot(2 * c + a))
                        for j in range(FPC):
                            for k in range(KD):
                                last = pe.matmul(bank(b + a)[:, j * ITEM:(j + 1) * ITEM],
                                                 w[:, k, j * P:(j + 1) * P], xg[:, k, :], start=k == 0, stop=k == KD - 1)
                        last.then_inc(e_gu, 1)
                pe.wait_ge(added, 6 * i + 6)
                for t in range(T):
                    last = pe.transpose(bank(0)[:, t * P:t * P + ROWS[t]], pick[0:ROWS[t], t, :],
                                        ident[0:ROWS[t], 0:ROWS[t]])
                last.then_inc(pick_turned, 1)
                pe.wait_ge(e_h, MOE_CHUNKS * i + (MOE_CHUNKS - 1))
                for c in range(MOE_CHUNKS):
                    if c == MOE_CHUNKS - 1:
                        pe.wait_ge(e_h, MOE_CHUNKS * i + MOE_CHUNKS)
                    item_loaded(pe, 2 * MOE_CHUNKS + c, i)
                    w = slot_view(item_slot(2 * MOE_CHUNKS + c), FPC)
                    for j in range(FPC):
                        f = FPC * c + j
                        for h in range(2):
                            last = pe.matmul(bank(6 + h), hE[:, f, :], w[:, j, h * CH:(h + 1) * CH],
                                             start=f == 0, stop=f == MOE_F - 1)
                    last.then_inc(e_down, 1)
                pe.wait_ge(pickT_copied, i + 1)
                gather(i + 2)
                for n in range(2 * T):
                    t, h = divmod(n, 2)
                    if n == 0:
                        pe.wait_ge(y_copied, i + 1)
                    elif n == 2:
                        pe.wait_ge(gather_copied, 2 * i + 4)
                    elif n >= 4:
                        pe.wait_ge(added, 6 * i + (n + 3))
                    pe.matmul(bank((6, 7, 0, 1)[n % 4])[0:ROWS[t], :], pickT[:, t * P:t * P + ROWS[t]],
                              y_item[:, h * CH:(h + 1) * CH], start=True, stop=True).then_inc(combined, 1)

            gather(1)
            count = pe.value_load(plan[0:1, 0:1], min_val=0, max_val=ITEMS)
            with pe.Fori(0, ITEMS) as i:
                with pe.If(i < count):
                    item(i)

        @block.scalar
        def _(act):
            st = Steps(act, act_step)

            def copy_unit(u, dst, src, scale=None):
                act.wait_ge(tp_full, u + 1)
                act.copy(dst, src(bank(u % 2))).then_inc(tp_free, 1)

            def to_feature(u, dst, gains=None):
                for t in range(T):
                    r = ROWS[t]
                    for g in range(2):
                        n = u + 2 * t + g
                        src = bank(n % 2)[:, 0:4 * r].rearrange("p (j r) -> p j r", j=4)
                        out = dst[:, 4 * g:4 * g + 4, t * P:t * P + r]
                        act.wait_ge(tp_full, n + 1)
                        if gains is None:
                            act.copy(out, src).then_inc(tp_free, 1)
                        else:
                            for j in range(4):
                                last = act.activation(out[:, j, :], src[:, j, :], ACT.Copy, scale=gains(4 * g + j))
                            last.then_inc(tp_free, 1)

            to_feature(0, xTv)
            for L in range(LAYERS):
                for m in range(2):
                    for t in range(T):
                        r = ROWS[t]
                        copy_unit(tp_at[L, "k"] + T * m + t, kT[:, HP * m:HP * m + HP, t * P:t * P + r],
                                  lambda b: b[:, 0:4 * r].rearrange("p (j r) -> p j r", j=4))
                n0, B, units = 2 * HEADS * L, NS * L, tp_at[L, "att"]
                if L == 0:
                    act.wait_ge(tables_in, 16 * 9)

                def head_exponentials(n):
                    m, h = HEAD_ORDER[n]
                    act.wait_ge(masked, n0 + n + 1)
                    if m == 0:
                        for q, cols in enumerate((slice(0, P), slice(P, 3 * P))):
                            last = act.activation(head_e[:, cols], head_e[:, cols], ACT.Exp, bias=stat[:, q:q + 1],
                                                  accum_out=stat[:, 2 + q:3 + q])
                    else:
                        last = act.activation(head_e, head_e, ACT.Exp, bias=sb_bias[:, L, h:h + 1])
                    last.then_inc(expd, 1)

                def weigh(g):
                    act.wait_ge(d_scored, (KTILES + 1) * (B + GSEQ * (g + 1)))
                    act.activation(probs[:, 0:PAST], bank(2, 2), ACT.Exp, bias=sb_bias_rows[:, L:L + 1], scale=SCALE)\
                        .then_inc(sb_exped, 1)
                    act.wait_ge(sb_new_masked, GROUPS * L + g + 1)
                    act.activation(probs[:, PAST:PAST + SAMPLE], probs[:, PAST:PAST + SAMPLE], ACT.Exp,
                                   bias=sb_bias_rows[:, L:L + 1]).then_inc(sb_exped, 1)
                    act.wait_ge(swa_taken, GROUPS * L + g + 1)
                    act.activation(swa_s, swa_s, ACT.Exp, bias=dstat[:, 0:1], accum_out=dstat[:, 1:2]).then_inc(swa_exped, 1)

                def take_values(s):
                    for a, m in enumerate((1, 0)):
                        act.wait_ge(d_o, 2 * (B + s) + a + 1)
                        for u in range(2):
                            at = (6 + m) * CH + 4 * u
                            src = psum[HD * u:HD * u + HD, at:at + 124].rearrange("p (a x) -> p a x", x=4)[:, ::10, :]
                            last = act.copy(oS[HD * u:HD * u + HD, HP * m:HP * m + HP, DEC * s:DEC * s + DEC], src)
                        last.then_inc(d_ocopied, 1)

                for step in ORDER:
                    u = units + UNIT_AT[step]
                    if step[0] == "score":
                        head_exponentials(step[1])
                    elif step[0] == "probs":
                        n = step[1]
                        if n0 + n:
                            act.wait_ge(pv_done, n0 + n)
                        copy_unit(u, head_pT, lambda b: b[:, 0:3 * P])
                    elif step[0] == "key":
                        t = KTILES * step[1] + step[2]
                        if t >= 4:
                            act.wait_ge(d_scored, (KTILES + 1) * B + t - 3 + (t - 4) // KTILES)
                        copy_unit(u, kstage[:, t % 4, :], lambda b: b)
                    elif step[0] == "weigh":
                        weigh(step[1])
                    elif step[0] == "turn":
                        if step[1] or L:
                            act.wait_ge(d_o, 2 * (B + GSEQ * step[1]))
                        for a, dst in enumerate((sb_probT[:, 0:4, :], sb_probT[:, 4:8, :], swa_probT[:, 0:4, :])):
                            copy_unit(u + a, dst, lambda b: b.rearrange("p (j q) -> p j q", j=4))
                        act.wait_ge(tp_full, u + 4)
                        b = bank((u + 3) % 2)
                        act.copy(swa_probT[:, 4, :], b[:, 0:P])
                        act.copy(swa_probT[0:SAMPLE, 5, :], b[0:SAMPLE, P:2 * P])
                        act.copy(sb_probT[0:SAMPLE, 8, :], b[0:SAMPLE, 2 * P:3 * P]).then_inc(tp_free, 1)
                    elif step[0] == "value":
                        take_values(step[1])
                for g in range(2):
                    copy_unit(tp_at[L, "sample"] + g, o_or_acc[0:SAMPLE, 2, 4 * g * P:4 * (g + 1) * P], lambda b: b[0:SAMPLE, :])
                for t in range(T):
                    r = ROWS[t]
                    if t == 0:
                        act.wait_ge(o_copied, n0 + 2 * HEADS)
                    if t == 2:
                        act.wait_ge(tp_free, tp_at[L, "merge"])
                    for m in range(2):
                        st.did(act.activation(mean_sq_out[0:r, :], o_or_acc[0:r, t, m * WID:(m + 1) * WID], ACT.Square,
                                              accum_out=norm[0:r, t, m:m + 1]))
                    act.wait_ge(sq_done, T * L + t + 1)
                    act.activation(norm[0:r, t, 4:6], norm[0:r, t, 2:4], ACT.Sqrt).then_inc(rms_root, 1)
                to_feature(tp_at[L, "merge"], qT, lambda k: g_mix[:, L, k:k + 1])

                def ln_roots(base):
                    for t in range(T):
                        act.wait_ge(var_ready, base + t + 1)
                        act.activation(norm[0:ROWS[t], t, 23:24], norm[0:ROWS[t], t, 22:23], ACT.Sqrt).then_inc(ln_root, 1)

                ln_roots(2 * T * L)
                to_feature(tp_at[L, "mix"], xTv)
                if L == 0:
                    for f in range(DENSE_F):
                        act.wait_ge(gu_done, 2 * f + 1)
                        if f >= 2:
                            act.wait_ge(gu_free, f - 1)
                        act.activation(silu_r[f % 2][:, 0:TOK], bank(2 + 2 * (f % 2))[:, 0:TOK], ACT.Exp, scale=-1.0)\
                            .then_inc(gu_exp, 1)
                    ln_roots(T)
                    to_feature(tp_at[L, "ffn"], xTv)
            act.wait_ge(logits_copied, 1)
            act.activation(vals[:, :, 3:4], vals[:, :, 2:3], ACT.Exp).then_inc(gate_exp2, 1)
            act.wait_ge(plan_ready, 1)

            def copy_gathered(i):
                for g in range(2):
                    act.wait_ge(gathered, 2 * i + (g + 1))
                    act.copy(xg[:, 4 * g:4 * g + 4, :], bank(g).rearrange("p (k s) -> p k s", k=4)).then_inc(gather_copied, 1)

            copy_gathered(0)
            count = act.value_load(plan[0:1, 0:1], min_val=0, max_val=ITEMS)
            with act.Fori(0, ITEMS) as i:
                with act.If(i < count):
                    for c in range(MOE_CHUNKS):
                        act.wait_ge(e_gu, 2 * MOE_CHUNKS * i + (2 * c + 1))
                        if c >= 2:
                            act.wait_ge(e_h, MOE_CHUNKS * i + (c - 1))
                        act.activation(silu_r[c % 2], bank(2 + 2 * (c % 2)), ACT.Exp, scale=-1.0).then_inc(e_exp, 1)
                    act.wait_ge(pick_turned, i + 1)
                    act.copy(pickT, bank(0)[:, 0:TOK]).then_inc(pickT_copied, 1)
                    act.wait_ge(e_down, MOE_CHUNKS * i + MOE_CHUNKS)
                    act.copy(y_item, psum[:, 6 * CH:8 * CH]).then_inc(y_copied, 1)
                    copy_gathered(i + 1)
            for t in range(T):
                act.wait_ge(var_ready, 3 * T + t + 1)
                act.activation(norm[0:ROWS[t], t, 23:24], norm[0:ROWS[t], t, 22:23], ACT.Sqrt).then_inc(ln_root, 1)

        @block.vector
        def _(v):
            st = Steps(v, dve_step)

            def layer_norm(t, base, gb_in, st):
                r = ROWS[t]
                x = x_tok[0:r, t, :]
                n = norm[0:r, t, :]
                for h in range(2):
                    st.did(v.bn_stats(n[:, 6 + 6 * h:12 + 6 * h], x[:, h * CH:(h + 1) * CH]))
                st.did(v.bn_aggr(n[:, 20:22], n[:, 6:18]))
                v.tensor_scalar(n[:, 22:23], n[:, 21:22], LN_EPS, None, ALU.add).then_inc(var_ready, 1)
                v.wait_ge(ln_root, base + t + 1)
                st.did(v.reciprocal(n[:, 19:20], n[:, 23:24]))
                st.did(v.tensor_scalar(x, x, n[:, 20:21], n[:, 19:20], ALU.subtract, ALU.mult))
                v.wait_ge(ln_in, gb_in)
                st.did(v.tensor_tensor(x, x, ln_gb[0:r, 0, :], ALU.mult))
                v.tensor_tensor(x, x, ln_gb[0:r, 1, :], ALU.add).then_inc(ln_done, 1)

            for L in range(LAYERS):
                unit = PROJ_UNITS * L
                for c in range(6):
                    for n in range(UNITS_Q if c % 3 == 0 else UNITS_KV):
                        b = bank(2 + unit % 6)
                        if c % 3 == 0:
                            v.wait_ge(proj_done, unit + 1)
                            v.tensor_copy(qT[:, HP * (c // 3) + n, :], b[:, 0:TOK]).then_inc(proj_free, 1)
                        else:
                            v.wait_ge(proj_done, unit + 1)
                            v.tensor_copy(kv[0:ROWS[n], n, 2 * (c // 3) + c % 3 - 1, :], b[0:ROWS[n], :]).then_inc(proj_free, 1)
                        unit += 1
                n0, B, W = 2 * HEADS * L, NS * L, GROUPS * L
                if L == 0:
                    v.wait_ge(tables_in, 16 * 9)
                v.wait_ge(proj_free, PROJ_UNITS * (L + 1))
                for q in qblk:
                    st.did(v.memset(q, 0.0))

                def queries(s):
                    if s >= 2:
                        v.wait_ge(d_scored, (KTILES + 1) * (B + s - 1))
                    for m in range(2):
                        for u in range(2):
                            rows = slice(HD * u, HD * u + HD)
                            dst = qblk[s % 2][rows, m, 4 * u:4 * u + 124].rearrange("p (a x) -> p a x", x=4)[:, ::10, :]
                            last = v.tensor_copy(dst, qT[rows, HP * m:HP * m + HP, SEQ + DEC * s:SEQ + DEC * (s + 1)])
                            if (m, u) == (1, 1):
                                last.then_inc(qblk_ready, 1)
                            else:
                                st.go(last)

                def mask(n):
                    m, h = HEAD_ORDER[n]
                    e, tmp = head_e, head_keep[:, 0:3 * P]
                    if n0 + n:
                        v.wait_ge(pv_done, n0 + n)
                    if m == 0:
                        st.did(v.scalar_tensor_tensor(tmp, prompt_tab[:, 0, :], -(2.0 ** (-8.0 * (h + 1) / HEADS)),
                                                      prompt_tab[:, 1, :], ALU.mult, ALU.add))
                    v.wait_ge(scored, n0 + n + 1)
                    score = v.scalar_tensor_tensor(e, bank(6)[:, 0:384], SCALE,
                                                   tmp if m == 0 else prompt_tab[:, 2, :], ALU.mult, ALU.add)
                    if m == 0:
                        st.did(score)
                        st.go(v.reduce_max(stat[:, 0:1], e[:, 0:P], AX, negate=True))
                        v.reduce_max(stat[:, 1:2], e[:, P:3 * P], AX, negate=True).then_inc(masked, 1)
                    else:
                        score.then_inc(masked, 1)

                def head_weights(n):
                    m, h = HEAD_ORDER[n]
                    e, keep = head_e, head_keep
                    v.wait_ge(expd, n0 + n + 1)
                    if m == 0:
                        v.reciprocal(stat[:, 4:6], stat[:, 2:4]).then_inc(prob_ready, 1)
                        return
                    halves = ((slice(0, P), slice(0, P), slice(1, P + 1)),
                              (slice(P, 3 * P), slice(P + 1, 3 * P + 1), slice(P + 2, 3 * P + 2)))
                    st.go(v.memset(keep[:, P:P + 1], 1.0))
                    st.go(v.memset(keep[:, 3 * P + 1:3 * P + 2], 1.0))
                    for cols, at, _ in halves:
                        last = v.tensor_scalar(keep[:, at], e[:, cols], BIG, 1.0, ALU.min, ALU.add)
                        st.go(last) if cols.start == 0 else st.did(last)
                    st.did(v.reciprocal(keep, keep))
                    for cols, at, _ in halves:
                        last = v.scalar_tensor_tensor(e[:, cols], e[:, cols], BIG, keep[:, at], ALU.min, ALU.mult)
                        st.go(last) if cols.start == 0 else st.did(last)
                    for cols, at, _ in halves:
                        k = keep[:, at]
                        last = v.tensor_tensor_scan(k[:, ::-1], k[:, ::-1], k[:, ::-1], 1.0, ALU.mult, ALU.min)
                        st.go(last) if cols.start == 0 else st.did(last)
                    cols, _, later = halves[0]
                    st.go(v.tensor_tensor(e[:, cols], e[:, cols], keep[:, later], ALU.mult))
                    cols, _, later = halves[1]
                    v.tensor_tensor(e[:, cols], e[:, cols], keep[:, later], ALU.mult).then_inc(prob_ready, 1)

                def take(n):
                    m, h = HEAD_ORDER[n]
                    v.wait_ge(pv_done, n0 + n + 1)
                    b = bank(6)[:, 384:512]
                    o = o_or_acc[:, 0:2, m * WID + h * HD:m * WID + (h + 1) * HD]
                    if m == 0:
                        st.go(v.tensor_scalar(o[:, 0, :], b[:, 0:HD], stat[:, 4:5], None, ALU.mult))
                        v.tensor_scalar(o[:, 1, :], b[:, HD:2 * HD], stat[:, 5:6], None, ALU.mult).then_inc(o_copied, 1)
                    else:
                        v.tensor_copy(o, b.rearrange("p (t d) -> p t d", t=2)).then_inc(o_copied, 1)
                    v.wait_ge(o_copied, n0 + n + 1)

                def weigh(g):
                    v.wait_ge(d_scored, (KTILES + 1) * (B + GSEQ * (g + 1)))
                    v.scalar_tensor_tensor(probs[:, PAST:PAST + SAMPLE], bank(5)[:, P + SAMPLE:P + 2 * SAMPLE], SCALE,
                                           new_bias[:, 1, g, :], ALU.mult, ALU.add).then_inc(sb_new_masked, 1)
                    st.go(v.scalar_tensor_tensor(swa_s[:, 0:SWA_KEYS], psum[:, 4 * CH:4 * CH + SWA_KEYS], SCALE,
                                                 past_bias[:, :], ALU.mult, ALU.add))
                    st.did(v.scalar_tensor_tensor(swa_s[:, SWA_KEYS:], bank(5)[:, P:P + SAMPLE], SCALE,
                                                  new_bias[:, 0, g, :], ALU.mult, ALU.add))
                    v.reduce_max(dstat[:, 0:1], swa_s, AX, negate=True).then_inc(swa_taken, 1)
                    v.wait_ge(sb_exped, 2 * (W + g + 1))
                    e, keep = probs, keeps[:, 0:PAST + SAMPLE]
                    st.go(v.memset(keeps[:, PAST + SAMPLE:], 1.0))
                    st.did(v.tensor_scalar(keep, e, BIG, 1.0, ALU.min, ALU.add))
                    st.did(v.reciprocal(keep, keep))
                    st.did(v.scalar_tensor_tensor(e, e, BIG, keep, ALU.min, ALU.mult))
                    st.did(v.tensor_tensor_scan(keep[:, ::-1], keep[:, ::-1], keep[:, ::-1], 1.0, ALU.mult, ALU.min))
                    v.tensor_tensor(e, e, keeps[:, 1:], ALU.mult).then_inc(sb_weights, 1)
                    v.wait_ge(swa_exped, W + g + 1)
                    st.did(v.reciprocal(dstat[:, 2:3], dstat[:, 1:2]))
                    v.tensor_scalar(swa_s, swa_s, dstat[:, 2:3], None, ALU.mult).then_inc(swa_weights, 1)

                queries(0)
                for step in ORDER:
                    if step[0] == "score":
                        mask(step[1])
                        head_weights(step[1])
                    elif step[0] == "probs":
                        take(step[1])
                    elif step[0] == "key" and step[2] == 0 and step[1] + 1 < NS:
                        queries(step[1] + 1)
                    elif step[0] == "weigh":
                        weigh(step[1])
                for t in range(T):
                    r = ROWS[t]
                    n = norm[0:r, t, :]
                    v.wait_ge(act_step, 2 * T * L + 2 * (t + 1))
                    v.tensor_scalar(n[:, 2:4], n[:, 0:2], 1.0 / WID, RMS_EPS, ALU.mult, ALU.add).then_inc(sq_done, 1)
                    v.wait_ge(rms_root, T * L + t + 1)
                    st.did(v.reciprocal(n[:, 18:20], n[:, 4:6]))
                    for m in range(2):
                        o = o_or_acc[0:r, t, m * WID:(m + 1) * WID]
                        last = v.tensor_scalar(o, o, n[:, 18 + m:19 + m], None, ALU.mult)
                        if m == 0:
                            st.go(last)
                        else:
                            last.then_inc(rms_scaled, 1)
                for c in range(2):
                    for t in range(T):
                        r = ROWS[t]
                        v.wait_ge(wo_done, 6 * L + T * c + t + 1)
                        x = x_tok[0:r, t, c * CH:(c + 1) * CH]
                        v.scalar_tensor_tensor(x, x, ALPHA, bank(2 + T * c + t)[0:r, :], ALU.mult, ALU.add).then_inc(wo_added, 1)
                v.wait_ge(wo_added, 6 * (L + 1))
                for t in range(T):
                    layer_norm(t, 2 * T * L, 64 * L + 32, st)
                if L == 0:
                    v.wait_ge(stored_kv, 160 * (L + 1))
                    v.wait_ge(stored_win, 16 * 2 * NS * (L + 1))
                    for f in range(DENSE_F):
                        a = 2 + 2 * (f % 2)
                        rr, tt = silu_r[f % 2][:, 0:TOK], silu_t[f % 2][:, 0:TOK]
                        v.wait_ge(gu_exp, f + 1)
                        st.did(v.tensor_scalar(rr, rr, BIG, 1.0, ALU.min, ALU.add))
                        st.did(v.reciprocal(rr, rr))
                        st.did(v.tensor_tensor(tt, rr, bank(a)[:, 0:TOK], ALU.mult))
                        v.wait_ge(gu_done, 2 * f + 2)
                        v.tensor_tensor(hT[:, f, :], tt, bank(a + 1)[:, 0:TOK], ALU.mult).then_inc(gu_free, 1)
                    v.wait_ge(down_done, len(DENSE_CHUNKS))
                    for t in range(T):
                        r = ROWS[t]
                        v.scalar_tensor_tensor(x_tok[0:r, t, :], x_tok[0:r, t, :], ALPHA,
                                               psum[0:r, (2 + 2 * t) * CH:(4 + 2 * t) * CH], ALU.mult, ALU.add)\
                            .then_inc(ffn_added, 2)
                        v.wait_ge(ffn_added, 2 * t + 2)
                        layer_norm(t, T, 64, st)
            v.wait_ge(router_in, 16 * 8)
            st.did(v.memset(logit, 0.0))
            v.wait_ge(logits_done, 1)
            for t in range(T):
                r = ROWS[t]
                st.did(v.tensor_copy(logit[0:r, t, :], bank(2)[0:r, t * EXPERTS:(t + 1) * EXPERTS]))
            for n, hot in enumerate((hot1, hot2)):
                st.did(v.reduce_max(vals[:, :, n:n + 1], logit, AX))
                st.did(v.tensor_tensor(tie, logit, vals[:, :, n:n + 1].to_broadcast([P, T, EXPERTS]), ALU.is_equal))
                st.did(v.tensor_tensor(tie, tie, descending, ALU.mult))
                st.did(v.reduce_max(vals[:, :, 4:5], tie, AX))
                st.did(v.tensor_tensor(hot, descending, vals[:, :, 4:5].to_broadcast([P, T, EXPERTS]), ALU.is_equal))
                if n == 0:
                    st.did(v.scalar_tensor_tensor(logit, hot, NEG, logit, ALU.mult, ALU.add))
            v.tensor_tensor(vals[:, :, 2:3], vals[:, :, 1:2], vals[:, :, 0:1], ALU.subtract).then_inc(logits_copied, 1)
            st.did(v.tensor_tensor(chosen, hot1, hot2, ALU.add))
            v.tensor_tensor(chosen, chosen, is_token, ALU.mult).then_inc(chosen_ready, 1)
            v.wait_ge(gate_exp2, 1)
            st.did(v.tensor_scalar(vals[:, :, 5:6], vals[:, :, 3:4], 1.0, None, ALU.add))
            st.did(v.reciprocal(vals[:, :, 6:7], vals[:, :, 5:6]))
            st.did(v.tensor_tensor(vals[:, :, 7:8], vals[:, :, 3:4], vals[:, :, 6:7], ALU.mult))
            st.did(v.tensor_tensor(hot1, hot1, vals[:, :, 6:7].to_broadcast([P, T, EXPERTS]), ALU.mult))
            st.did(v.tensor_tensor(hot2, hot2, vals[:, :, 7:8].to_broadcast([P, T, EXPERTS]), ALU.mult))
            st.did(v.tensor_tensor(gates, hot1, hot2, ALU.add))
            v.wait_ge(ranks_done, 1)
            v.wait_ge(chosen_ready, 1)
            st.did(v.tensor_scalar(ranks, bank(3)[:, 0:T * EXPERTS].rearrange("p (t e) -> p t e", t=T), 1.0, None, ALU.add))
            st.did(v.tensor_tensor(ranks, ranks, chosen, ALU.mult))
            tokens, items, upto, first = (per_expert[:, a, :] for a in range(4))
            st.did(v.tensor_copy(tokens, bank(3)[:, T * EXPERTS:(T + 1) * EXPERTS]))
            st.did(v.tensor_scalar(items, tokens, 0.0, None, ALU.is_gt))
            for p in range(1, PASSES):
                st.did(v.scalar_tensor_tensor(items, tokens, float(ITEM * p), items, ALU.is_gt, ALU.add))
            st.did(v.tensor_scalar(first, items, 0.0, None, ALU.mult))
            st.did(v.tensor_tensor_scan(upto, items, first, 0.0, ALU.add, ALU.add))
            st.did(v.tensor_tensor(first, upto, items, ALU.subtract))

            def every_item(x):
                return x.unsqueeze(1).to_broadcast([P, NI, EXPERTS])

            st.did(v.tensor_tensor(first_rank, item_number, every_item(first), ALU.subtract))
            st.did(v.tensor_tensor(of_item, first_rank, every_item(items), ALU.is_lt))
            st.did(v.tensor_scalar(wide, first_rank, 0.0, None, ALU.is_ge))
            st.did(v.tensor_tensor(of_item, of_item, wide, ALU.mult))
            st.did(v.tensor_scalar(first_rank, first_rank, float(ITEM), None, ALU.mult))
            for t in range(T):
                st.did(v.tensor_tensor(wide, every_item(ranks[:, t, :]), first_rank, ALU.subtract))
                st.did(v.tensor_tensor(wide, wide, of_item, ALU.mult))
                st.did(v.reduce_sum(rank_of[:, t, :], wide, AX))
                st.did(v.tensor_tensor(wide, every_item(gates[:, t, :]), of_item, ALU.mult))
                st.did(v.reduce_sum(gate_of[:, t, :], wide, AX))
            st.did(v.tensor_tensor(wide, expert_number, of_item, ALU.mult))
            st.did(v.reduce_sum(plan_f[:, 1:NI + 1], wide, AX))
            st.did(v.tensor_copy(plan_f[:, 0:1], upto[:, EXPERTS - 1:EXPERTS]))
            v.memset(o_or_acc[:, :, :], 0.0).then_inc(added, 6)
            v.wait_ge(added, 6)
            v.tensor_copy(plan[0:1, 0:NI + 1], plan_f[0:1, :]).then_inc(plan_ready, 1)
            v.wait_ge(plan_ready, 1)
            v.wait_ge(stored_kv, 160 * LAYERS)
            v.wait_ge(stored_win, 16 * 2 * NS * LAYERS)

            def make_pick(i, steps):
                for t in range(T):
                    r = rank_of[0:ROWS[t], t, :]
                    last = v.tensor_scalar(pick[0:ROWS[t], t, :], slot_number[0:ROWS[t], :], r[:, bass.ds(i, 1)], None, ALU.is_equal)
                    if t < T - 1:
                        steps.go(last)
                last.then_inc(pick_ready, 1)

            make_pick(0, st)
            K = 2 + 3 * MOE_CHUNKS
            entry = st.n
            count = v.value_load(plan[0:1, 0:1], min_val=0, max_val=ITEMS)
            with v.Fori(0, ITEMS) as i:
                with v.If(i < count):
                    st.base, st.n = K * i, entry
                    for c in range(MOE_CHUNKS):
                        b = 2 + 2 * (c % 2)
                        rr, tt = silu_r[c % 2], silu_t[c % 2]
                        v.wait_ge(e_exp, MOE_CHUNKS * i + (c + 1))
                        st.did(v.tensor_scalar(rr, rr, BIG, 1.0, ALU.min, ALU.add))
                        st.did(v.reciprocal(rr, rr))
                        st.did(v.tensor_tensor(tt, rr, bank(b), ALU.mult))
                        v.wait_ge(e_gu, 2 * MOE_CHUNKS * i + (2 * c + 2))
                        v.tensor_tensor(hE[:, FPC * c:FPC * (c + 1), :], tt.rearrange("p (f s) -> p f s", f=FPC),
                                        bank(b + 1).rearrange("p (f s) -> p f s", f=FPC), ALU.mult).then_inc(e_h, 1)
                    v.wait_ge(pick_turned, i + 1)
                    make_pick(i + 1, st)
                    v.wait_ge(added, 6 * i + 6)
                    for n in range(2 * T):
                        t, h = divmod(n, 2)
                        v.wait_ge(combined, 6 * i + (n + 1))
                        acc = o_or_acc[0:ROWS[t], t, h * CH:(h + 1) * CH]
                        v.scalar_tensor_tensor(acc, bank((6, 7, 0, 1)[n % 4])[0:ROWS[t], :],
                                               gate_of[0:ROWS[t], t, bass.ds(i, 1)], acc, ALU.mult, ALU.add).then_inc(added, 1)
                    assert st.n - entry == K, st.n - entry
            tail = Steps(v, dve_tail)
            v.wait_ge(added, count * 6 + 6)
            for t in range(T):
                r = ROWS[t]
                tail.did(v.scalar_tensor_tensor(x_tok[0:r, t, :], x_tok[0:r, t, :], ALPHA, o_or_acc[0:r, t, :], ALU.mult, ALU.add))
                layer_norm(t, 3 * T, 128, tail)


_OUTS = [(1, 256, 1024), (8, 4, 1024),
         (2, 1, 256, 8, 64), (2, 1, 256, 8, 64), (2, 8, 4, 8, 64), (2, 8, 4, 8, 64),
         (2, 1, 256, 8, 64), (2, 1, 256, 8, 64), (2, 8, 1024, 8, 64), (2, 8, 1024, 8, 64)]


def kernel(**inputs):
    import numpy as _np
    import concourse.bacc as _bacc
    from concourse import mybir as _mybir
    from concourse.bass_utils import run_bass_kernel_spmd as _run

    nc = _bacc.Bacc("TRN2", target_bir_lowering=False, num_devices=1)
    arrays, ins = {}, {}
    inputs = {n: _np.asarray(a) for n, a in inputs.items()}
    g = _np.concatenate([inputs["g_mix_a"], inputs["g_mix_b"]], 1).reshape(2, 8, 128)
    inputs["g_mix_cols"] = g.transpose(2, 0, 1)
    inputs["sb_bias_all"] = _np.broadcast_to(inputs["sb_bias"], (128, 2, 8))
    inputs["sb_bias_rows"] = _np.tile(_np.repeat(inputs["sb_bias"], 4, axis=1), 4).T
    for name, a in list(inputs.items()) + list(position_tables().items()):
        a = _np.ascontiguousarray(a)
        arrays[f"in_{name}"] = a
        ins[name] = nc.dram_tensor(f"in_{name}", a.shape, _mybir.dt.from_np(a.dtype), kind="ExternalInput").ap()
    outs = [nc.dram_tensor(f"out_{i}", shape, _mybir.dt.float32, kind="ExternalOutput").ap()
            for i, shape in enumerate(_OUTS)]
    hybrid_decode_step(nc, ins, outs)
    r = _run(nc, [arrays], core_ids=[0])
    return tuple(r.results[0][f"out_{i}"] for i in range(len(_OUTS)))
```

```python
from contextlib import ExitStack

import numpy as np

import concourse.bass as bass
from concourse import mybir

F32 = mybir.dt.float32
I32 = mybir.dt.int32
ALU = mybir.AluOpType
ACT = mybir.ActivationFunctionType
AX = mybir.AxisListType.X

P = 128
D = 1024
KD = D // P
SEQ, NS, DEC = 256, 8, 4
LAYERS = 2
HEADS, HD = 8, 64
HP = HEADS // 2
WID = HEADS * HD
PAST, PAGE = 1024, 128
PAGES = PAST // PAGE
SAMPLE = NS * DEC
ROWS = (P, P, SAMPLE)
T = len(ROWS)
TOK = SEQ + SAMPLE
FF, FFE, EXPERTS = 2816, 3584, 8
CH = 512
FPC = CH // P
SLOT = KD * CH
NSLOT = 7
TOP_K = 2
ITEM = 128
PASSES = -(-TOK // ITEM)
ITEMS = TOP_K * TOK // ITEM + EXPERTS
SPARSE = 512
SWA_TILES = 5
SWA_KEYS = SWA_TILES * P
KTILES = PAGES + SWA_TILES
GSEQ = P // SAMPLE
GROUPS = NS // GSEQ
SCALE = HD ** -0.5
ALPHA = (2 * LAYERS) ** 0.25
LN_EPS, RMS_EPS = 1e-5, 1e-6
BIG = 1e34
NEG = -1e30
BRANCHES = ((128, 1), (512, 4), (2048, 16))


def position_tables():
    def ln_count(dist):
        n = sum((dist % d == 0) & (dist <= w) for w, d in BRANCHES)
        return np.where((dist >= 0) & (n > 0), np.log(np.maximum(n, 1)), NEG)

    q, k = np.arange(P)[:, None], np.arange(P)[None, :]
    dist = np.concatenate([q - k, q - k + P, q - k], 1)
    slopes = 2.0 ** (-8.0 * np.arange(1, HEADS + 1) / HEADS)
    col = np.arange(SWA_KEYS)
    dense = SPARSE + (SWA_TILES - 1) * (col % P) + col // P
    s = col - (PAST - SPARSE)
    row = np.where(s < 0, dense, 16 * (s % 32) + s // 32)
    far = PAST + np.arange(DEC)[:, None] - row[None, :]
    past = -slopes[:, None, None] * far[None] + ln_count(far)[None]
    i, seq, owner, j = (a.reshape(s) for a, s in ((np.arange(DEC), (DEC, 1, 1, 1)), (np.arange(NS), (1, NS, 1, 1)),
                                                 (np.arange(NS), (1, 1, NS, 1)), (np.arange(DEC), (1, 1, 1, DEC))))
    own = np.where(seq == owner, ln_count(i - j), NEG)
    new_a = -slopes[:, None, None, None, None] * (i - j)[None] + own[None]
    new_b = np.broadcast_to(np.where((seq == owner) & (j < i), 0.0, NEG), new_a.shape)

    def by_group(a):
        a = a.transpose(2, 0, 1, 3, 4).reshape(GROUPS, P, SAMPLE)
        return a.transpose(1, 0, 2)

    tok = np.arange(P)[:, None, None] + P * np.arange(T)[None, :, None]
    one = np.ones((1, 1, EXPERTS))
    tabs = {
        "distance": dist, "ln_branches": ln_count(dist), "strict_mask": np.where(dist > 0, 0.0, NEG),
        "past_bias": np.tile(past.reshape(HEADS * DEC, SWA_KEYS), (P // (HEADS * DEC), 1)),
        "new_bias": np.stack([by_group(new_a), by_group(new_b)], 1),
        "own_head": (q % SAMPLE) // DEC == np.arange(HEADS)[None, :],
        "token_of": (SAMPLE // GROUPS) * np.arange(GROUPS)[None, :, None] + (DEC * (q // SAMPLE) + q % DEC)[:, :, None]
        == np.arange(SAMPLE)[None, None, :],
        "identity": np.eye(P), "earlier": np.triu(np.ones((P, P)), 1), "ones": np.ones((P, P)),
        "slot_number": np.broadcast_to(1.0 + np.arange(ITEM), (P, ITEM)),
        "descending": np.broadcast_to(np.arange(EXPERTS, 0, -1), (P, T, EXPERTS)),
        "is_token": (tok < TOK) * one,
        "item_number": np.broadcast_to(np.arange(ITEMS + 1)[None, :, None], (P, ITEMS + 1, EXPERTS)),
        "expert_number": np.broadcast_to(np.arange(EXPERTS)[None, None, :], (P, ITEMS + 1, EXPERTS)),
    }
    return {n: np.ascontiguousarray(a, np.float32) for n, a in tabs.items()}


class Steps:

    def __init__(self, eng, sem):
        self.eng, self.sem, self.n, self.base = eng, sem, 0, None

    def value(self):
        return self.n if self.base is None else self.base + self.n

    def go(self, ins):
        self.n += 1
        ins.then_inc(self.sem, 1)

    def did(self, ins):
        self.go(ins)
        self.eng.wait_ge(self.sem, self.value())


PROJ_SLOTS = ((2, 3, 4, 5, 6, 0), (6, 1, 0, 2, 3, 4))
WO_SLOTS = ((1, 0), (1, 0))
CYCLE = ((2, 3, 4, 5, 6, 1, 0), (2, 3, 4, 5, 6, 1, 0))
DENSE_CHUNKS = [(c, min(FPC, FF // P - FPC * c)) for c in range(-(-FF // CH))]
DENSE_F = FF // P
DOWN_WHOLE = len(DENSE_CHUNKS) - 2
MOE_CHUNKS = FFE // CH
MOE_F = FFE // P
UNITS_Q, UNITS_KV = FPC, T
PROJ_UNITS = 2 * UNITS_Q + 4 * UNITS_KV


def attention_order():
    starts = [(s, j) for s in range(GSEQ) for j in (0, 6)]
    ends = [(s + j // KTILES, j % KTILES) for s in range(GSEQ) for j in (8, 15)]
    ends[-1] = (GSEQ - 1, KTILES - 1)
    starts += [(5, 0), (5, 4), (5, 8), (6, 0), (6, 4), (6, 8), (7, 0), (7, 6)]
    ends += [(5, 6), (5, 10), (6, 1), (6, 6), (6, 10), (7, 1), (7, 7), (7, 12)]
    steps = []
    woven = {at: [("value", s, 0), ("value", s, 1)] for s, at in enumerate(((5, 4), (6, 0), (6, 8), (7, 6)))}
    woven[5, 4] = [("turn", 0, 0), ("turn", 0, 1)] + woven[5, 4]
    woven[7, 9] = [("select", 0)]
    for s in range(NS):
        for j in range(KTILES):
            if (s, j) in ends:
                steps.append(("probs", ends.index((s, j))))
            steps += woven.get((s, j), [])
            steps.append(("key", s, j))
            if (s, j) in starts:
                steps.append(("score", starts.index((s, j))))
        if s % GSEQ == GSEQ - 1:
            steps.append(("weigh", s // GSEQ))
    steps += [("turn", 1, 0), ("value", 4, 0), ("value", 5, 0), ("turn", 1, 1), ("value", 4, 1), ("value", 5, 1)]
    steps += [("value", s, m) for s in range(6, NS) for m in range(2)] + [("select", 1)]
    return steps


ORDER = attention_order()


def before(kind, step):
    return sum(x[0] == kind for x in ORDER[:ORDER.index(step)])


HEAD_ORDER = [(1, h) for h in range(HEADS)] + [(0, h) for h in range(HEADS)]
UNITS_OF = {"key": 1, "probs": 1}
UNIT_AT, ATT_UNITS = {}, 0
for _step in ORDER:
    UNIT_AT[_step] = ATT_UNITS
    ATT_UNITS += 2 + _step[2] if _step[0] == "turn" else UNITS_OF.get(_step[0], 0)
VALUES_AT = [0] * GSEQ + [1, 0] * (GSEQ // 2)
LAST_THERE = [max((x for x in range(s) if VALUES_AT[x] == VALUES_AT[s]), default=None) for s in range(NS)]
HALF = PAGES // 2
OUT_AT, OUT_UNITS = {}, 0
for _step in ORDER:
    OUT_AT[_step] = OUT_UNITS
    OUT_UNITS += {"value": 1, "select": 2}.get(_step[0], 0)


def out_unit(L, *step):
    return OUT_UNITS * L + OUT_AT[step]


ITEM_LOADS = 3 * MOE_CHUNKS


def hybrid_decode_step(nc, ins, outs):
    y_p, y_s, sbk_p, sbv_p, sbk_s, sbv_s, swk_p, swv_p, swk_s, swv_s = outs
    ctx = ExitStack()
    with ctx:
        def sb(name, shape, dt=F32):
            return ctx.enter_context(nc.sbuf_tensor(name, shape, dt))

        def sem(name):
            return ctx.enter_context(nc.semaphore(name))

        ring = sb("ring", [P, NSLOT * SLOT])
        xT = sb("xT", [P, KD * TOK])
        x_tok = sb("x_tok", [P, T, D])
        kv_or_h = sb("kv_or_h", [P, DENSE_F * TOK])
        q_or_o = sb("q_or_o", [P, KD * TOK])
        k_or_ln = sb("k_or_ln", [P, KD * TOK])
        o_or_acc = sb("o_or_acc", [P, T, D])
        prompt_tab = sb("prompt_tab", [P, 3, 3 * P])
        past_bias = sb("past_bias", [P, SWA_KEYS])
        new_bias = sb("new_bias", [P, 2, GROUPS, SAMPLE])
        ident = sb("ident", [P, P])
        sb_probT = sb("sb_probT", [P, PAGES + 1, P])
        swa_probT = sb("swa_probT", [P, SWA_TILES + 1, P])
        own_head = sb("own_head", [P, HEADS])
        token_of = sb("token_of", [P, GROUPS, SAMPLE])
        g_mix = sb("g_mix", [P, LAYERS, KD])
        sb_bias = sb("sb_bias", [P, LAYERS, HEADS])
        sb_bias_rows = sb("sb_bias_rows", [P, LAYERS])
        stats = sb("stats", [P, 2, 8])
        norm = sb("norm", [P, T, 24])
        dstat = sb("dstat", [P, 4])
        pages = sb("pages", [1, NS * PAGES], I32)
        plan = sb("plan", [1, ITEMS + 2], I32)
        psum = ctx.enter_context(nc.psum_tensor("psum", [P, 8 * CH], F32))

        def bank(b, n=1):
            return psum[:, b * CH:(b + n) * CH]

        xTv = xT[:, :].rearrange("p (k t) -> p k t", k=KD)
        kv = kv_or_h[:, 0:T * 4 * WID].rearrange("p (t g f) -> p t g f", t=T, g=4)
        hT = kv_or_h[:, :].rearrange("p (f t) -> p f t", f=DENSE_F)
        hE = kv_or_h[:, 0:MOE_F * ITEM].rearrange("p (f t) -> p f t", f=MOE_F)
        qT = q_or_o[:, :].rearrange("p (k t) -> p k t", k=KD)
        kT = k_or_ln[:, :].rearrange("p (k t) -> p k t", k=KD)
        ln_gb = k_or_ln[:, 0:2 * D].rearrange("p (a d) -> p a d", a=2)
        probs = xT[:, 0:PAST + SAMPLE]
        keeps = xT[:, PAST + SAMPLE:2 * (PAST + SAMPLE) + 1]
        own_o = keeps[:, 0:2 * WID].rearrange("p (m d) -> p m d", m=2)
        att, att_at = ring[:, 2 * SLOT:7 * SLOT], [0]

        def take_att(*shape):
            n = int(np.prod(shape))
            v = att[:, att_at[0]:att_at[0] + n]
            att_at[0] += n
            assert att_at[0] <= 5 * SLOT
            return v.rearrange("p (a b) -> p a b", b=shape[-1]) if len(shape) > 1 else v

        k_half = [take_att(PAGES // 2, WID) for _ in range(3)]
        k_swa = take_att(SWA_TILES, WID)
        v_sb = [take_att(PAGES, WID), att[:, 0:PAGES * WID].rearrange("p (a b) -> p a b", b=WID)]
        v_swa = [take_att(SWA_TILES, WID), k_swa]
        kstage = take_att(4, WID)
        swa_s = take_att(SWA_KEYS + SAMPLE)
        head_es, head_keep = [take_att(3 * P) for _ in range(2)], take_att(3 * P + 2)
        head_pT = take_att(3 * P)
        qblk = [take_att(2, HP * SAMPLE) for _ in range(2)]
        silu_r = [q_or_o[:, a * CH:(a + 1) * CH] for a in (0, 2)]
        silu_t = [q_or_o[:, a * CH:(a + 1) * CH] for a in (1, 3)]
        beside_h = kv_or_h[:, MOE_F * ITEM:]
        pick = beside_h[:, 0:T * ITEM].rearrange("p (t s) -> p t s", t=T)
        pickT = beside_h[:, T * ITEM:T * ITEM + TOK]
        xg = xT[:, 0:KD * ITEM].rearrange("p (k s) -> p k s", k=KD)
        y_item = xT[:, KD * ITEM:KD * ITEM + D]
        ptab = prompt_tab[:, :, :].rearrange("p a b -> p (a b)")
        earlier, ones, slot_number = ptab[:, 0:P], ptab[:, P:2 * P], ptab[:, 2 * P:3 * P]
        w_router = ptab[:, 3 * P:3 * P + KD * EXPERTS].rearrange("p (k e) -> p k e", k=KD)
        NI = ITEMS + 1

        def rows_of(where, at, n, m):
            return where[:, at:at + n * m].rearrange("p (t e) -> p t e", t=n)
        descending, is_token = rows_of(ptab, 448, T, 8), rows_of(ptab, 472, T, 8)
        item_number, expert_number = rows_of(ptab, 496, NI, 8), rows_of(ptab, 600, NI, 8)
        rank_of, gate_of = rows_of(ptab, 704, T, NI), rows_of(ptab, 744, T, NI)
        chosen, gates, ranks = (rows_of(ptab, 784 + 24 * a, T, 8) for a in range(3))
        vals = rows_of(ptab, 856, T, 8)
        logit, tie, hot1, hot2 = (rows_of(q_or_o, 24 * a, T, 8) for a in range(4))
        of_item, first_rank, wide = (rows_of(q_or_o, 104 + 104 * a, NI, 8) for a in range(3))
        per_expert = rows_of(q_or_o, 420, 4, 8)
        plan_f = q_or_o[:, 460:460 + NI + 1]
        mean_sq_out = xT[:, 0:WID]

        w_loaded = [sem(f"w_loaded{s}") for s in range(NSLOT)]
        tables_in, ident_in, x_in, router_in = sem("tables_in"), sem("ident_in"), sem("x_in"), sem("router_in")
        ln_in = sem("ln_in")
        tp_full, tp_free = sem("transposes_done"), sem("transposes_copied")
        proj_done, proj_free = sem("projections_done"), sem("projections_copied")
        scored, masked, expd, prob_ready = sem("scored"), sem("masked"), sem("exponentials"), sem("probs_ready")
        pv_done, o_copied = sem("pv_done"), sem("o_copied")
        khalf_in = [sem(f"khalf_in{a}") for a in range(3)]
        kswa_in = sem("kswa_in")
        vsb_in, vswa_in = ([sem(f"{name}{a}") for a in range(2)] for name in ("vsb_in", "vswa_in"))
        qblk_ready = sem("qblk_ready")
        d_scored, sb_exped, swa_taken = sem("dec_scored"), sem("sb_exponentials"), sem("swa_scores_taken")
        sb_new_masked, swa_exped = sem("sb_new_masked"), sem("swa_exponentials")
        sb_weights, swa_weights = sem("sb_weights"), sem("swa_weights")
        d_o, d_ocopied = sem("dec_o_done"), sem("dec_o_copied")
        sq_done, rms_root, rms_scaled = sem("squares_summed"), sem("rms_root"), sem("rms_scaled")
        wo_done, wo_added = sem("wo_done"), sem("wo_added")
        var_ready, ln_root, ln_done = sem("var_ready"), sem("ln_root"), sem("ln_done")
        gu_done, gu_exp, gu_free = sem("gate_up_done"), sem("gate_exp"), sem("gate_up_used")
        down_done, ffn_added = sem("down_done"), sem("ffn_added")
        stored_kv, stored_win, stored_y, shifted = sem("stored_kv"), sem("stored_window"), sem("stored_y"), sem("shifted")
        logits_done, logits_copied, chosen_ready = sem("logits_done"), sem("logits_copied"), sem("chosen_ready")
        gate_exped, ranks_done, plan_ready = sem("gate_exponentials"), sem("ranks_done"), sem("plan_ready")
        pick_ready, gathered, gather_copied = sem("pick_ready"), sem("gathered"), sem("gather_copied")
        pick_turned, pickT_copied = sem("pick_turned"), sem("pickT_copied")
        e_gu, e_exp, e_h, e_down = sem("expert_gate_up"), sem("expert_exp"), sem("expert_h"), sem("expert_down")
        y_copied, combined, added = sem("y_copied"), sem("combined"), sem("combined_added")
        act_step, dve_step, dve_tail = sem("act_step"), sem("dve_step"), sem("dve_tail")

        KHALF_USES = [len(range(a, 2 * NS, 3)) for a in range(3)]
        tp_at = {}
        u = 0
        for L in range(LAYERS):
            for name, n in ((("x", 6),) if L == 0 else ()) + (("k", 6), ("att", ATT_UNITS),
                                                              ("merge", 6), ("mix", 6)) + ((("ffn", 6),) if L == 0 else ()):
                tp_at[L, name] = u
                u += n
        loads = [0] * NSLOT

        def slot_view(s, k=KD):
            return ring[:, s * SLOT:(s + 1) * SLOT].rearrange("p (k f) -> p k f", k=k)

        stream = []
        used = [None] * NSLOT

        def chunk(key, slot, src, shape_k, freed):
            loads[slot] += 1
            stream.append((key, slot, src, shape_k, used[slot], loads[slot]))
            used[slot] = freed

        for L in range(LAYERS):
            w_in = ins["w_in"][L].rearrange("(k p) f -> p k f", p=P)
            at = 0
            for c in range(6):
                at += UNITS_Q if c % 3 == 0 else UNITS_KV
                chunk((L, "proj", c), PROJ_SLOTS[L][c], w_in[:, :, c * CH:(c + 1) * CH], KD,
                      (proj_done, PROJ_UNITS * L + at))
            w_o = ins["w_o"][L].rearrange("(k p) f -> p k f", p=P)
            for c in range(2):
                chunk((L, "wo", c), WO_SLOTS[L][c], w_o[:, :, c * CH:(c + 1) * CH], KD,
                      (wo_done, 2 * T * L + 2 * (T - 1) + c + 1))
            if L == 0:
                n = 0
                wg, wu = (ins[w][0].rearrange("(k p) f -> p k f", p=P) for w in ("w_gate", "w_up"))
                for c, m in DENSE_CHUNKS:
                    for b, w in enumerate((wg, wu)):
                        chunk((L, "gu"[b], c), CYCLE[L][n % NSLOT], w[:, :, c * CH:c * CH + m * P], KD,
                              (gu_done, 2 * (FPC * c + m) - 1 + b))
                        n += 1
                wd = ins["w_down"][0].rearrange("(f p) d -> p f d", p=P)
                for c, m in DENSE_CHUNKS:
                    chunk((L, "d", c), CYCLE[L][n % NSLOT], wd[:, FPC * c:FPC * c + m, :], FPC,
                          (down_done, c + 1 if c < DOWN_WHOLE else DOWN_WHOLE + T))
                    n += 1
        loaded_at = {key: (slot, 16 * n) for key, slot, _, _, _, n in stream}
        moe_base, moe_used = list(loads), list(used)
        we = [ins[w].rearrange("o e (k p) f -> (o e) p k f", p=P) for w in ("we_gate", "we_up")]
        wed = ins["we_down"].rearrange("o e (f p) d -> (o e) p f d", p=P)
        item_loads = [("gu"[n % 2], n // 2) if n < 2 * MOE_CHUNKS else ("d", n - 2 * MOE_CHUNKS) for n in range(ITEM_LOADS)]

        def item_slot(n):
            return CYCLE[1][n % NSLOT]

        def item_loaded(eng, n, i):
            s = item_slot(n)
            eng.wait_ge(w_loaded[s], 16 * 3 * i + 16 * (moe_base[s] + n // NSLOT + 1))

        def arrived(eng, key):
            s, v = loaded_at[key]
            eng.wait_ge(w_loaded[s], v)
            return slot_view(s, FPC if key[1] == "d" else KD)

        def projection_used(L, slot):
            c = PROJ_SLOTS[L].index(slot)
            return proj_done, PROJ_UNITS * L + sum(UNITS_KV if x % 3 else UNITS_Q for x in range(c + 1))

        def page_numbers(eng, first_page, n):
            return [eng.value_load(pages[0:1, first_page + j:first_page + j + 1],
                                   min_val=0, max_val=ins["cache_sb_k"].shape[1] - 1) for j in range(n)]

        def load_pages(eng, L, dst, name, loaded, numbers):
            cache = ins[name][L].rearrange("b n h d -> b n (h d)")
            for j, page in enumerate(numbers):
                eng.dma_start(dst[:, j, :], cache[bass.ds(page, 1), :, :].rearrange("o p f -> (o p) f"))\
                   .then_inc(loaded, 16)

        def load_window(eng, L, dst, name, loaded, s):
            seq = ins[name][L, s].rearrange("n h d -> n (h d)")
            near = seq[SPARSE:PAST, :].rearrange("(p c) f -> p c f", c=SWA_TILES - 1)
            eng.dma_start(dst[:, 0:SWA_TILES - 1, :], near).then_inc(loaded, 16)
            far = seq[0:SPARSE, :].rearrange("(a b) f -> a b f", b=16)
            for b in range(DEC):
                eng.dma_start(dst[32 * b:32 * b + 32, SWA_TILES - 1, :], far[:, b, :]).then_inc(loaded, 16)

        block = ctx.enter_context(nc.Block())

        @block.sync
        def _(sp):
            def tab(dst, name):
                sp.dma_start(dst, ins[name]).then_inc(tables_in, 16)

            for t in range(2):
                sp.dma_start(x_tok[:, t, :], ins["x_prompt"][0, t * P:(t + 1) * P, :]).then_inc(x_in, 16)
            sp.dma_start(x_tok[0:SAMPLE, 2, :], ins["x_sample"].rearrange("b t d -> (b t) d")).then_inc(x_in, 16)
            sp.dma_start(ident[:, :], ins["identity"]).then_inc(ident_in, 16)

            def load(n):
                key, slot, src, k, freed, _ = stream[n]
                if freed:
                    sp.wait_ge(*freed)
                w = src.shape[-1] if k == KD else None
                dst = slot_view(slot, k)
                dst = dst[:, :, 0:w] if k == KD else dst[:, 0:src.shape[1], :]
                sp.dma_start(dst, src).then_inc(w_loaded[slot], 16)

            names = {key: n for n, (key, *_) in enumerate(stream)}
            for n in range(6):
                load(n)
            sp.dma_start(pages[:, :], ins["page_table"].rearrange("(o a) b -> o (a b)", o=1)).then_inc(tables_in, 16)
            for a, name in enumerate(("distance", "ln_branches", "strict_mask")):
                tab(prompt_tab[:, a, :], name)
            tab(past_bias[:, :], "past_bias")
            tab(new_bias[:, :, :, :], "new_bias")
            tab(own_head[:, :], "own_head")
            tab(token_of[:, :, :], "token_of")
            tab(g_mix[:, :, :], "g_mix_cols")
            tab(sb_bias[:, :, :], "sb_bias_all")
            tab(sb_bias_rows[:, :], "sb_bias_rows")

            for L in range(LAYERS):
                if L == 1:
                    for c in range(6):
                        load(names[L, "proj", c])

                def unit_done(step):
                    return tp_at[L, "att"] + UNIT_AT[step] + 1

                def load_half(n, numbers):
                    if n >= 3:
                        sp.wait_ge(tp_full, unit_done(("key", (n - 3) // 2, 4 * ((n - 3) % 2) + 3)))
                    load_pages(sp, L, k_half[n % 3], "cache_sb_k", khalf_in[n % 3], numbers)

                sp.wait_ge(tables_in, 16 * 11)
                numbers = page_numbers(sp, 0, HALF)
                for s in range(NS):
                    if s == 0:
                        sp.wait_ge(*projection_used(L, 2))
                    load_half(2 * s, numbers)
                    numbers = page_numbers(sp, PAGES * s + HALF, HALF)
                    load_half(2 * s + 1, numbers)
                    if s < NS - 1:
                        numbers = page_numbers(sp, PAGES * (s + 1), HALF)
                    else:
                        numbers = page_numbers(sp, PAGES * VALUES_AT.index(1), PAGES)
                    if s:
                        sp.wait_ge(tp_full, unit_done(("key", s - 1, KTILES - 1)))
                    else:
                        sp.wait_ge(*projection_used(L, 3))
                        sp.wait_ge(*projection_used(L, 4))
                    load_window(sp, L, k_swa, "cache_swa_k", kswa_in, s)
                    if s == 0:
                        for c in range(2):
                            load(names[L, "wo", c])
                for s in range(NS):
                    if VALUES_AT[s] == 1:
                        last = LAST_THERE[s]
                        sp.wait_ge(*((d_o, out_unit(L, "value", last, 1) + 1) if last is not None
                                     else (tp_full, unit_done(("key", NS - 1, PAGES - 1)))))
                        load_pages(sp, L, v_sb[1], "cache_sb_v", vsb_in[1], numbers)
                        later = [x for x in range(s + 1, NS) if VALUES_AT[x] == 1]
                        if later:
                            numbers = page_numbers(sp, PAGES * later[0], PAGES)
                        sp.wait_ge(*((d_o, out_unit(L, "value", last, 0) + 1) if last is not None
                                     else (tp_full, unit_done(("key", NS - 1, KTILES - 1)))))
                        load_window(sp, L, v_swa[1], "cache_swa_v", vswa_in[1], s)
                sp.wait_ge(d_o, OUT_UNITS * (L + 1))
                sp.wait_ge(tp_full, tp_at[L, "merge"])
                for a, name in enumerate(("ln_mix_g", "ln_mix_b")):
                    sp.dma_start(ln_gb[:, a, :], ins[name][L].partition_broadcast(P)).then_inc(ln_in, 16)
                if L == 0:
                    first = names[L, "g", 0]
                    for n in range(first, names[L, "d", 0]):
                        load(n)
                    sp.wait_ge(ln_done, 2 * T * L + T)
                    for a, name in enumerate(("ln_ffn_g", "ln_ffn_b")):
                        sp.dma_start(ln_gb[:, a, :], ins[name][L].partition_broadcast(P)).then_inc(ln_in, 16)
                    for n in range(names[L, "d", 0], names[L, "d", 0] + len(DENSE_CHUNKS)):
                        load(n)

            def item_load(n, e, i):
                what, c = item_loads[n]
                s = item_slot(n)
                if n < NSLOT:
                    if i is None:
                        sp.wait_ge(*moe_used[s])
                    else:
                        sp.wait_ge(e_down, MOE_CHUNKS * i + (n + 1 - MOE_CHUNKS))
                elif n - NSLOT < 2 * MOE_CHUNKS:
                    v = n - NSLOT + 1
                    sp.wait_ge(e_gu, v if i is None else 2 * MOE_CHUNKS * i + v)
                if what == "d":
                    src, dst = wed[bass.ds(e, 1), :, FPC * c:FPC * (c + 1), :], slot_view(s, FPC)
                else:
                    src, dst = we["gu".index(what)][bass.ds(e, 1), :, :, c * CH:(c + 1) * CH], slot_view(s)
                sp.dma_start(dst, src.rearrange("o p k f -> (o p) k f")).then_inc(w_loaded[s], 16)

            sp.wait_ge(masked, 2 * HEADS * LAYERS)
            for dst, name in ((earlier, "earlier"), (ones, "ones"), (slot_number, "slot_number"),
                              (descending, "descending"), (is_token, "is_token"),
                              (item_number, "item_number"), (expert_number, "expert_number")):
                sp.dma_start(dst, ins[name]).then_inc(router_in, 16)
            sp.dma_start(w_router, ins["w_router"][0].rearrange("(k p) e -> p k e", p=P)).then_inc(router_in, 16)
            def item_expert(i):
                return sp.value_load(plan[0:1, bass.ds(i + 1, 1)], min_val=0, max_val=EXPERTS - 1)

            for n in range(ITEM_LOADS):
                item_load(n, 0, None)
                if n == NSLOT - 1:
                    sp.wait_ge(ln_done, 2 * T + T)
                    for a, name in enumerate(("ln_ffn_g", "ln_ffn_b")):
                        sp.dma_start(ln_gb[:, a, :], ins[name][1].partition_broadcast(P)).then_inc(ln_in, 16)
            sp.wait_ge(plan_ready, 1)
            count = sp.value_load(plan[0:1, 0:1], min_val=0, max_val=ITEMS)
            with sp.Fori(1, ITEMS) as i:
                with sp.If(i < count):
                    e = item_expert(i)
                    for n in range(ITEM_LOADS):
                        item_load(n, e, i)
            for t, dst in enumerate((y_p[0, 0:P, :], y_p[0, P:SEQ, :], y_s.rearrange("b t d -> (b t) d"))):
                sp.wait_ge(ln_done, 2 * T * LAYERS - T + t + 1)
                sp.dma_start(dst, x_tok[0:ROWS[t], t, :]).then_inc(stored_y, 16)
            sp.wait_ge(stored_y, 16 * T)

        @block.gpsimd
        def _(pool):
            copies = [(src[L].rearrange("b n h d -> b (n h d)"), dst[L].rearrange("b n h d -> b (n h d)"), b)
                      for L in range(LAYERS)
                      for src, dst in ((ins["cache_swa_k"], swk_s), (ins["cache_swa_v"], swv_s)) for b in range(NS)]

            def shift(done, value):
                src, dst, b = copies.pop(0)
                n = (PAST - DEC) * WID
                pool.wait_ge(done, value)
                pool.dma_start(dst[b, 0:n].rearrange("(a c) -> a c", a=240),
                               src[b, DEC * WID:PAST * WID].rearrange("(a c) -> a c", a=240)).then_inc(shifted, 16)

            for L in range(LAYERS):
                for n in range(6):
                    shift(proj_done, PROJ_UNITS * L + 7 + 2 * n)
                pool.wait_ge(proj_free, PROJ_UNITS * (L + 1))
                if L == 0:
                    pool.wait_ge(tables_in, 16 * 11)
                for g, (prompt, sample) in enumerate(((swk_p, None), (swv_p, None), (sbk_p, sbk_s), (sbv_p, sbv_s))):
                    for t in range(2):
                        pool.dma_start(prompt[L, 0, t * P:(t + 1) * P].rearrange("t h d -> t (h d)"), kv[:, t, g, :])\
                            .then_inc(stored_kv, 16)
                    if sample is not None:
                        pool.dma_start(sample[L].rearrange("b t h d -> (b t) (h d)"), kv[0:SAMPLE, 2, g, :])\
                            .then_inc(stored_kv, 16)
                here = [s for s in range(NS) if VALUES_AT[s] == 0]
                numbers = page_numbers(pool, 0, PAGES)
                for s in here:
                    if s:
                        pool.wait_ge(d_o, out_unit(L, "value", LAST_THERE[s], 1) + 1)
                    load_pages(pool, L, v_sb[0], "cache_sb_v", vsb_in[0], numbers)
                    if s != here[-1]:
                        numbers = page_numbers(pool, PAGES * here[here.index(s) + 1], PAGES)
                    if s:
                        pool.wait_ge(d_o, out_unit(L, "value", LAST_THERE[s], 0) + 1)
                    load_window(pool, L, v_swa[0], "cache_swa_v", vswa_in[0], s)
                    if s == 0:
                        for g, dst in enumerate((swk_s, swv_s)):
                            for b in range(NS):
                                pool.dma_start(dst[L, b, PAST - DEC:PAST].rearrange("t h d -> t (h d)"),
                                               kv[DEC * b:DEC * b + DEC, 2, g, :]).then_inc(stored_win, 16)
                if L == 0:
                    for n in range(11):
                        shift(gu_done, 4 * n + 1)
                    for n in range(len(DENSE_CHUNKS)):
                        shift(down_done, n + 1)
            while copies:
                shift(e_gu, 4 * len(copies))
            pool.wait_ge(stored_kv, 16 * LAYERS * 10)
            pool.wait_ge(stored_win, 16 * LAYERS * 2 * NS)
            pool.wait_ge(shifted, 16 * LAYERS * 2 * NS)

        @block.tensor
        def _(pe):
            def transpose_unit(u, parts, dst):
                if u >= 2:
                    pe.wait_ge(tp_free, u - 1)
                for o, src in zip(dst(bank(u % 2)), parts):
                    last = pe.transpose(o, src, ident[0:src.shape[0], 0:src.shape[0]])
                last.then_inc(tp_full, 1)

            def token_to_feature(u, src):
                for t, ready in enumerate(src):
                    ready(t)
                    r = ROWS[t]
                    for g in range(2):
                        transpose_unit(u + 2 * t + g, [src_tok[0:r, t, (4 * g + j) * P:(4 * g + j + 1) * P] for j in range(4)],
                                       lambda b: [b[:, j * r:(j + 1) * r] for j in range(4)])

            pe.wait_ge(ident_in, 16)
            pe.wait_ge(x_in, 48)
            src_tok = x_tok
            token_to_feature(0, [lambda t: None] * T)
            for L in range(LAYERS):
                pe.wait_ge(tp_free, tp_at[L, "k"])
                unit = PROJ_UNITS * L
                for c in range(6):
                    w = arrived(pe, (L, "proj", c))
                    for n in range(UNITS_Q if c % 3 == 0 else UNITS_KV):
                        if L == 1 and unit - PROJ_UNITS * L < 6:
                            pe.wait_ge(ffn_added, 6)
                        if unit >= 6:
                            pe.wait_ge(proj_free, unit - 5)
                        b = bank(2 + unit % 6)
                        for k in range(KD):
                            if c % 3 == 0:
                                last = pe.matmul(b[:, 0:TOK], w[:, k, n * P:(n + 1) * P], xTv[:, k, :],
                                                 start=k == 0, stop=k == KD - 1)
                            else:
                                last = pe.matmul(b[0:ROWS[n], :], xTv[:, k, n * P:n * P + ROWS[n]], w[:, k, :],
                                                 start=k == 0, stop=k == KD - 1)
                        last.then_inc(proj_done, 1)
                        unit += 1
                pe.wait_ge(proj_free, PROJ_UNITS * (L + 1))
                for m in range(2):
                    for t in range(T):
                        r = ROWS[t]
                        transpose_unit(tp_at[L, "k"] + T * m + t, [kv[0:r, t, 2 * m, j * P:(j + 1) * P] for j in range(4)],
                                       lambda b: [b[:, j * r:(j + 1) * r] for j in range(4)])
                pe.wait_ge(tp_free, tp_at[L, "att"])
                n0, B, units = 2 * HEADS * L, NS * L, tp_at[L, "att"]

                def bank6_free(scores, outputs):
                    if n0 + scores:
                        pe.wait_ge(masked, n0 + scores)
                    if n0 + outputs:
                        pe.wait_ge(o_copied, n0 + outputs)

                def head_scores(n):
                    m, h = HEAD_ORDER[n]
                    rows = slice(HD * (h % 2), HD * (h % 2) + HD)
                    k = HP * m + h // 2
                    bank6_free(n, before("probs", ("score", n)))
                    b = bank(6)
                    pe.matmul(b[:, 0:P], qT[rows, k, 0:P], kT[rows, k, 0:P], start=True, stop=True)
                    pe.matmul(b[:, P:3 * P], qT[rows, k, P:SEQ], kT[rows, k, 0:SEQ], start=True, stop=True)\
                        .then_inc(scored, 1)

                def head_values(n):
                    m, h = HEAD_ORDER[n]
                    u = units + UNIT_AT["probs", n]
                    pe.wait_ge(prob_ready, n0 + n + 1)
                    transpose_unit(u, [head_es[n % 2][:, j * P:(j + 1) * P] for j in range(3)],
                                   lambda b: [b[:, j * P:(j + 1) * P] for j in range(3)])
                    pe.wait_ge(tp_free, u + 1)
                    bank6_free(before("score", ("probs", n)), n)
                    o = bank(6)[:, 384:512]
                    v = [kv[:, t, 2 * m + 1, h * HD:(h + 1) * HD] for t in range(2)]
                    pe.matmul(o[:, 0:HD], head_pT[:, 0:P], v[0], start=True, stop=True)
                    pe.matmul(o[:, HD:2 * HD], head_pT[:, P:2 * P], v[0], start=True, stop=False)
                    pe.matmul(o[:, HD:2 * HD], head_pT[:, 2 * P:3 * P], v[1], start=False, stop=True).then_inc(pv_done, 1)

                def keys_scored(s, j):
                    pe.wait_ge(tp_free, units + UNIT_AT["key", s, j] + 1)
                    m = 1 if j < PAGES else 0
                    at = 2 * CH + j * P if j < PAGES else 4 * CH + (j - PAGES) * P
                    rows = slice(SAMPLE * (s % GSEQ), SAMPLE * (s % GSEQ) + SAMPLE)
                    stage = kstage[:, (KTILES * s + j) % 4, :]
                    for a in range(HP):
                        last = pe.matmul(psum[rows, at:at + P], qblk[s % 2][:, m, a * SAMPLE:(a + 1) * SAMPLE],
                                         stage[:, a * P:(a + 1) * P], start=a == 0, stop=a == HP - 1)
                    last.then_inc(d_scored, 1)

                def new_keys_scored(s):
                    rows = slice(SAMPLE * (s % GSEQ), SAMPLE * (s % GSEQ) + SAMPLE)
                    for m in (1, 0):
                        at = 5 * CH + P + SAMPLE * m
                        for a in range(HP):
                            last = pe.matmul(psum[rows, at:at + SAMPLE], qblk[s % 2][:, m, a * SAMPLE:(a + 1) * SAMPLE],
                                             kT[:, HP * m + a, SEQ:TOK], start=a == 0, stop=a == HP - 1)
                    last.then_inc(d_scored, 1)

                def key_tile(s, j):
                    g = s // GSEQ
                    if j == 0:
                        pe.wait_ge(qblk_ready, B + s + 1)
                    if j in (0, PAGES // 2):
                        n = 2 * s + j // 4
                        pe.wait_ge(khalf_in[n % 3], 64 * (KHALF_USES[n % 3] * L + n // 3 + 1))
                    if j == PAGES:
                        pe.wait_ge(kswa_in, 16 * 5 * (B + s + 1))
                    src = k_half[(2 * s + j // 4) % 3][:, j % 4, :] if j < PAGES else k_swa[:, j - PAGES, :]
                    transpose_unit(units + UNIT_AT["key", s, j], [src[:, a * P:(a + 1) * P] for a in range(HP)],
                                   lambda b: [b[:, a * P:(a + 1) * P] for a in range(HP)])
                    if j == 1 and s % GSEQ == 0 and (g or L):
                        pe.wait_ge(sb_exped, 2 * (GROUPS * L + g))
                    if j == PAGES + 1 and s % GSEQ == 0 and (g or L):
                        pe.wait_ge(swa_taken, GROUPS * L + g)
                    if j:
                        keys_scored(s, j - 1)
                    if j == KTILES - 1:
                        keys_scored(s, j)
                        new_keys_scored(s)

                def turn(g, m):
                    u = units + UNIT_AT["turn", g, m]
                    pe.wait_ge(sb_weights if m else swa_weights, GROUPS * L + g + 1)
                    src = probs if m else swa_s
                    for a in range(2 if m else 1):
                        transpose_unit(u + a, [src[:, (4 * a + j) * P:(4 * a + j + 1) * P] for j in range(4)],
                                       lambda b: [b[:, j * P:(j + 1) * P] for j in range(4)])
                    if m:
                        transpose_unit(u + 2, [probs[:, PAST:PAST + SAMPLE]], lambda b: [b[0:SAMPLE, 0:P]])
                    else:
                        transpose_unit(u + 1, [swa_s[:, 4 * P:5 * P], swa_s[:, SWA_KEYS:SWA_KEYS + SAMPLE]],
                                       lambda b: [b[:, 0:P], b[0:SAMPLE, P:2 * P]])

                def out_quadrant(n):
                    if n >= 4:
                        pe.wait_ge(d_ocopied, n - 3)
                    return bank(7)[SAMPLE * (n % 4):SAMPLE * (n % 4) + SAMPLE, :]

                def value(s, m):
                    if s % GSEQ == 0:
                        pe.wait_ge(tp_free, units + UNIT_AT["turn", s // GSEQ, m] + 2 + m)
                    cols = slice(SAMPLE * (s % GSEQ), SAMPLE * (s % GSEQ) + SAMPLE)
                    where = VALUES_AT[s]
                    uses = VALUES_AT.count(where) * L + VALUES_AT[:s + 1].count(where)
                    if m:
                        count, v, pT, vnew = PAGES, v_sb[where], sb_probT, kv[0:SAMPLE, 2, 3, :]
                        pe.wait_ge(vsb_in[where], 16 * PAGES * uses)
                    else:
                        count, v, pT, vnew = SWA_TILES, v_swa[where], swa_probT, kv[0:SAMPLE, 2, 1, :]
                        pe.wait_ge(vswa_in[where], 16 * 5 * uses)
                    o = out_quadrant(out_unit(L, "value", s, m))
                    for j in range(count):
                        pe.matmul(o, pT[:, j, cols], v[:, j, :], start=j == 0, stop=False)
                    pe.matmul(o, pT[0:SAMPLE, count, cols], vnew, start=False, stop=True).then_inc(d_o, 1)

                def select(g):
                    n = out_unit(L, "select", g)
                    pe.wait_ge(d_ocopied, n)
                    for m in range(2):
                        pe.matmul(out_quadrant(n + m), token_of[:, g, :], own_o[:, m, :], start=True, stop=True)\
                          .then_inc(d_o, 1)

                for step in ORDER:
                    if step[0] == "score":
                        head_scores(step[1])
                    elif step[0] == "probs":
                        head_values(step[1])
                    elif step[0] == "key":
                        key_tile(step[1], step[2])
                    elif step[0] == "turn":
                        turn(step[1], step[2])
                    elif step[0] == "value":
                        value(step[1], step[2])
                    elif step[0] == "select":
                        select(step[1])
                pe.wait_ge(d_ocopied, OUT_UNITS * (L + 1))

                src_tok = o_or_acc
                token_to_feature(tp_at[L, "merge"], [lambda t: pe.wait_ge(rms_scaled, T * L + t + 1)] * T)
                pe.wait_ge(tp_free, tp_at[L, "mix"])
                w_o = [arrived(pe, (L, "wo", c)) for c in range(2)]
                for t in range(T):
                    for c, w in enumerate(w_o):
                        b = bank(2 + 2 * t + c)
                        for k in range(KD):
                            last = pe.matmul(b[0:ROWS[t], :], qT[:, k, t * P:t * P + ROWS[t]], w[:, k, :],
                                             start=k == 0, stop=k == KD - 1)
                        last.then_inc(wo_done, 1)
                src_tok = x_tok
                token_to_feature(tp_at[L, "mix"], [lambda t: pe.wait_ge(ln_done, 2 * T * L + t + 1)] * T)
                pe.wait_ge(tp_free, tp_at[L, "mix"] + 6)
                pe.wait_ge(wo_added, 6 * (L + 1))
                if L == 0:
                    for c, m in DENSE_CHUNKS:
                        wg, wu = arrived(pe, (L, "g", c)), arrived(pe, (L, "u", c))
                        for j in range(m):
                            f = FPC * c + j
                            if f >= 2:
                                pe.wait_ge(gu_free, f - 1)
                            for a, w in enumerate((wg, wu)):
                                for k in range(KD):
                                    last = pe.matmul(bank(2 + 2 * (f % 2) + a)[:, 0:TOK], w[:, k, j * P:(j + 1) * P],
                                                     xTv[:, k, :], start=k == 0, stop=k == KD - 1)
                                last.then_inc(gu_done, 1)
                    pe.wait_ge(gu_free, DENSE_F)

                    def down(f, w, t):
                        for h in range(2):
                            last = pe.matmul(bank(2 + 2 * t + h)[0:ROWS[t], :], hT[:, f, t * P:t * P + ROWS[t]],
                                             w[:, f % FPC, h * CH:(h + 1) * CH], start=f == 0, stop=f == DENSE_F - 1)
                        return last

                    for c, m in DENSE_CHUNKS[:DOWN_WHOLE]:
                        w = arrived(pe, (L, "d", c))
                        for j in range(m):
                            for t in range(T):
                                last = down(FPC * c + j, w, t)
                        last.then_inc(down_done, 1)
                    rest = [(c, m, arrived(pe, (L, "d", c))) for c, m in DENSE_CHUNKS[DOWN_WHOLE:]]
                    for t in range(T):
                        for c, m, w in rest:
                            for j in range(m):
                                last = down(FPC * c + j, w, t)
                        last.then_inc(down_done, 1)
                    token_to_feature(tp_at[L, "ffn"], [lambda t: pe.wait_ge(ln_done, T + t + 1)] * T)

            pe.wait_ge(router_in, 16 * 8)
            for t in range(T):
                for k in range(KD):
                    last = pe.matmul(bank(2)[0:ROWS[t], t * EXPERTS:(t + 1) * EXPERTS], xTv[:, k, t * P:t * P + ROWS[t]],
                                     w_router[:, k, :], start=k == 0, stop=k == KD - 1)
            last.then_inc(logits_done, 1)
            pe.wait_ge(chosen_ready, 1)
            for t in range(T):
                for s in range(t + 1):
                    pe.matmul(bank(3)[:, t * EXPERTS:(t + 1) * EXPERTS], earlier if s == t else ones, chosen[:, s, :],
                              start=s == 0, stop=s == t)
            for s in range(T):
                last = pe.matmul(bank(3)[:, T * EXPERTS:(T + 1) * EXPERTS], ones, chosen[:, s, :],
                                 start=s == 0, stop=s == T - 1)
            last.then_inc(ranks_done, 1)

            def gather(value):
                pe.wait_ge(pick_ready, value)
                for g in range(2):
                    for j in range(4):
                        k = 4 * g + j
                        for t in range(T):
                            last = pe.matmul(bank(g)[:, j * ITEM:(j + 1) * ITEM],
                                             x_tok[0:ROWS[t], t, k * P:(k + 1) * P], pick[0:ROWS[t], t, :],
                                             start=t == 0, stop=t == T - 1)
                    last.then_inc(gathered, 1)

            def item(i):
                pe.wait_ge(gather_copied, 2 * i + 2)
                for c in range(MOE_CHUNKS):
                    b = 2 + 2 * (c % 2)
                    if c >= 2:
                        pe.wait_ge(e_h, MOE_CHUNKS * i + (c - 1))
                    for a in range(2):
                        item_loaded(pe, 2 * c + a, i)
                        w = slot_view(item_slot(2 * c + a))
                        for j in range(FPC):
                            for k in range(KD):
                                last = pe.matmul(bank(b + a)[:, j * ITEM:(j + 1) * ITEM],
                                                 w[:, k, j * P:(j + 1) * P], xg[:, k, :], start=k == 0, stop=k == KD - 1)
                        last.then_inc(e_gu, 1)
                pe.wait_ge(added, 6 * i + 6)
                for t in range(T):
                    last = pe.transpose(bank(0)[:, t * P:t * P + ROWS[t]], pick[0:ROWS[t], t, :],
                                        ident[0:ROWS[t], 0:ROWS[t]])
                last.then_inc(pick_turned, 1)
                pe.wait_ge(e_h, MOE_CHUNKS * i + (MOE_CHUNKS - 1))
                for c in range(MOE_CHUNKS):
                    if c == MOE_CHUNKS - 1:
                        pe.wait_ge(e_h, MOE_CHUNKS * i + MOE_CHUNKS)
                    item_loaded(pe, 2 * MOE_CHUNKS + c, i)
                    w = slot_view(item_slot(2 * MOE_CHUNKS + c), FPC)
                    for j in range(FPC):
                        f = FPC * c + j
                        for h in range(2):
                            last = pe.matmul(bank(6 + h), hE[:, f, :], w[:, j, h * CH:(h + 1) * CH],
                                             start=f == 0, stop=f == MOE_F - 1)
                    last.then_inc(e_down, 1)
                pe.wait_ge(pickT_copied, i + 1)
                gather(i + 2)
                for n in range(2 * T):
                    t, h = divmod(n, 2)
                    if n == 0:
                        pe.wait_ge(y_copied, i + 1)
                    elif n == 2:
                        pe.wait_ge(gather_copied, 2 * i + 4)
                    elif n >= 4:
                        pe.wait_ge(added, 6 * i + (n + 3))
                    pe.matmul(bank((6, 7, 0, 1)[n % 4])[0:ROWS[t], :], pickT[:, t * P:t * P + ROWS[t]],
                              y_item[:, h * CH:(h + 1) * CH], start=True, stop=True).then_inc(combined, 1)

            gather(1)
            pe.wait_ge(plan_ready, 1)
            count = pe.value_load(plan[0:1, 0:1], min_val=0, max_val=ITEMS)
            with pe.Fori(0, ITEMS) as i:
                with pe.If(i < count):
                    item(i)

        @block.scalar
        def _(act):
            st = Steps(act, act_step)

            def copy_unit(u, dst, src):
                act.wait_ge(tp_full, u + 1)
                act.copy(dst, src(bank(u % 2))).then_inc(tp_free, 1)

            def to_feature(u, dst, gains=None):
                for t in range(T):
                    r = ROWS[t]
                    for g in range(2):
                        n = u + 2 * t + g
                        src = bank(n % 2)[:, 0:4 * r].rearrange("p (j r) -> p j r", j=4)
                        out = dst[:, 4 * g:4 * g + 4, t * P:t * P + r]
                        act.wait_ge(tp_full, n + 1)
                        if gains is None:
                            act.copy(out, src).then_inc(tp_free, 1)
                        else:
                            for j in range(4):
                                last = act.activation(out[:, j, :], src[:, j, :], ACT.Copy, scale=gains(4 * g + j))
                            last.then_inc(tp_free, 1)

            to_feature(0, xTv)
            for L in range(LAYERS):
                for m in range(2):
                    for t in range(T):
                        r = ROWS[t]
                        copy_unit(tp_at[L, "k"] + T * m + t, kT[:, HP * m:HP * m + HP, t * P:t * P + r],
                                  lambda b: b[:, 0:4 * r].rearrange("p (j r) -> p j r", j=4))
                n0, B, units = 2 * HEADS * L, NS * L, tp_at[L, "att"]
                if L == 0:
                    act.wait_ge(tables_in, 16 * 11)

                def head_exponentials(n):
                    m, h = HEAD_ORDER[n]
                    head_e, stat = head_es[n % 2], stats[:, n % 2, :]
                    act.wait_ge(masked, n0 + n + 1)
                    if m == 0:
                        for q, cols in enumerate((slice(0, P), slice(P, 3 * P))):
                            last = act.activation(head_e[:, cols], head_e[:, cols], ACT.Exp, bias=stat[:, q:q + 1],
                                                  accum_out=stat[:, 2 + q:3 + q])
                    else:
                        last = act.activation(head_e, head_e, ACT.Exp, bias=sb_bias[:, L, h:h + 1])
                    last.then_inc(expd, 1)

                def weigh(g):
                    act.wait_ge(d_scored, (KTILES + 1) * (B + GSEQ * (g + 1)))
                    act.activation(probs[:, 0:PAST], bank(2, 2), ACT.Exp, bias=sb_bias_rows[:, L:L + 1], scale=SCALE)\
                        .then_inc(sb_exped, 1)
                    act.wait_ge(sb_new_masked, GROUPS * L + g + 1)
                    act.activation(probs[:, PAST:PAST + SAMPLE], probs[:, PAST:PAST + SAMPLE], ACT.Exp,
                                   bias=sb_bias_rows[:, L:L + 1]).then_inc(sb_exped, 1)
                    act.wait_ge(swa_taken, GROUPS * L + g + 1)
                    act.activation(swa_s, swa_s, ACT.Exp, bias=dstat[:, 0:1], accum_out=dstat[:, 1:2]).then_inc(swa_exped, 1)

                for step in ORDER:
                    u = units + UNIT_AT[step]
                    if step[0] == "score":
                        head_exponentials(step[1])
                    elif step[0] == "probs":
                        n = step[1]
                        if n0 + n:
                            act.wait_ge(pv_done, n0 + n)
                        copy_unit(u, head_pT, lambda b: b[:, 0:3 * P])
                    elif step[0] == "key":
                        t = KTILES * step[1] + step[2]
                        if t >= 4:
                            act.wait_ge(d_scored, (KTILES + 1) * B + t - 3 + (t - 4) // KTILES)
                        copy_unit(u, kstage[:, t % 4, :], lambda b: b)
                    elif step[0] == "weigh":
                        weigh(step[1])
                    elif step[0] == "turn":
                        g, m = step[1:]
                        if g or L:
                            act.wait_ge(d_o, out_unit(L, *step))
                        if m:
                            for a in range(2):
                                copy_unit(u + a, sb_probT[:, 4 * a:4 * a + 4, :], lambda b: b.rearrange("p (j q) -> p j q", j=4))
                            copy_unit(u + 2, sb_probT[0:SAMPLE, 8, :], lambda b: b[0:SAMPLE, 0:P])
                        else:
                            copy_unit(u, swa_probT[:, 0:4, :], lambda b: b.rearrange("p (j q) -> p j q", j=4))
                            act.wait_ge(tp_full, u + 2)
                            b = bank((u + 1) % 2)
                            act.copy(swa_probT[:, 4, :], b[:, 0:P])
                            act.copy(swa_probT[0:SAMPLE, 5, :], b[0:SAMPLE, P:2 * P]).then_inc(tp_free, 1)
                for t in range(T):
                    r = ROWS[t]
                    if t == 0:
                        act.wait_ge(o_copied, n0 + 2 * HEADS)
                    if t == 2:
                        act.wait_ge(d_ocopied, OUT_UNITS * (L + 1))
                    for m in range(2):
                        st.did(act.activation(mean_sq_out[0:r, :], o_or_acc[0:r, t, m * WID:(m + 1) * WID], ACT.Square,
                                              accum_out=norm[0:r, t, m:m + 1]))
                    act.wait_ge(sq_done, T * L + t + 1)
                    act.activation(norm[0:r, t, 4:6], norm[0:r, t, 2:4], ACT.Sqrt).then_inc(rms_root, 1)
                to_feature(tp_at[L, "merge"], qT, lambda k: g_mix[:, L, k:k + 1])

                def ln_roots(base):
                    for t in range(T):
                        act.wait_ge(var_ready, base + t + 1)
                        act.activation(norm[0:ROWS[t], t, 23:24], norm[0:ROWS[t], t, 22:23], ACT.Sqrt).then_inc(ln_root, 1)

                ln_roots(2 * T * L)
                to_feature(tp_at[L, "mix"], xTv)
                if L == 0:
                    for f in range(DENSE_F):
                        act.wait_ge(gu_done, 2 * f + 1)
                        if f >= 2:
                            act.wait_ge(gu_free, f - 1)
                        act.activation(silu_r[f % 2][:, 0:TOK], bank(2 + 2 * (f % 2))[:, 0:TOK], ACT.Exp, scale=-1.0)\
                            .then_inc(gu_exp, 1)
                    ln_roots(T)
                    to_feature(tp_at[L, "ffn"], xTv)
            act.wait_ge(logits_copied, 1)
            act.activation(vals[:, :, 3:4], vals[:, :, 2:3], ACT.Exp).then_inc(gate_exped, 1)

            def copy_gathered(i):
                for g in range(2):
                    act.wait_ge(gathered, 2 * i + (g + 1))
                    act.copy(xg[:, 4 * g:4 * g + 4, :], bank(g).rearrange("p (k s) -> p k s", k=4)).then_inc(gather_copied, 1)

            copy_gathered(0)
            act.wait_ge(plan_ready, 1)
            count = act.value_load(plan[0:1, 0:1], min_val=0, max_val=ITEMS)
            with act.Fori(0, ITEMS) as i:
                with act.If(i < count):
                    for c in range(MOE_CHUNKS):
                        act.wait_ge(e_gu, 2 * MOE_CHUNKS * i + (2 * c + 1))
                        if c >= 2:
                            act.wait_ge(e_h, MOE_CHUNKS * i + (c - 1))
                        act.activation(silu_r[c % 2], bank(2 + 2 * (c % 2)), ACT.Exp, scale=-1.0).then_inc(e_exp, 1)
                    act.wait_ge(pick_turned, i + 1)
                    act.copy(pickT, bank(0)[:, 0:TOK]).then_inc(pickT_copied, 1)
                    act.wait_ge(e_down, MOE_CHUNKS * i + MOE_CHUNKS)
                    act.copy(y_item, psum[:, 6 * CH:8 * CH]).then_inc(y_copied, 1)
                    copy_gathered(i + 1)
            for t in range(T):
                act.wait_ge(var_ready, 3 * T + t + 1)
                act.activation(norm[0:ROWS[t], t, 23:24], norm[0:ROWS[t], t, 22:23], ACT.Sqrt).then_inc(ln_root, 1)

        @block.vector
        def _(v):
            st = Steps(v, dve_step)

            def layer_norm(t, base, gb_in, st):
                r = ROWS[t]
                x = x_tok[0:r, t, :]
                n = norm[0:r, t, :]
                for h in range(2):
                    st.did(v.bn_stats(n[:, 6 + 6 * h:12 + 6 * h], x[:, h * CH:(h + 1) * CH]))
                st.did(v.bn_aggr(n[:, 20:22], n[:, 6:18]))
                v.tensor_scalar(n[:, 22:23], n[:, 21:22], LN_EPS, None, ALU.add).then_inc(var_ready, 1)
                v.wait_ge(ln_in, gb_in)
                st.go(v.scalar_tensor_tensor(x, x, n[:, 20:21], ln_gb[0:r, 0, :], ALU.subtract, ALU.mult))
                v.wait_ge(ln_root, base + t + 1)
                st.did(v.reciprocal(n[:, 19:20], n[:, 23:24]))
                v.scalar_tensor_tensor(x, x, n[:, 19:20], ln_gb[0:r, 1, :], ALU.mult, ALU.add).then_inc(ln_done, 1)

            for L in range(LAYERS):
                unit = PROJ_UNITS * L
                for c in range(6):
                    for n in range(UNITS_Q if c % 3 == 0 else UNITS_KV):
                        b = bank(2 + unit % 6)
                        if c % 3 == 0:
                            v.wait_ge(proj_done, unit + 1)
                            v.tensor_copy(qT[:, HP * (c // 3) + n, :], b[:, 0:TOK]).then_inc(proj_free, 1)
                        else:
                            v.wait_ge(proj_done, unit + 1)
                            v.tensor_copy(kv[0:ROWS[n], n, 2 * (c // 3) + c % 3 - 1, :], b[0:ROWS[n], :]).then_inc(proj_free, 1)
                        unit += 1
                n0, B, W = 2 * HEADS * L, NS * L, GROUPS * L
                if L == 0:
                    v.wait_ge(tables_in, 16 * 11)
                v.wait_ge(proj_free, PROJ_UNITS * (L + 1))
                for q in qblk:
                    st.did(v.memset(q, 0.0))

                def queries(s):
                    if s >= 2:
                        v.wait_ge(d_scored, (KTILES + 1) * (B + s - 1))
                    for m in range(2):
                        for u in range(2):
                            rows = slice(HD * u, HD * u + HD)
                            dst = qblk[s % 2][rows, m, 4 * u:4 * u + 124].rearrange("p (a x) -> p a x", x=4)[:, ::10, :]
                            last = v.tensor_copy(dst, qT[rows, HP * m:HP * m + HP, SEQ + DEC * s:SEQ + DEC * (s + 1)])
                            if (m, u) == (1, 1):
                                last.then_inc(qblk_ready, 1)
                            else:
                                st.go(last)

                def mask(n):
                    m, h = HEAD_ORDER[n]
                    e, tmp, stat = head_es[n % 2], head_keep[:, 0:3 * P], stats[:, n % 2, :]
                    if n0 + n >= 2:
                        v.wait_ge(pv_done, n0 + n - 1)
                    if n0 + n:
                        v.wait_ge(prob_ready, n0 + n)
                    if m == 0:
                        st.did(v.scalar_tensor_tensor(tmp, prompt_tab[:, 0, :], -(2.0 ** (-8.0 * (h + 1) / HEADS)),
                                                      prompt_tab[:, 1, :], ALU.mult, ALU.add))
                    v.wait_ge(scored, n0 + n + 1)
                    score = v.scalar_tensor_tensor(e, bank(6)[:, 0:384], SCALE,
                                                   tmp if m == 0 else prompt_tab[:, 2, :], ALU.mult, ALU.add)
                    if m == 0:
                        st.did(score)
                        st.go(v.reduce_max(stat[:, 0:1], e[:, 0:P], AX, negate=True))
                        v.reduce_max(stat[:, 1:2], e[:, P:3 * P], AX, negate=True).then_inc(masked, 1)
                    else:
                        score.then_inc(masked, 1)

                def head_weights(n):
                    m, h = HEAD_ORDER[n]
                    e, keep, stat = head_es[n % 2], head_keep, stats[:, n % 2, :]
                    v.wait_ge(expd, n0 + n + 1)
                    if m == 0:
                        v.reciprocal(stat[:, 4:6], stat[:, 2:4]).then_inc(prob_ready, 1)
                        return
                    halves = ((slice(0, P), slice(0, P), slice(1, P + 1)),
                              (slice(P, 3 * P), slice(P + 1, 3 * P + 1), slice(P + 2, 3 * P + 2)))
                    st.go(v.memset(keep[:, P:P + 1], 1.0))
                    st.go(v.memset(keep[:, 3 * P + 1:3 * P + 2], 1.0))
                    for cols, at, _ in halves:
                        last = v.tensor_scalar(keep[:, at], e[:, cols], BIG, 1.0, ALU.min, ALU.add)
                        st.go(last) if cols.start == 0 else st.did(last)
                    st.did(v.reciprocal(keep, keep))
                    for cols, at, _ in halves:
                        last = v.scalar_tensor_tensor(e[:, cols], e[:, cols], BIG, keep[:, at], ALU.min, ALU.mult)
                        st.go(last) if cols.start == 0 else st.did(last)
                    for cols, at, _ in halves:
                        k = keep[:, at]
                        last = v.tensor_tensor_scan(k[:, ::-1], k[:, ::-1], k[:, ::-1], 1.0, ALU.mult, ALU.min)
                        st.go(last) if cols.start == 0 else st.did(last)
                    cols, _, later = halves[0]
                    st.go(v.tensor_tensor(e[:, cols], e[:, cols], keep[:, later], ALU.mult))
                    cols, _, later = halves[1]
                    v.tensor_tensor(e[:, cols], e[:, cols], keep[:, later], ALU.mult).then_inc(prob_ready, 1)

                def take(n):
                    m, h = HEAD_ORDER[n]
                    v.wait_ge(pv_done, n0 + n + 1)
                    b, stat = bank(6)[:, 384:512], stats[:, n % 2, :]
                    o = o_or_acc[:, 0:2, m * WID + h * HD:m * WID + (h + 1) * HD]
                    if m == 0:
                        st.go(v.tensor_scalar(o[:, 0, :], b[:, 0:HD], stat[:, 4:5], None, ALU.mult))
                        v.tensor_scalar(o[:, 1, :], b[:, HD:2 * HD], stat[:, 5:6], None, ALU.mult).then_inc(o_copied, 1)
                    else:
                        v.tensor_copy(o, b.rearrange("p (t d) -> p t d", t=2)).then_inc(o_copied, 1)
                    v.wait_ge(o_copied, n0 + n + 1)

                def weigh(g):
                    v.wait_ge(d_scored, (KTILES + 1) * (B + GSEQ * (g + 1)))
                    v.scalar_tensor_tensor(probs[:, PAST:PAST + SAMPLE], bank(5)[:, P + SAMPLE:P + 2 * SAMPLE], SCALE,
                                           new_bias[:, 1, g, :], ALU.mult, ALU.add).then_inc(sb_new_masked, 1)
                    st.go(v.scalar_tensor_tensor(swa_s[:, 0:SWA_KEYS], psum[:, 4 * CH:4 * CH + SWA_KEYS], SCALE,
                                                 past_bias[:, :], ALU.mult, ALU.add))
                    st.did(v.scalar_tensor_tensor(swa_s[:, SWA_KEYS:], bank(5)[:, P:P + SAMPLE], SCALE,
                                                  new_bias[:, 0, g, :], ALU.mult, ALU.add))
                    v.reduce_max(dstat[:, 0:1], swa_s, AX, negate=True).then_inc(swa_taken, 1)
                    v.wait_ge(sb_exped, 2 * (W + g + 1))
                    e, keep = probs, keeps[:, 0:PAST + SAMPLE]
                    st.go(v.memset(keeps[:, PAST + SAMPLE:], 1.0))
                    st.go(v.tensor_scalar(keep, e, BIG, 1.0, ALU.min, ALU.add))
                    v.wait_ge(swa_exped, W + g + 1)
                    st.did(v.reciprocal(dstat[:, 2:3], dstat[:, 1:2]))
                    v.tensor_scalar(swa_s, swa_s, dstat[:, 2:3], None, ALU.mult).then_inc(swa_weights, 1)
                    st.did(v.reciprocal(keep, keep))
                    st.did(v.scalar_tensor_tensor(e, e, BIG, keep, ALU.min, ALU.mult))
                    st.did(v.tensor_tensor_scan(keep[:, ::-1], keep[:, ::-1], keep[:, ::-1], 1.0, ALU.mult, ALU.min))
                    v.tensor_tensor(e, e, keeps[:, 1:], ALU.mult).then_inc(sb_weights, 1)
                    v.wait_ge(sb_weights, W + g + 1)

                def quadrant(n):
                    v.wait_ge(d_o, n + 1)
                    return bank(7)[SAMPLE * (n % 4):SAMPLE * (n % 4) + SAMPLE, :]

                def take_values(s, m):
                    rows = slice(SAMPLE * (s % GSEQ), SAMPLE * (s % GSEQ) + SAMPLE)
                    o = quadrant(out_unit(L, "value", s, m))
                    v.tensor_tensor(own_o[rows, m, :].rearrange("p (h d) -> p h d", h=HEADS),
                                    o.rearrange("p (h d) -> p h d", h=HEADS),
                                    own_head[rows, :, None].to_broadcast([SAMPLE, HEADS, HD]), ALU.mult)\
                     .then_inc(d_ocopied, 1)

                def select(g):
                    for m in range(2):
                        o = quadrant(out_unit(L, "select", g) + m)
                        dst = o_or_acc[0:SAMPLE, 2, m * WID:(m + 1) * WID]
                        if g == 0:
                            v.tensor_copy(dst, o).then_inc(d_ocopied, 1)
                        else:
                            v.tensor_tensor(dst, dst, o, ALU.add).then_inc(d_ocopied, 1)

                queries(0)
                for step in ORDER:
                    if step[0] == "score":
                        mask(step[1])
                        head_weights(step[1])
                    elif step[0] == "probs":
                        take(step[1])
                    elif step[0] == "key" and step[2] == 0 and step[1] + 1 < NS:
                        queries(step[1] + 1)
                    elif step[0] == "weigh":
                        weigh(step[1])
                    elif step[0] == "value":
                        take_values(step[1], step[2])
                    elif step[0] == "select":
                        select(step[1])
                for t in range(T):
                    r = ROWS[t]
                    n = norm[0:r, t, :]
                    v.wait_ge(act_step, 2 * T * L + 2 * (t + 1))
                    v.tensor_scalar(n[:, 2:4], n[:, 0:2], 1.0 / WID, RMS_EPS, ALU.mult, ALU.add).then_inc(sq_done, 1)
                    v.wait_ge(rms_root, T * L + t + 1)
                    st.did(v.reciprocal(n[:, 18:20], n[:, 4:6]))
                    for m in range(2):
                        o = o_or_acc[0:r, t, m * WID:(m + 1) * WID]
                        last = v.tensor_scalar(o, o, n[:, 18 + m:19 + m], None, ALU.mult)
                        if m == 0:
                            st.go(last)
                        else:
                            last.then_inc(rms_scaled, 1)
                for t in range(T):
                    for c in range(2):
                        r = ROWS[t]
                        v.wait_ge(wo_done, 2 * T * L + 2 * t + c + 1)
                        x = x_tok[0:r, t, c * CH:(c + 1) * CH]
                        v.scalar_tensor_tensor(x, x, ALPHA, bank(2 + 2 * t + c)[0:r, :], ALU.mult, ALU.add).then_inc(wo_added, 1)
                    v.wait_ge(wo_added, 2 * T * L + 2 * t + 2)
                    layer_norm(t, 2 * T * L, 64 * L + 32, st)
                if L == 0:
                    v.wait_ge(stored_kv, 160 * (L + 1))
                    v.wait_ge(stored_win, 16 * 2 * NS * (L + 1))
                    for f in range(DENSE_F):
                        a = 2 + 2 * (f % 2)
                        rr, tt = silu_r[f % 2][:, 0:TOK], silu_t[f % 2][:, 0:TOK]
                        v.wait_ge(gu_exp, f + 1)
                        st.did(v.tensor_scalar(rr, rr, BIG, 1.0, ALU.min, ALU.add))
                        st.did(v.reciprocal(rr, rr))
                        st.did(v.tensor_tensor(tt, rr, bank(a)[:, 0:TOK], ALU.mult))
                        v.wait_ge(gu_done, 2 * f + 2)
                        v.tensor_tensor(hT[:, f, :], tt, bank(a + 1)[:, 0:TOK], ALU.mult).then_inc(gu_free, 1)
                    for t in range(T):
                        r = ROWS[t]
                        v.wait_ge(down_done, DOWN_WHOLE + t + 1)
                        v.scalar_tensor_tensor(x_tok[0:r, t, :], x_tok[0:r, t, :], ALPHA,
                                               psum[0:r, (2 + 2 * t) * CH:(4 + 2 * t) * CH], ALU.mult, ALU.add)\
                            .then_inc(ffn_added, 2)
                        v.wait_ge(ffn_added, 2 * t + 2)
                        layer_norm(t, T, 64, st)
            v.wait_ge(router_in, 16 * 8)
            st.did(v.memset(logit, 0.0))
            v.wait_ge(tp_free, tp_at[LAYERS - 1, "mix"])
            v.memset(o_or_acc[:, :, :], 0.0).then_inc(added, 6)
            v.wait_ge(added, 6)
            v.wait_ge(stored_kv, 160 * LAYERS)
            v.wait_ge(stored_win, 16 * 2 * NS * LAYERS)

            def make_pick(rank, steps):
                for t in range(T):
                    last = v.tensor_scalar(pick[0:ROWS[t], t, :], slot_number[0:ROWS[t], :], rank(t), None, ALU.is_equal)
                    if t < T - 1:
                        steps.go(last)
                last.then_inc(pick_ready, 1)

            v.wait_ge(logits_done, 1)
            for t in range(T):
                r = ROWS[t]
                st.did(v.tensor_copy(logit[0:r, t, :], bank(2)[0:r, t * EXPERTS:(t + 1) * EXPERTS]))
            for n, hot in enumerate((hot1, hot2)):
                st.did(v.reduce_max(vals[:, :, n:n + 1], logit, AX))
                st.did(v.tensor_tensor(tie, logit, vals[:, :, n:n + 1].to_broadcast([P, T, EXPERTS]), ALU.is_equal))
                st.did(v.tensor_tensor(tie, tie, descending, ALU.mult))
                st.did(v.reduce_max(vals[:, :, 4:5], tie, AX))
                st.did(v.tensor_tensor(hot, descending, vals[:, :, 4:5].to_broadcast([P, T, EXPERTS]), ALU.is_equal))
                if n == 0:
                    st.did(v.scalar_tensor_tensor(logit, hot, NEG, logit, ALU.mult, ALU.add))
            v.tensor_tensor(vals[:, :, 2:3], vals[:, :, 1:2], vals[:, :, 0:1], ALU.subtract).then_inc(logits_copied, 1)
            st.did(v.tensor_tensor(chosen, hot1, hot2, ALU.add))
            v.tensor_tensor(chosen, chosen, is_token, ALU.mult).then_inc(chosen_ready, 1)
            v.wait_ge(gate_exped, 1)
            st.did(v.tensor_scalar(vals[:, :, 5:6], vals[:, :, 3:4], 1.0, None, ALU.add))
            st.did(v.reciprocal(vals[:, :, 6:7], vals[:, :, 5:6]))
            st.did(v.tensor_tensor(vals[:, :, 7:8], vals[:, :, 3:4], vals[:, :, 6:7], ALU.mult))
            st.did(v.tensor_tensor(hot1, hot1, vals[:, :, 6:7].to_broadcast([P, T, EXPERTS]), ALU.mult))
            st.did(v.tensor_tensor(hot2, hot2, vals[:, :, 7:8].to_broadcast([P, T, EXPERTS]), ALU.mult))
            st.did(v.tensor_tensor(gates, hot1, hot2, ALU.add))
            v.wait_ge(ranks_done, 1)
            v.wait_ge(chosen_ready, 1)
            st.did(v.tensor_scalar(ranks, bank(3)[:, 0:T * EXPERTS].rearrange("p (t e) -> p t e", t=T), 1.0, None, ALU.add))
            st.did(v.tensor_tensor(ranks, ranks, chosen, ALU.mult))
            make_pick(lambda t: ranks[0:ROWS[t], t, 0:1], st)
            tokens, items, upto, first = (per_expert[:, a, :] for a in range(4))
            st.did(v.tensor_copy(tokens, bank(3)[:, T * EXPERTS:(T + 1) * EXPERTS]))
            st.did(v.tensor_scalar(items, tokens, 0.0, None, ALU.is_gt))
            for p in range(1, PASSES):
                st.did(v.scalar_tensor_tensor(items, tokens, float(ITEM * p), items, ALU.is_gt, ALU.add))
            st.did(v.tensor_scalar(items[:, 0:1], items[:, 0:1], 1.0, None, ALU.max))
            st.did(v.tensor_scalar(first, items, 0.0, None, ALU.mult))
            st.did(v.tensor_tensor_scan(upto, items, first, 0.0, ALU.add, ALU.add))
            st.did(v.tensor_tensor(first, upto, items, ALU.subtract))

            def every_item(x):
                return x.unsqueeze(1).to_broadcast([P, NI, EXPERTS])

            st.did(v.tensor_tensor(first_rank, item_number, every_item(first), ALU.subtract))
            st.did(v.tensor_tensor(of_item, first_rank, every_item(items), ALU.is_lt))
            st.did(v.tensor_scalar(wide, first_rank, 0.0, None, ALU.is_ge))
            st.did(v.tensor_tensor(of_item, of_item, wide, ALU.mult))
            st.did(v.tensor_scalar(first_rank, first_rank, float(ITEM), None, ALU.mult))
            for t in range(T):
                st.did(v.tensor_tensor(wide, every_item(ranks[:, t, :]), first_rank, ALU.subtract))
                st.did(v.tensor_tensor(wide, wide, of_item, ALU.mult))
                st.did(v.reduce_sum(rank_of[:, t, :], wide, AX))
                st.did(v.tensor_tensor(wide, every_item(gates[:, t, :]), of_item, ALU.mult))
                st.did(v.reduce_sum(gate_of[:, t, :], wide, AX))
            st.did(v.tensor_tensor(wide, expert_number, of_item, ALU.mult))
            st.did(v.reduce_sum(plan_f[:, 1:NI + 1], wide, AX))
            st.did(v.tensor_copy(plan_f[:, 0:1], upto[:, EXPERTS - 1:EXPERTS]))
            v.tensor_copy(plan[0:1, 0:NI + 1], plan_f[0:1, :]).then_inc(plan_ready, 1)
            v.wait_ge(plan_ready, 1)
            K = 2 + 3 * MOE_CHUNKS
            entry = st.n
            count = v.value_load(plan[0:1, 0:1], min_val=0, max_val=ITEMS)
            with v.Fori(0, ITEMS) as i:
                with v.If(i < count):
                    st.base, st.n = K * i, entry
                    for c in range(MOE_CHUNKS):
                        b = 2 + 2 * (c % 2)
                        rr, tt = silu_r[c % 2], silu_t[c % 2]
                        v.wait_ge(e_exp, MOE_CHUNKS * i + (c + 1))
                        st.did(v.tensor_scalar(rr, rr, BIG, 1.0, ALU.min, ALU.add))
                        st.did(v.reciprocal(rr, rr))
                        st.did(v.tensor_tensor(tt, rr, bank(b), ALU.mult))
                        v.wait_ge(e_gu, 2 * MOE_CHUNKS * i + (2 * c + 2))
                        v.tensor_tensor(hE[:, FPC * c:FPC * (c + 1), :], tt.rearrange("p (f s) -> p f s", f=FPC),
                                        bank(b + 1).rearrange("p (f s) -> p f s", f=FPC), ALU.mult).then_inc(e_h, 1)
                    v.wait_ge(pick_turned, i + 1)
                    make_pick(lambda t: rank_of[0:ROWS[t], t, :][:, bass.ds(i + 1, 1)], st)
                    v.wait_ge(added, 6 * i + 6)
                    for n in range(2 * T):
                        t, h = divmod(n, 2)
                        v.wait_ge(combined, 6 * i + (n + 1))
                        acc = o_or_acc[0:ROWS[t], t, h * CH:(h + 1) * CH]
                        v.scalar_tensor_tensor(acc, bank((6, 7, 0, 1)[n % 4])[0:ROWS[t], :],
                                               gate_of[0:ROWS[t], t, bass.ds(i, 1)], acc, ALU.mult, ALU.add).then_inc(added, 1)
                    assert st.n - entry == K, st.n - entry
            tail = Steps(v, dve_tail)
            v.wait_ge(added, count * 6 + 6)
            for t in range(T):
                r = ROWS[t]
                tail.did(v.scalar_tensor_tensor(x_tok[0:r, t, :], x_tok[0:r, t, :], ALPHA, o_or_acc[0:r, t, :], ALU.mult, ALU.add))
                layer_norm(t, 3 * T, 128, tail)


_OUTS = [(1, 256, 1024), (8, 4, 1024),
         (2, 1, 256, 8, 64), (2, 1, 256, 8, 64), (2, 8, 4, 8, 64), (2, 8, 4, 8, 64),
         (2, 1, 256, 8, 64), (2, 1, 256, 8, 64), (2, 8, 1024, 8, 64), (2, 8, 1024, 8, 64)]


def kernel(**inputs):
    import numpy as _np
    import concourse.bacc as _bacc
    from concourse import mybir as _mybir
    from concourse.bass_utils import run_bass_kernel_spmd as _run

    nc = _bacc.Bacc("TRN2", target_bir_lowering=False, num_devices=1)
    arrays, ins = {}, {}
    inputs = {n: _np.asarray(a) for n, a in inputs.items()}
    g = _np.concatenate([inputs["g_mix_a"], inputs["g_mix_b"]], 1).reshape(2, 8, 128)
    inputs["g_mix_cols"] = g.transpose(2, 0, 1)
    inputs["sb_bias_all"] = _np.broadcast_to(inputs["sb_bias"], (128, 2, 8))
    inputs["sb_bias_rows"] = _np.tile(_np.repeat(inputs["sb_bias"], 4, axis=1), 4).T
    for name, a in list(inputs.items()) + list(position_tables().items()):
        a = _np.ascontiguousarray(a)
        arrays[f"in_{name}"] = a
        ins[name] = nc.dram_tensor(f"in_{name}", a.shape, _mybir.dt.from_np(a.dtype), kind="ExternalInput").ap()
    outs = [nc.dram_tensor(f"out_{i}", shape, _mybir.dt.float32, kind="ExternalOutput").ap()
            for i, shape in enumerate(_OUTS)]
    hybrid_decode_step(nc, ins, outs)
    r = _run(nc, [arrays], core_ids=[0])
    return tuple(r.results[0][f"out_{i}"] for i in range(len(_OUTS)))
```
